# Optimizing a Trainium2 kernel written in Bass

```python
import jax, jax.numpy as jnp
from jax import lax
import numpy as np

D_MODEL = 1024
BATCH = 1
SEQ = 512
DEPTH = 2

GRID_W = 64
CTX_LEN = 256
EPS = 1e-6
ROPE_BASE = 10000.0
NEG_INF = -1e30

D_MIX = D_MODEL
GROUP_W = D_MIX // 4
MLA_HEADS = 4
MLA_NOPE = 64
MLA_ROPE = 32
MLA_V = GROUP_W // MLA_HEADS
MLA_Q_RANK = D_MODEL // 4
MLA_KV_RANK = D_MODEL // 8
Q_BLOCK = 128
FN_W = GROUP_W
FN_GROUPS = 4
NA_HEADS = 4
NA_HD = GROUP_W // NA_HEADS
NA_WIN_H = 8
NA_WIN_W = 16
NA_QCOL = 16
NA_KCOL = NA_QCOL + NA_WIN_W
CV_W = GROUP_W
CV_K = 31
D_FF = 4 * D_MODEL

IN_WIDTHS = (MLA_Q_RANK, MLA_KV_RANK, MLA_ROPE, GROUP_W, GROUP_W, GROUP_W, FN_W, 2 * CV_W)
D_IN = MLA_Q_RANK + MLA_KV_RANK + MLA_ROPE + 3 * GROUP_W + FN_W + 2 * CV_W

kernel_name = "hybrid_mla_fnet_natten_conformer_dit"

def rmsnorm(x, g):
    xf = x.astype(jnp.float32)
    y = xf * lax.rsqrt(jnp.mean(xf * xf, axis=-1, keepdims=True) + EPS)
    return (y * g.astype(jnp.float32)).astype(x.dtype)

def layernorm(x, g, b):
    xf = x.astype(jnp.float32)
    mu = jnp.mean(xf, axis=-1, keepdims=True)
    var = jnp.mean(jnp.square(xf - mu), axis=-1, keepdims=True)
    y = (xf - mu) * lax.rsqrt(var + EPS)
    return (y * g.astype(jnp.float32) + b.astype(jnp.float32)).astype(x.dtype)

def modulate(h, shift, scale):
    return h * (1 + scale[:, None, :]) + shift[:, None, :]

def axial_rope(n, dim):
    t = jnp.arange(n)
    row = (t // GRID_W).astype(jnp.float32)
    col = (t % GRID_W).astype(jnp.float32)
    per_axis = dim // 2
    inv = ROPE_BASE ** (-jnp.arange(0, per_axis, 2, dtype=jnp.float32) / per_axis)
    ang = jnp.concatenate([row[:, None] * inv, col[:, None] * inv], axis=-1)
    return jnp.cos(ang), jnp.sin(ang)

def apply_rope(x, cos, sin):
    half = x.shape[-1] // 2
    xf = x.astype(jnp.float32)
    x1, x2 = xf[..., :half], xf[..., half:]
    return jnp.concatenate([x1 * cos - x2 * sin, x1 * sin + x2 * cos], axis=-1).astype(x.dtype)

def attend(q, k, v):
    s = jnp.einsum('bqhd,bkhd->bhqk', q, k).astype(jnp.float32) * (q.shape[-1] ** -0.5)
    w = jax.nn.softmax(s, axis=-1).astype(v.dtype)
    return jnp.einsum('bhqk,bkhd->bqhd', w, v)

def mla_q(q_a, q_norm, w_uq, rope):
    B, L, _ = q_a.shape
    q = (rmsnorm(q_a, q_norm) @ w_uq).reshape(B, L, MLA_HEADS, MLA_NOPE + MLA_ROPE)
    if rope is not None:
        cos, sin = rope
        q = jnp.concatenate([q[..., :MLA_NOPE], apply_rope(q[..., MLA_NOPE:], cos[:, None], sin[:, None])], axis=-1)
    return q

def mla_kv(kv_a, k_r, kv_norm, w_ukv, rope):
    B, L, _ = kv_a.shape
    kv = (rmsnorm(kv_a, kv_norm) @ w_ukv).reshape(B, L, MLA_HEADS, MLA_NOPE + MLA_V)
    if rope is not None:
        cos, sin = rope
        k_r = apply_rope(k_r, cos, sin)
    k_r = jnp.broadcast_to(k_r[:, :, None, :], (B, L, MLA_HEADS, MLA_ROPE))
    k = jnp.concatenate([kv[..., :MLA_NOPE], k_r], axis=-1)
    return k, kv[..., MLA_NOPE:]

def mla_latent(q, k, v, kc, vc):
    B, S, H, d = q.shape
    k_all = jnp.concatenate([k, kc], axis=1)
    v_all = jnp.concatenate([v, vc], axis=1)
    qb = q.reshape(B, S // Q_BLOCK, Q_BLOCK, H, d).transpose(1, 0, 2, 3, 4)
    ob = lax.map(lambda qi: attend(qi, k_all, v_all), qb)
    return ob.transpose(1, 0, 2, 3, 4).reshape(B, S, H * MLA_V)

def natten_cols():
    n_cb = GRID_W // NA_QCOL
    qcol = np.arange(GRID_W).reshape(n_cb, NA_QCOL)
    win_start = np.clip(qcol - NA_WIN_W // 2, 0, GRID_W - NA_WIN_W)
    blk_start = np.clip(np.arange(n_cb) * NA_QCOL - NA_WIN_W // 2, 0, GRID_W - NA_KCOL)
    kcol = blk_start[:, None] + np.arange(NA_KCOL)
    ws = win_start[:, :, None]
    in_win = (kcol[:, None, :] >= ws) & (kcol[:, None, :] < ws + NA_WIN_W)
    rel_idx = np.clip(kcol[:, None, :] - qcol[:, :, None] + NA_WIN_W - 1, 0, 2 * NA_WIN_W - 2)
    return kcol, in_win, rel_idx

def natten_latent(q, k, v, kc, vc, rpb):
    B, S, H, d = q.shape
    rows = S // GRID_W
    wh = min(NA_WIN_H, rows)
    n_cb = GRID_W // NA_QCOL
    kcol, in_win, rel_idx = natten_cols()
    qg = q.reshape(B, rows, n_cb, NA_QCOL, H, d)
    kg = k.reshape(B, rows, GRID_W, H, d)[:, :, kcol]
    vg = v.reshape(B, rows, GRID_W, H, d)[:, :, kcol]
    rpb = rpb.astype(jnp.float32)
    scale = d ** -0.5
    n_loc = wh * NA_KCOL

    def row_block(r):
        rs = jnp.clip(r - wh // 2, 0, rows - wh)
        kb = lax.dynamic_slice_in_dim(kg, rs, wh, axis=1)
        vb = lax.dynamic_slice_in_dim(vg, rs, wh, axis=1)
        qr = lax.dynamic_index_in_dim(qg, r, axis=1, keepdims=False)
        dr_idx = rs + jnp.arange(wh) - r + (NA_WIN_H - 1)
        bias = rpb[:, dr_idx][:, :, rel_idx].transpose(0, 2, 3, 1, 4)
        bias = jnp.where(in_win[:, :, None, :], bias, NEG_INF)
        s_loc = jnp.einsum('bcqhd,bwckhd->bhcqwk', qr, kb).astype(jnp.float32) * scale + bias[None]
        s_ctx = jnp.einsum('bcqhd,bkhd->bhcqk', qr, kc).astype(jnp.float32) * scale
        s = jnp.concatenate([s_loc.reshape(B, H, n_cb, NA_QCOL, n_loc), s_ctx], axis=-1)
        w = jax.nn.softmax(s, axis=-1).astype(v.dtype)
        w_loc = w[..., :n_loc].reshape(B, H, n_cb, NA_QCOL, wh, NA_KCOL)
        return (jnp.einsum('bhcqwk,bwckhd->bcqhd', w_loc, vb)
                + jnp.einsum('bhcqk,bkhd->bcqhd', w[..., n_loc:], vc))

    o = lax.map(row_block, jnp.arange(rows))
    return o.transpose(1, 0, 2, 3, 4, 5).reshape(B, S, H * d)

def heads(u, n_heads):
    B, L, W = u.shape
    return u.reshape(B, L, n_heads, W // n_heads)

def fourier_mix(u):
    B, L, W = u.shape
    ug = u.reshape(B, L, FN_GROUPS, W // FN_GROUPS).astype(jnp.float32)
    f = jnp.fft.fft2(ug, axes=(1, 3), norm='ortho').real
    return f.reshape(B, L, W).astype(u.dtype)

def conformer_conv(u, w_dw, b_dw, ln_g, ln_b):
    a, g = jnp.split(u, 2, axis=-1)
    y = a * jax.nn.sigmoid(g)
    y = lax.conv_general_dilated(y, w_dw[:, None, :], window_strides=(1,),
                                 padding=[(CV_K // 2, CV_K // 2)],
                                 dimension_numbers=('NWC', 'WIO', 'NWC'),
                                 feature_group_count=CV_W) + b_dw
    y = layernorm(y, ln_g, ln_b)
    return jax.nn.silu(y)

def sq_relu_mlp(h, w1, w2):
    return jnp.square(jax.nn.relu(h @ w1)) @ w2

def split_cols(p):
    return jnp.split(p, np.cumsum(IN_WIDTHS)[:-1].tolist(), axis=-1)

def trunk_layer(x, xc, mod_x, mod_c, rope, prm, last):
    (w_in, q_norm, w_uq, kv_norm, w_ukv, rpb, cv_w, cv_b, cv_g, cv_beta,
     w_out, g1, g2, w1, w2) = prm
    sh1, sc1, gt1, sh2, sc2, gt2 = jnp.split(mod_x, 6, axis=-1)
    csh1, csc1, cgt1, csh2, csc2, cgt2 = jnp.split(mod_c, 6, axis=-1)

    h = modulate(rmsnorm(x, g1), sh1, sc1)
    hc = modulate(rmsnorm(xc, g1), csh1, csc1)
    q_a, kv_a, k_r, na_q, na_k, na_v, fn_u, cv_u = split_cols(h @ w_in)
    cq_a, ckv_a, ck_r, cna_q, cna_k, cna_v, cfn_u, ccv_u = split_cols(hc @ w_in)

    mk_c, mv_c = mla_kv(ckv_a, ck_r, kv_norm, w_ukv, None)
    nk_c, nv_c = heads(cna_k, NA_HEADS), heads(cna_v, NA_HEADS)

    mq = mla_q(q_a, q_norm, w_uq, rope)
    mk, mv = mla_kv(kv_a, k_r, kv_norm, w_ukv, rope)
    o_mla = mla_latent(mq, mk, mv, mk_c, mv_c)
    o_na = natten_latent(heads(na_q, NA_HEADS), heads(na_k, NA_HEADS), heads(na_v, NA_HEADS), nk_c, nv_c, rpb)
    o_fn = fourier_mix(fn_u)
    o_cv = conformer_conv(cv_u, cv_w, cv_b, cv_g, cv_beta)
    y = jnp.concatenate([o_mla, o_na, o_fn, o_cv], axis=-1) @ w_out
    x = x + gt1[:, None, :] * y
    x = x + gt2[:, None, :] * sq_relu_mlp(modulate(rmsnorm(x, g2), sh2, sc2), w1, w2)

    if not last:
        B, C, _ = hc.shape
        o_mla_c = attend(mla_q(cq_a, q_norm, w_uq, None), mk_c, mv_c).reshape(B, C, MLA_HEADS * MLA_V)
        o_na_c = attend(heads(cna_q, NA_HEADS), nk_c, nv_c).reshape(B, C, GROUP_W)
        yc = jnp.concatenate([o_mla_c, o_na_c, fourier_mix(cfn_u),
                              conformer_conv(ccv_u, cv_w, cv_b, cv_g, cv_beta)], axis=-1) @ w_out
        xc = xc + cgt1[:, None, :] * yc
        xc = xc + cgt2[:, None, :] * sq_relu_mlp(modulate(rmsnorm(xc, g2), csh2, csc2), w1, w2)
    return x, xc

def setup_inputs(seed: int = 0) -> dict:
    key = jax.random.key(seed)
    ks = iter(jax.random.split(key, 32))

    def nrm(shape, scale):
        return jax.random.normal(next(ks), shape, jnp.float32) * scale

    def gain(shape):
        return 1.0 + nrm(shape, 0.05)

    L = DEPTH
    return {
        "x": nrm((BATCH, SEQ, D_MODEL), 1.0),
        "c": nrm((BATCH, D_MODEL), 1.0),
        "ctx": nrm((BATCH, CTX_LEN, D_MODEL), 1.0),
        "c_ctx": nrm((D_MODEL,), 1.0),
        "w_mod": nrm((L, D_MODEL, 6 * D_MODEL), 0.5 * D_MODEL ** -0.5),
        "b_mod": nrm((L, 6 * D_MODEL), 0.01),
        "norm1_g": gain((L, D_MODEL)),
        "norm2_g": gain((L, D_MODEL)),
        "w_in": nrm((L, D_MODEL, D_IN), D_MODEL ** -0.5),
        "mla_q_norm": gain((L, MLA_Q_RANK)),
        "mla_w_uq": nrm((L, MLA_Q_RANK, MLA_HEADS * (MLA_NOPE + MLA_ROPE)), MLA_Q_RANK ** -0.5),
        "mla_kv_norm": gain((L, MLA_KV_RANK)),
        "mla_w_ukv": nrm((L, MLA_KV_RANK, MLA_HEADS * (MLA_NOPE + MLA_V)), MLA_KV_RANK ** -0.5),
        "na_rpb": nrm((L, NA_HEADS, 2 * NA_WIN_H - 1, 2 * NA_WIN_W - 1), 0.5),
        "cv_w_dw": nrm((L, CV_K, CV_W), CV_K ** -0.5),
        "cv_b_dw": nrm((L, CV_W), 0.01),
        "cv_ln_g": gain((L, CV_W)),
        "cv_ln_b": nrm((L, CV_W), 0.01),
        "w_out": nrm((L, D_MIX, D_MODEL), D_MIX ** -0.5),
        "w_ff1": nrm((L, D_MODEL, D_FF), D_MODEL ** -0.5),
        "w_ff2": nrm((L, D_FF, D_MODEL), D_FF ** -0.5),
        "final_g": gain((D_MODEL,)),
    }

def reference(x, c, ctx, c_ctx, w_mod, b_mod, norm1_g, norm2_g, w_in, mla_q_norm, mla_w_uq,
              mla_kv_norm, mla_w_ukv, na_rpb, cv_w_dw, cv_b_dw, cv_ln_g, cv_ln_b, w_out,
              w_ff1, w_ff2, final_g):
    rope = axial_rope(x.shape[1], MLA_ROPE)
    xc = ctx
    for i in range(DEPTH):
        mod_x = jax.nn.silu(c) @ w_mod[i] + b_mod[i]
        mod_c = jax.nn.silu(c_ctx)[None, :] @ w_mod[i] + b_mod[i]
        prm = (w_in[i], mla_q_norm[i], mla_w_uq[i], mla_kv_norm[i], mla_w_ukv[i], na_rpb[i],
               cv_w_dw[i], cv_b_dw[i], cv_ln_g[i], cv_ln_b[i], w_out[i],
               norm1_g[i], norm2_g[i], w_ff1[i], w_ff2[i])
        x, xc = trunk_layer(x, xc, mod_x, mod_c, rope, prm, i == DEPTH - 1)
    return rmsnorm(x, final_g)


_drawn_inputs = setup_inputs


def setup_inputs(seed=0):
    import zlib

    import numpy as np

    out = dict(_drawn_inputs(seed))
    spreads = {}
    factors = {'ctx': 3.145,
     'b_mod': 2.688,
     'norm1_g': 5.208,
     'mla_q_norm': 8.0,
     'mla_w_uq': 2.798,
     'mla_kv_norm': 8.0,
     'na_rpb': 7.895,
     'cv_b_dw': 8.0,
     'cv_ln_g': 7.353,
     'cv_ln_b': 8.0}
    for name, (base, spread) in spreads.items():
        noise = np.random.default_rng([zlib.crc32(name.encode()), seed]).standard_normal(out[name].shape)
        drawn = base * np.exp(spread * noise) if base else spread * noise
        out[name] = __import__('jax').numpy.asarray(drawn.astype(out[name].dtype))
    for name, factor in factors.items():
        out[name] = (out[name] * factor).astype(out[name].dtype)
    return out
```

```python
from contextlib import ExitStack

import concourse.bass as bass
from concourse import mybir

F32 = mybir.dt.float32
F32R = mybir.dt.float32r
ACT = mybir.ActivationFunctionType
ALU = mybir.AluOpType
AX_X = mybir.AxisListType.X

P = 128
D = 1024
KT = D // P
LAT, CTX = 512, 256
T = LAT + CTX
LAYERS = 2
ROWS, COLS = 8, 64
HEADS = 4
HD = 64
FFC = 4
TAPS, HALO = 31, 15
CTX0 = HALO + LAT + HALO
PADW = CTX0 + CTX + 2 * HALO
CONVW = PADW - 2 * HALO
EPS = 1e-6
MLA_SCALE = 96 ** -0.5
NA_SCALE = HD ** -0.5
WINDOW0 = [0, 64, 192, 256]
VARIANT = [0, 1, 1, 2]

PB, PG1, PG2, PQN, PKVN, PCW, PCB, PLG, PLB = 0, 48, 56, 64, 66, 67, 129, 131, 133
PL = 135
PC = LAYERS * PL
PF = PC + 2 * KT
PE_ = PF + KT
NPAR = PE_ + 1
SH1, SC1, GT1, SH2, SC2, GT2 = (KT * i for i in range(6))

TILES = ["a0", "g0", "a1", "g1", "kv", "kr", "q0", "q1", "f0", "f1", "nq0", "nq1", "nk0", "nk1", "nv0", "nv1"]
KEYS = {"kv", "kr", "nk0", "nk1", "nv0", "nv1"}


CONV_STEP = 5
CONV_ORDER = [(0, k) for k in range(2 * CONV_STEP)]
for _k in range(TAPS):
    CONV_ORDER += [(1, _k)] + ([(0, _k + 2 * CONV_STEP)] if _k + 2 * CONV_STEP < TAPS else [])


def panel_order():
    order = [("mod", 0, c, s) for c in range(4) for s in range(4)]
    m0 = [("mod", 0, c, s) for c in range(4, 12) for s in range(4)]
    for i in range(16):
        order += [("in", 0, i)] + m0[2 * i:2 * i + 2]
    order += [("out", 0, i) for i in range(8)]
    m1 = [("mod", 1, c, s) for c in range(12) for s in range(4)]
    for j in range(FFC):
        k = 12 * j
        for i in range(16):
            order.append(("ff1", 0, 8 * j + i) if i < 8 else ("ff2", 0, j, i - 8))
            if i % 4 < 3:
                order.append(m1[k])
                k += 1
    order += [("in", 1, i) for i in range(16)] + [("out", 1, i) for i in range(8)]
    for j in range(FFC):
        order += [("ff1", 1, 8 * j + i) for i in range(8)] + [("ff2", 1, j, i) for i in range(8)]
    return order


IN_STEPS = [[], []]
for _i in range(16):
    IN_STEPS[0] += [("g", _i), ("m", 2 * _i), ("m", 2 * _i + 1)]
    IN_STEPS[1] += [("g", _i)]
FF_STEPS = [[], []]
for _i in range(16):
    FF_STEPS[0] += [("g", _i)] + ([("m", 3 * (_i // 4) + _i % 4)] if _i % 4 < 3 else [])
    FF_STEPS[1] += [("g", _i)]
P_IN = [16, 16 + 48 + 8 + 112]
P_OUT = [P_IN[0] + 48, P_IN[1] + 16]
P_FF = [P_OUT[0] + 8, P_OUT[1] + 8]
NPANEL = P_FF[1] + 64
RAWS = 4
AHEAD = RAWS - 1


def trunk(nc, x, panels, par, w_uq, w_ukv, bias, rope, dft, dft_ch, out):
    ctx = ExitStack()
    with ctx:
        base = (nc.sbuf_base + 31) // 32 * 32
        places = {}

        def at(name, shape, dt, offset):
            places[name] = offset
            return nc.alloc_sbuf_tensor_at(name, shape, dt, offset=base + offset)

        top = [0]

        def new(name, shape, dt=F32, size=None):
            n = 4
            for s in shape[1:]:
                n *= s
            o = top[0]
            top[0] += ((size or n) + 31) // 32 * 32
            return at(name, shape, dt, o)

        ROW = T * 4
        X = new("X", [P, KT, T])
        HHI = new("HHI", [P, KT, T], F32R)
        HLO = new("HLO", [P, KT, T], F32R)
        CHI = new("CHI", [P, KT, T], F32R)
        CLO = new("CLO", [P, KT, T], F32R)
        RAW = new("RAW", [P, RAWS, 1024])
        WLO = at("WLO", [P, RAWS, 1024], F32R, places["RAW"])
        WHI = new("WHI", [P, RAWS, 1024], F32R)
        YPAD = new("YPAD", [P, 2, PADW])
        NAQ = new("NAQ", [P, 2, T])
        NAK = new("NAK", [P, 2, T])
        CACC = new("CACC", [P, 2, CONVW])
        BM = new("BM", [P, 3, HEADS, 256])
        CS = new("CS", [P, T])
        CSD = new("CSD", [P, 256])
        IDENT = new("IDENT", [P, P])
        ONES = new("ONES", [P, P])
        PAR = new("PAR", [P, NPAR])
        MODT = new("MODT", [P, LAYERS, 48, 2])
        AC = new("AC", [P, LAYERS, 2, KT, 2])
        CW = new("CW", [P, KT, P], F32R)
        CSILU = new("CSILU", [P, KT, 2])
        MODROW = new("MODROW", [P, 512])
        MT = new("MT", [P, 4, 2])
        NMX = new("NMX", [P, 2, 24])
        SUM = new("SUM", [P, 2, 24])
        RIN = new("RIN", [P, 2, 24])
        assert base + top[0] <= nc.sbuf_usable_end, (base + top[0], nc.sbuf_usable_end)

        h0 = places["HHI"]
        QT = at("QT", [P, HEADS, T], F32, h0)
        KTT = at("KTT", [P, HEADS, T], F32, h0 + 4 * ROW)
        VM = at("VM", [P, 6, 256], F32, h0 + 8 * ROW)
        VN = at("VN", [P, 9, 256], F32, h0 + 10 * ROW)
        PEXP = at("PEXP", [P, 3, T], F32, h0 + 13 * ROW)
        DFT = at("DFT", [P, 2, 1024], F32, h0 + 13 * ROW)
        c0, l0 = places["CHI"], places["CLO"]
        QA = at("QA", [P, 2, T], F32, l0)
        WUQ = at("WUQ", [P, 2, 512], F32, l0 + 2 * ROW)
        WUKV = at("WUKV", [P, 512], F32, l0 + 2 * ROW + 4096)
        NAVT = at("NAVT", [P, 2, T], F32, l0 + 4 * ROW)
        SIG = at("SIG", [P, T], F32, l0 + 6 * ROW)
        PTN = at("PTN", [P, 3, 4, P], F32, places["YPAD"])
        RSTDC = at("RSTDC", [P, T], F32, l0 + 6 * ROW)
        KVA = at("KVA", [P, T], F32, c0)
        RKV = at("RKV", [P, T], F32, c0 + ROW)
        SQQ = at("SQQ", [P, 2, T], F32, c0 + 2 * ROW)
        AB = [at("AB0", [P, 6, 256], F32, c0 + 2 * ROW), at("AB1", [P, 6, 256], F32, l0 + 2 * ROW)]
        FU = at("FU", [P, 2, T], F32, c0 + 4 * ROW)
        KRT = at("KRT", [P, T], F32, c0 + 6 * ROW)
        ROT = at("ROT", [P, T], F32, c0 + 7 * ROW)
        SQC = at("SQC", [P, 2, T], F32, l0 + 6 * ROW)
        RSTD = at("RSTD", [P, T], F32, places["YPAD"])
        PTC = at("PTC", [P, 2, 2, CTX], F32, places["YPAD"])
        XN = at("XN", [P, 2, T], F32, places["NAQ"])
        HT = at("HT", [P, 2, T], F32, places["NAK"])
        SQ = at("SQ", [P, 2, T], F32, places["CACC"])
        RELU = at("RELU", [P, 2, T], F32, places["NAQ"])
        SQF = at("SQF", [P, 2, T], F32, places["NAK"])
        PTM = [at("PTM0", [P, 6, LAT], F32, places["NAQ"]), at("PTM1", [P, 6, LAT], F32, places["BM"])]
        CTMP = at("CTMP", [P, T], F32, places["CS"])
        OUTT = at("OUTT", [P, 2, LAT], F32, places["NAK"])

        PS = ctx.enter_context(nc.psum_tensor("PS", [P, 8 * 512], F32))
        G = [PS[:, 0:1024], PS[:, 1024:2048]]
        bank = [PS[:, 512 * b:512 * (b + 1)] for b in range(8)]
        STAT = PS[:, 2048:2048 + T]
        MODACC, MODTP = bank[7], bank[6]

        def sem(name):
            return ctx.enter_context(nc.semaphore(name))

        raw_in = [sem(f"raw_in{i}") for i in range(RAWS)]
        hi_done, lo_done, w_used = sem("hi_done"), sem("lo_done"), sem("w_used")
        job_done, pads_ready = sem("job_done"), sem("pads_ready")
        g_free = [sem("g_free0"), sem("g_free1")]
        par_in, x_in, const_in, c_ready, cw_ready, consts = (
            sem(n) for n in ("par_in", "x_in", "const_in", "c_ready", "cw_ready", "consts"))
        mod_row, mod_tp, mod_part, mod_done = (
            sem(n) for n in ("mod_row", "mod_tp", "mod_part", "mod_done"))
        ac_ready = sem("ac_ready")
        sq_ready, sq_used, ln_done, rstd_ready, xn_ready, hhi_ready, hlo_ready = (
            sem(n) for n in
            ("sq_ready", "sq_used", "ln_done", "rstd_ready", "xn_ready", "hhi_ready",
             "hlo_ready"))
        L2 = range(LAYERS)

        def per_layer(*names):
            return ([sem(f"{n}_l{k}") for k in L2] for n in names)

        (bias_in, rope_in, wu_in, in_evac, glu_done, conv_step, kv_stat, kv_ln, kv_rstd, q_stat, q_ln,
         q_rstd, kvn_ready, qn_ready, kr_part, kr_ready, q_nope, q_part, kt_ready,
         dft_used, cat_hi, cat_lo) = per_layer(
            "bias_in", "rope_in", "wu_in", "in_evac", "glu_done", "conv_step", "kv_stat", "kv_ln",
            "kv_rstd", "q_stat", "q_ln", "q_rstd", "kvn_ready", "qn_ready", "kr_part", "kr_ready", "q_nope",
            "q_part", "kt_ready", "dft_used", "cat_hi", "cat_lo")
        dft_in = [[sem(f"dft_in{s}_l{k}") for s in range(2)] for k in L2]
        (mean_done, cen_done, csq_done, var_done, cln_done, crstd_done, cn_done) = per_layer(
            "mean_done", "cen_done", "csq_done", "var_done", "cln_done", "crstd_done", "cn_done")
        def per_att(n):
            return [[sem(f"{n}_{a}_l{k}") for a in ("na", "mla")] for k in L2]

        (s_ready, s_bias, nm_ready, exp_done, ri_ready, pn_ready, t_ready, pt_ready, pt_used) = (
            per_att(n) for n in ("s_ready", "s_bias", "nm_ready", "exp_done", "ri_ready", "pn_ready", "t_ready",
                                 "pt_ready", "pt_used"))
        hid_hi, hid_lo = per_layer("hid_hi", "hid_lo")
        out_ready, out_sent = sem("out_ready"), [sem("out_sent0"), sem("out_sent1")]

        def pcol(l, c, n=1):
            return PAR[:, l * PL + c:l * PL + c + n]

        EPSC = PAR[:, PE_:PE_ + 1]

        def width(l, tile):
            return T if l == 0 or tile in KEYS else LAT

        def spans(w):
            return [(0, LAT)] if w == LAT else [(0, LAT), (LAT, T)]

        G_IN = [0]
        JOBS = [["kn0", "kn1", "kn2", "kn3", "vm0", "vm1", "q0", "q1", "q2", "q3", "vn0", "vn1", "vn2"]
                + [f"ab{t}" for t in range(6 if l == 0 else 4)] for l in L2]
        G_JOB = [16]
        G_DFT = [G_JOB[0] + len(JOBS[0])]
        G_OUT = [G_DFT[0]]
        G_FF = [G_OUT[0] + 8]
        G_IN.append(G_FF[0] + 64)
        G_JOB.append(G_IN[1] + 16)
        G_DFT.append(G_JOB[1] + len(JOBS[1]))
        G_OUT.append(G_DFT[1])
        G_FF.append(G_OUT[1] + 8)
        JD = [0, len(JOBS[0]) + 2]

        def units(l, a):
            if a == 0:
                return [u for hh in range(2) for u in
                        [(2 * hh + p, q, False) for q in range(4) for p in range(2)]
                        + ([(2 * hh + p, q, True) for q in range(2) for p in range(2)] if l == 0 else [])]
            return [u for h in range(HEADS) for u in
                    [(h, q, False) for q in range(4)] + ([(h, q, True) for q in range(2)] if l == 0 else [])]

        def n_att(l):
            return len(units(l, 0)), len(units(l, 1))

        S_RING, T_RING, P_RING = [3, 2], [2, 1], 3

        def s_at(a, u, n):
            return PS[:, (512, 1024)[a] * (u % S_RING[a]):][:, 0:n]

        def t_at(a, u, n):
            return bank[3 + u % 2][:, 0:n] if a == 0 else PS[:, 2048:2048 + n]

        def av_at(a, c):
            return bank[(5, 6)[a] + c]

        CAT_ORDER = [6, 7, 4, 5, 2, 3, 0, 1]

        def in_sq(l, tile):
            n = G_IN[l] + TILES.index(tile)
            return g_free[n % 2], n // 2 + 1

        block = ctx.enter_context(nc.Block())

        @block.sync
        def _(sp):
            def load(i, p, n):
                sp.dma_start(RAW[:, i, :], panels[p, :, :]).then_inc(raw_in[i], 16)

            def stream(first, count):
                p = first
                while p < first + count and (p % RAWS or first + count - p < RAWS):
                    if p >= RAWS:
                        sp.wait_ge(w_used, p - RAWS + 1)
                    load(p % RAWS, p, 1)
                    p += 1
                turns = (first + count - p) // RAWS
                if turns:
                    with sp.Fori(0, turns) as j:
                        for i in range(RAWS):
                            if p + i >= RAWS:
                                sp.wait_ge(w_used, j * RAWS + (p + i - RAWS + 1))
                            load(i, j * RAWS + (p + i), 1)
                p += RAWS * turns
                while p < first + count:
                    sp.wait_ge(w_used, p - RAWS + 1)
                    load(p % RAWS, p, 1)
                    p += 1

            sp.dma_start(PAR[:], par).then_inc(par_in, 16)
            for p in range(RAWS):
                load(p, p, 1)
            sp.dma_start(X[:], x).then_inc(x_in, 16)
            sp.dma_start(CSD[:], dft_ch).then_inc(const_in, 16)
            sp.dma_start(CS[64:P, :], rope).then_inc(rope_in[0], 16)
            sp.dma_start(BM[:], bias[0]).then_inc(bias_in[0], 16)
            stream(RAWS, P_IN[0] + 8 - RAWS)
            for l in L2:
                if l == 1:
                    stream(P_FF[0] + 6, P_IN[1] + 8 - P_FF[0] - 6)
                sp.wait_ge(w_used, P_IN[l] + 1)
                sp.dma_start(WUQ[:], w_uq[l]).then_inc(wu_in[l], 16)
                sp.dma_start(WUKV[:], w_ukv[l]).then_inc(wu_in[l], 16)
                stream(P_IN[l] + 8, P_FF[l] + 6 - P_IN[l] - 8)
                if l == 0:
                    sp.wait_ge(cat_lo[0], 8)
                    sp.dma_start(BM[:], bias[1]).then_inc(bias_in[1], 16)
                    sp.dma_start(CS[64:P, :], rope).then_inc(rope_in[1], 16)
            stream(P_FF[1] + 6, NPANEL - P_FF[1] - 6)
            for kt in range(KT):
                sp.wait_ge(out_ready, kt + 1)
                sp.dma_start(out[:, kt, :], OUTT[:, kt % 2, :]).then_inc(out_sent[kt % 2], 16)
            for half in range(2):
                sp.wait_ge(out_sent[half], 16 * KT // 2)

        @block.scalar
        def _(act):
            def split_hi(i, p):
                act.wait_ge(raw_in[i], slot_turn(p) * 16)
                act.activation(WHI[:, i, :], RAW[:, i, :], ACT.Copy).then_inc(hi_done, 1)

            def slot_turn(p):
                return p // RAWS + 1

            def mod_copy(p):
                act.wait_ge(w_used, p + 1)
                act.activation(MODROW[0:4, :], MODACC[0:4, :], ACT.Copy).then_inc(mod_row, 1)

            def square(k, kt, w, n):
                act.wait_ge(g_free[n % 2], n // 2 + 1)
                if kt >= 2:
                    act.wait_ge(sq_used, KT * k + kt - 1)
                act.activation(SQ[:, kt % 2, 0:w], X[:, kt, 0:w], ACT.Square).then_inc(sq_ready, 1)

            def rstd(k, w):
                act.wait_ge(sq_used, KT * (k + 1))
                act.activation(RSTD[:, 0:w], STAT[:, 0:w], ACT.Ln, bias=EPSC, scale=1.0 / D).then_inc(ln_done, 1)
                act.wait_ge(ln_done, k + 1)
                act.activation(RSTD[:, 0:w], RSTD[:, 0:w], ACT.Exp, scale=-0.5).then_inc(rstd_ready, 1)

            def modulate(k, l, n, w):
                act.wait_ge(ac_ready, 2 * l + n + 1)
                for kt in range(KT):
                    act.wait_ge(xn_ready, KT * k + kt + 1)
                    if kt >= 2:
                        act.wait_ge(hlo_ready, KT * k + kt - 1)
                    for v, (a, b) in enumerate(spans(w)):
                        sh = MODT[:, l, (SH1, SH2)[n] + kt, v:v + 1]
                        ac = AC[:, l, n, kt, v:v + 1]
                        act.activation(HT[:, kt % 2, a:b], XN[:, kt % 2, a:b], ACT.Identity, bias=sh, scale=ac)
                        last = act.activation(HHI[:, kt, a:b], XN[:, kt % 2, a:b], ACT.Identity, bias=sh, scale=ac)
                    last.then_inc(hhi_ready, 1)

            def cat_tile(l, f, pieces):
                if f:
                    act.wait_ge(cat_lo[l], f)
                c = CAT_ORDER[f]
                for a, b, src, func, kw, perm in pieces:
                    for dst in (CTMP[:, a:b], CHI[:, c, a:b]):
                        if perm:
                            dst = dst.rearrange("p (c r) -> p c r", r=ROWS)
                        last = act.activation(dst, src, func, **kw)
                last.then_inc(cat_hi[l], 1)

            def attention(l, a):
                us = units(l, a)
                f = (4, 6)[a]

                def probs(u):
                    h, q, c = us[u]
                    n = CTX if c else (LAT, T)[a]
                    act.wait_ge(nm_ready[l][a], u + 1)
                    if u >= P_RING:
                        act.wait_ge(t_ready[l][a], u - P_RING + 1)
                    act.activation(PEXP[:, u % P_RING, 0:n], s_at(a, u, n), ACT.Exp, bias=NMX[:, a, u:u + 1],
                                   scale=(1.0, MLA_SCALE)[a], accum_out=SUM[:, a, u:u + 1]).then_inc(
                        exp_done[l][a], 1)

                def turned(u):
                    h, q, c = us[u]
                    act.wait_ge(t_ready[l][a], u + 1)
                    if a == 0:
                        n = CTX if c else LAT
                        if u >= P_RING:
                            act.wait_ge(pt_used[l][a], u - P_RING + 1)
                        dst = PTN[:, u % P_RING, 0:n // P, :]
                        src = t_at(a, u, n).rearrange("p (t q) -> p t q", q=P)
                    else:
                        n = CTX if c else T
                        if h >= 2 and q == 0:
                            act.wait_ge(pt_used[l][a], (2 * (h - 2) + (2 if c else 1)) if l == 0 else h - 1)
                        big = PTC[:, h % 2, :, :] if c else PTM[h % 2][:, :, :]
                        dst = big[:, :, q * P:(q + 1) * P]
                        src = t_at(a, u, n).rearrange("p (t q) -> p t q", q=P)
                    act.activation(dst, src, ACT.Copy).then_inc(pt_ready[l][a], 1)

                def finish(hh):
                    act.wait_ge(pt_used[l][a], (hh + 1) * (len(us) // 2 if a == 0 else 4 if l == 0 else 2))
                    pieces = [(0, LAT, av_at(a, 0), ACT.Copy, {}, False)]
                    if l == 0:
                        pieces.append((LAT, T, av_at(a, 1)[:, 0:CTX], ACT.Copy, {}, False))
                    cat_tile(l, f + hh, pieces)

                lag = 2
                per = len(us) // 2
                if a == 0:
                    act.wait_ge(conv_step[l], 2 * TAPS)
                for s in range(len(us) + 5):
                    if s < len(us):
                        probs(s)
                    if 0 <= s - lag < len(us):
                        turned(s - lag)
                    if s - 4 in (per - 1, 2 * per - 1):
                        finish((s - 4) // per)

            def conv_squares(l):
                w = T if l == 0 else LAT
                for ct in range(2):
                    act.wait_ge(cen_done[l], ct + 1)
                    for a, b in spans(w):
                        s = 0 if a == 0 else CTX0 - LAT
                        last = act.activation(SQC[:, ct, a:b], CACC[:, ct, a + s:b + s], ACT.Square)
                    last.then_inc(csq_done[l], 1)

            def conv_rstd(l):
                w = T if l == 0 else LAT
                act.wait_ge(var_done[l], 1)
                act.activation(RSTDC[:, 0:w], STAT[:, 0:w], ACT.Ln, bias=EPSC, scale=1.0 / 256).then_inc(cln_done[l], 1)
                act.wait_ge(cln_done[l], 1)
                act.activation(RSTDC[:, 0:w], RSTDC[:, 0:w], ACT.Exp, scale=-0.5).then_inc(crstd_done[l], 1)

            def conv_tiles(l):
                act.wait_ge(q_part[l], 2 * HEADS)
                for ct in range(2):
                    act.wait_ge(cn_done[l], ct + 1)
                    kw = dict(bias=pcol(l, PLB + ct), scale=pcol(l, PLG + ct))
                    pieces = [(0, LAT, CACC[:, ct, 0:LAT].rearrange("p (r c) -> p c r", r=ROWS), ACT.Silu, kw, True)]
                    if l == 0:
                        pieces.append((LAT, T, CACC[:, ct, CTX0:CTX0 + CTX], ACT.Silu, kw, False))
                    cat_tile(l, ct, pieces)

            act.wait_ge(par_in, 16)
            act.activation(CSILU[:].rearrange("p a b -> p (a b)"), PAR[:, PC:PC + 2 * KT], ACT.Silu).then_inc(c_ready, 1)
            for p in range(AHEAD):
                split_hi(p, p)
            act.wait_ge(x_in, 16)
            for c in range(4):
                for s in range(4):
                    p = 4 * c + s
                    split_hi((p + AHEAD) % RAWS, p + AHEAD)
                    if s == 1:
                        for kt in (2 * c, 2 * c + 1):
                            if kt >= 2:
                                act.wait_ge(sq_used, KT * 0 + kt - 1)
                            act.activation(SQ[:, kt % 2, :], X[:, kt, :], ACT.Square).then_inc(sq_ready, 1)
                mod_copy(4 * c + 3)

            for l in L2:
                w = T if l == 0 else LAT
                k = 2 * l
                rstd(k, T)
                modulate(k, l, 0, T)
                for idx, (kind, i) in enumerate(IN_STEPS[l]):
                    p = P_IN[l] + idx
                    split_hi((p + AHEAD) % RAWS, p + AHEAD)
                    if kind == "m":
                        if i % 4 == 3:
                            mod_copy(p)
                        continue
                    tile, n = TILES[i], G_IN[l] + i
                    wt = width(l, tile)
                    src = G[n % 2][:, 0:wt]
                    if tile == "kr":
                        continue
                    act.wait_ge(w_used, p + 1)
                    free = g_free[n % 2]
                    ct = int(tile[-1]) if tile[-1].isdigit() else 0
                    if tile[0] == "a":
                        act.activation(CACC[:, ct, 0:wt], src, ACT.Copy).then_inc(free, 1)
                    elif tile[0] == "g":
                        if ct:
                            act.wait_ge(glu_done[l], 1)
                        act.activation(SIG[:, 0:wt], src, ACT.Sigmoid).then_inc(free, 1)
                    elif tile == "kv":
                        act.activation(KVA[:, 0:wt], src, ACT.Copy)
                        act.activation(RKV[:, 0:wt], src, ACT.Square).then_inc(free, 1)
                    elif tile[0] == "q":
                        act.activation(QA[:, ct, 0:wt], src, ACT.Copy)
                        act.activation(SQQ[:, ct, 0:wt], src, ACT.Square).then_inc(free, 1)
                    else:
                        dst, sc = {"f": (FU, 1.0), "nq": (NAQ, NA_SCALE), "nk": (NAK, 1.0), "nv": (NAVT, 1.0)}[tile[:-1]]
                        act.activation(dst[:, ct, 0:wt], src, ACT.Copy, scale=sc).then_inc(free, 1)
                    if tile == "f0":
                        act.wait_ge(kv_stat[l], 1)
                        act.activation(RKV[:], STAT, ACT.Ln, bias=EPSC, scale=1.0 / 128).then_inc(kv_ln[l], 1)
                        act.wait_ge(kv_ln[l], 1)
                        act.activation(RKV[:], RKV[:], ACT.Exp, scale=-0.5).then_inc(kv_rstd[l], 1)
                    if tile == "nq0":
                        act.wait_ge(q_stat[l], 1)
                        rq = SQQ[:, 0, 0:w]
                        act.activation(rq, STAT[:, 0:w], ACT.Ln, bias=EPSC, scale=1.0 / 256).then_inc(q_ln[l], 1)
                        act.wait_ge(q_ln[l], 1)
                        act.activation(rq, rq, ACT.Exp, scale=-0.5).then_inc(q_rstd[l], 1)
                for s in range(2):
                    act.dma_start(DFT[:, s, :], dft[s]).then_inc(dft_in[l][s], 16)
                act.wait_ge(kr_ready[l], 1)
                for h in range(HEADS):
                    last = act.activation(KTT[64:96, h, :], KRT[64:96, :], ACT.Copy)
                last.then_inc(kt_ready[l], 1)
                for i, job in enumerate(JOBS[l]):
                    n = G_JOB[l] + i
                    if job[:2] == "ab":
                        continue
                    act.wait_ge(job_done, JD[l] + i + 1)
                    j = int(job[-1])
                    free = g_free[n % 2]
                    if job[:2] == "kn":
                        act.activation(KTT[0:64, j, :], G[n % 2][0:64, 0:T], ACT.Copy).then_inc(free, 1)
                    elif job[0] == "q":
                        act.activation(QT[0:64, j, 0:w], G[n % 2][0:64, 0:w], ACT.Copy).then_inc(q_nope[l], 1)
                    else:
                        V = VM if job[:2] == "vm" else VN
                        act.activation(V[:, 3 * j:3 * j + 3, :].rearrange("p t d -> p (t d)"), G[n % 2][:, 0:T],
                                       ACT.Copy).then_inc(free, 1)
                    if job == "kn3":
                        conv_squares(l)
                    if job == "q0":
                        conv_rstd(l)
                conv_tiles(l)
                slices = 5 if l == 0 else 4
                for s in range(2, slices):
                    act.wait_ge(dft_used[l], s - 1)
                    act.dma_start(DFT[:, s % 2, :], dft[s]).then_inc(dft_in[l][s % 2], 16)
                for ct in range(2):
                    n = G_DFT[l] + ct
                    act.wait_ge(job_done, JD[l] + len(JOBS[l]) + ct + 1)
                    pieces = [(0, LAT, G[n % 2][:, 0:LAT], ACT.Copy, dict(scale=(LAT * HD) ** -0.5), False)]
                    if l == 0:
                        pieces.append((LAT, T, G[n % 2][:, LAT:T], ACT.Copy, dict(scale=(CTX * HD) ** -0.5), False))
                    cat_tile(l, 2 + ct, pieces)
                attention(l, 0)
                attention(l, 1)
                k = 2 * l + 1
                for m in range(KT):
                    split_hi((P_OUT[l] + m + AHEAD) % RAWS, P_OUT[l] + m + AHEAD)
                    if m:
                        square(k, m - 1, w, G_OUT[l] + m - 1)
                square(k, KT - 1, w, G_OUT[l] + KT - 1)
                rstd(k, w)
                modulate(k, l, 1, w)

                def chunk(l, j, last_chunk):
                    w = T if l == 0 else LAT
                    steps = FF_STEPS[l]
                    for idx, (kind, i) in enumerate(steps):
                        q = P_FF[l] + idx + AHEAD
                        if not (l == 1 and last_chunk and idx >= len(steps) - AHEAD):
                            turn = (q // RAWS + 1) + j * (len(steps) // RAWS)
                            act.wait_ge(raw_in[q % RAWS], turn * 16)
                            act.activation(WHI[:, q % RAWS, :], RAW[:, q % RAWS, :], ACT.Copy).then_inc(hi_done, 1)
                        if kind == "m":
                            if i % 4 == 3:
                                mod_copy(j * len(steps) + (P_FF[l] + idx))
                            continue
                        n = G_FF[l] + i
                        if i < KT:
                            act.wait_ge(w_used, j * len(steps) + (P_FF[l] + idx + 1))
                            if i >= 2:
                                act.wait_ge(hid_lo[l], j * KT + (i - 1))
                            act.activation(RELU[:, i % 2, 0:w], G[n % 2][:, 0:w], ACT.Relu).then_inc(
                                g_free[n % 2], 1)
                            act.wait_ge(g_free[n % 2], j * KT + (n // 2 + 1))
                            act.activation(SQF[:, i % 2, 0:w], RELU[:, i % 2, 0:w], ACT.Square)
                            act.activation(CHI[:, i, 0:w], RELU[:, i % 2, 0:w], ACT.Square).then_inc(hid_hi[l], 1)
                        elif last_chunk and i > KT:
                            square(2 * l + 2, i - KT - 1, w, n - 1 + 16 * (FFC - 1))
                    if last_chunk:
                        square(2 * l + 2, KT - 1, w, G_FF[l] + 16 * FFC - 1)

                with act.Fori(0, FFC - 1) as j:
                    chunk(l, j, False)
                chunk(l, FFC - 1, True)
            rstd(4, LAT)

        @block.tensor
        def _(pe):
            def three(dst, wk, k_slot, hi, lo, kt, w, start, stop):
                wcol = slice(wk * P, (wk + 1) * P)
                for wt, xt, first, last in ((WHI, hi, True, False), (WHI, lo, False, False), (WLO, hi, False, True)):
                    for a, b in spans(w):
                        mm = pe.matmul(dst[:, a:b], wt[:, k_slot, wcol], xt[:, kt, a:b], start=start and first,
                                       stop=stop and last)
                return mm

            def mod_panel(p_slot, s):
                for kk in range(2):
                    for wt in (WHI, WLO):
                        mm = pe.matmul(MODACC, CW[:, 2 * s + kk, :], wt[:, p_slot, 512 * kk:512 * (kk + 1)],
                                       start=(s == 0 and kk == 0 and wt is WHI), stop=(s == 3 and kk == 1 and wt is WLO))
                return mm

            def mod_turn(c):
                pe.wait_ge(mod_row, c + 1)
                if not isinstance(c, int) or c >= 1:
                    pe.wait_ge(mod_done, c)
                for i in range(4):
                    mm = pe.transpose(MODTP[:, i * P:(i + 1) * P], MODROW[:, i * P:(i + 1) * P], IDENT[:])
                mm.then_inc(mod_tp, 1)

            def ones_sum(dst, srcs, w, stop_at=None):
                for j, s in enumerate(srcs):
                    for a, b in spans(w):
                        mm = pe.matmul(dst[:, a:b], ONES[:], s[a:b] if isinstance(s, list) else s(a, b),
                                       start=(j == 0), stop=(j == len(srcs) - 1))
                return mm

            def stat(k, kt, w):
                pe.wait_ge(sq_ready, KT * k + kt + 1)
                for a, b in spans(w):
                    mm = pe.matmul(STAT[:, a:b], ONES[:], SQ[:, kt % 2, a:b], start=(kt == 0), stop=(kt == KT - 1))
                mm.then_inc(sq_used, 1)

            def attention(l, a):
                us = units(l, a)
                per = len(us) // 2

                def scores(u):
                    h, q, c = us[u]
                    if u >= S_RING[a]:
                        pe.wait_ge(exp_done[l][a], u - S_RING[a] + 1)
                    q0 = (LAT if c else 0) + q * P
                    if a == 0:
                        hp = slice(HD * (h % 2), HD * (h % 2) + HD)
                        lhs = NAQ[hp, h // 2, q0:q0 + P]
                        keys = [(0, LAT, T)] if c else [(0, WINDOW0[q], WINDOW0[q] + 256), (256, LAT, T)]
                        src = [(o, NAK[hp, h // 2, x0:x1]) for o, x0, x1 in keys]
                    else:
                        lhs = QT[0:96, h, q0:q0 + P]
                        keys = [(0, LAT, T)] if c else [(0, 0, LAT), (LAT, LAT, T)]
                        src = [(o, KTT[0:96, h, x0:x1]) for o, x0, x1 in keys]
                    S = s_at(a, u, 768 if a else 512)
                    for o, k in src:
                        mm = pe.matmul(S[:, o:o + k.shape[-1]], lhs, k, start=True, stop=True)
                    mm.then_inc(s_ready[l][a], 1)

                def turn(u):
                    h, q, c = us[u]
                    n = (CTX if c else (LAT, T)[a]) // P
                    pe.wait_ge(pn_ready[l][a], u + 1)
                    if u >= T_RING[a]:
                        pe.wait_ge(pt_ready[l][a], u - T_RING[a] + 1)
                    tp = t_at(a, u, n * P)
                    for t in range(n):
                        mm = pe.transpose(tp[:, t * P:(t + 1) * P], PEXP[:, u % P_RING, t * P:(t + 1) * P], IDENT[:])
                    mm.then_inc(t_ready[l][a], 1)

                def values(u):
                    h, q, c = us[u]
                    pe.wait_ge(pt_ready[l][0], u + 1)
                    if u >= per:
                        pe.wait_ge(cat_hi[l], 5)
                    if c:
                        tiles = [4, 5]
                    else:
                        tiles = {0: [0, 1], 1: [6, 7], 2: [7, 8], 3: [2, 3]}[q] + [4, 5]
                    dst = av_at(0, int(c))[HD * (h % 2):HD * (h % 2) + HD, q * P:(q + 1) * P]
                    for t, vt in enumerate(tiles):
                        mm = pe.matmul(dst, VN[:, vt, HD * h:HD * h + HD], PTN[:, u % P_RING, t, :],
                                       start=(t == 0), stop=(t == len(tiles) - 1))
                    mm.then_inc(pt_used[l][0], 1)

                def values_head(u):
                    h, q, c = us[u]
                    if q != (1 if c else 3):
                        return
                    pe.wait_ge(pt_ready[l][1], u + 1)
                    if h >= 2:
                        pe.wait_ge(cat_hi[l], 7)
                    tiles = [4, 5] if c else range(6)
                    n = CTX if c else LAT
                    src = PTC[:, h % 2, :, :] if c else PTM[h % 2]
                    dst = av_at(1, int(c))[HD * (h % 2):HD * (h % 2) + HD, 0:n]
                    for t, vt in enumerate(tiles):
                        mm = pe.matmul(dst, VM[:, vt, HD * h:HD * h + HD], src[:, t, :], start=(t == 0),
                                       stop=(t == len(tiles) - 1))
                    mm.then_inc(pt_used[l][1], 1)

                la, lb = 2, 3
                for s in range(len(us) + lb):
                    if s < len(us):
                        scores(s)
                    if 0 <= s - la < len(us):
                        turn(s - la)
                    if 0 <= s - lb < len(us):
                        (values, values_head)[a](s - lb)

            def conv_mean(l):
                w = T if l == 0 else LAT
                pe.wait_ge(conv_step[l], 2 * TAPS)
                for ct in range(2):
                    for a, b in spans(w):
                        s = 0 if a == 0 else CTX0 - LAT
                        mm = pe.matmul(STAT[:, a:b], ONES[:], CACC[:, ct, a + s:b + s], start=(ct == 0), stop=(ct == 1))
                mm.then_inc(mean_done[l], 1)

            def conv_variance(l):
                w = T if l == 0 else LAT
                pe.wait_ge(cen_done[l], 2)
                for ct in range(2):
                    pe.wait_ge(csq_done[l], ct + 1)
                    for a, b in spans(w):
                        mm = pe.matmul(STAT[:, a:b], ONES[:], SQC[:, ct, a:b], start=(ct == 0), stop=(ct == 1))
                mm.then_inc(var_done[l], 1)

            pe.wait_ge(consts, 2)
            pe.wait_ge(cw_ready, 3)
            for c in range(4):
                for s in range(4):
                    p = 4 * c + s
                    pe.wait_ge(lo_done, p + 1)
                    if s == 0 and c:
                        pe.wait_ge(mod_row, c)
                    mm = mod_panel(p % RAWS, s)
                    mm.then_inc(w_used, 1)
                    if s >= 2:
                        stat(0, 2 * c + s - 2, T)
                mod_turn(c)

            for l in L2:
                w = T if l == 0 else LAT
                k = 2 * l
                for idx, (kind, i) in enumerate(IN_STEPS[l]):
                    p = P_IN[l] + idx
                    pe.wait_ge(lo_done, p + 1)
                    if kind == "m":
                        c = 4 + i // 4
                        if i % 4 == 0:
                            pe.wait_ge(mod_row, c)
                        mm = mod_panel(p % RAWS, i % 4)
                        mm.then_inc(w_used, 1)
                        continue
                    n = G_IN[l] + i
                    if n >= 2:
                        pe.wait_ge(g_free[n % 2], n // 2)
                    wt = width(l, TILES[i])
                    for kt in range(KT):
                        if i == 0:
                            pe.wait_ge(hlo_ready, KT * k + kt + 1)
                        mm = three(G[n % 2], kt, p % RAWS, HHI, HLO, kt, wt, kt == 0, kt == KT - 1)
                    mm.then_inc(w_used, 1)
                    if l == 0 and i and i % 2 == 0:
                        mod_turn(4 + i // 2 - 1)
                    if TILES[i] == "q1":
                        pe.wait_ge(*in_sq(l, "kv"))
                        for a, b in spans(T):
                            mm = pe.matmul(STAT[:, a:b], ONES[:], RKV[:, a:b], start=True, stop=True)
                        mm.then_inc(kv_stat[l], 1)
                    if TILES[i] == "f1":
                        pe.wait_ge(*in_sq(l, "q1"))
                        pe.wait_ge(kv_ln[l], 1)
                        for ct in range(2):
                            for a, b in spans(w):
                                mm = pe.matmul(STAT[:, a:b], ONES[:], SQQ[:, ct, a:b], start=(ct == 0), stop=(ct == 1))
                        mm.then_inc(q_stat[l], 1)
                if l == 0:
                    mod_turn(11)
                conv_mean(l)
                pe.wait_ge(wu_in[l], 32)
                pe.wait_ge(kvn_ready[l], 1)
                for i, job in enumerate(JOBS[l]):
                    n = G_JOB[l] + i
                    j = int(job[-1])
                    pe.wait_ge(g_free[n % 2], n // 2)
                    dst = G[n % 2]
                    if job[:2] == "kn":
                        for a, b in spans(T):
                            mm = pe.matmul(dst[0:64, a:b], WUKV[:, 64 * j:64 * j + 64], KVA[:, a:b], start=True, stop=True)
                    elif job[:2] == "vm":
                        for t in range(3):
                            mm = pe.matmul(dst[:, 256 * t:256 * t + 256], KVA[:, (3 * j + t) * P:(3 * j + t + 1) * P],
                                           WUKV[:, 256:512], start=True, stop=True)
                    elif job[0] == "q":
                        if j == 0:
                            pe.wait_ge(qn_ready[l], 1)
                        for ct in range(2):
                            for a, b in spans(w):
                                mm = pe.matmul(dst[:, a:b], WUQ[:, ct, P * j:P * j + P], QA[:, ct, a:b], start=(ct == 0),
                                               stop=(ct == 1))
                    elif job[:2] == "vn":
                        for t in range(3):
                            vt = 3 * j + t
                            t0 = vt * P if vt < 6 else 64 + (vt - 6) * P
                            for ct in range(2):
                                mm = pe.transpose(dst[:, 256 * t + P * ct:256 * t + P * ct + P], NAVT[:, ct, t0:t0 + P],
                                                  IDENT[:])
                    else:
                        if j == 0:
                            pe.wait_ge(const_in, 16)
                        for ct in range(2):
                            mm = pe.matmul(dst[:, 256 * ct:256 * ct + 256], FU[:, ct, P * j:P * j + P], CSD[:], start=True,
                                           stop=True)
                    mm.then_inc(job_done, 1)
                    if job == "vm1":
                        conv_variance(l)
                n = G_DFT[l]
                pe.wait_ge(g_free[n % 2], n // 2)
                pe.wait_ge(g_free[(n + 1) % 2], (n + 1) // 2)
                for s in range(4):
                    pe.wait_ge(dft_in[l][s % 2], 16 * (s // 2 + 1))
                    for ct in range(2):
                        for cs in range(2):
                            mm = pe.matmul(G[(n + ct) % 2][:, 0:LAT], AB[ct][:, s, cs * P:(cs + 1) * P],
                                           DFT[:, s % 2, cs * 512:(cs + 1) * 512], start=(s == 0 and cs == 0),
                                           stop=(s == 3 and cs == 1))
                        if l == 1 and s == 3:
                            mm.then_inc(job_done, 1)
                    if l == 0 or s < 3:
                        mm.then_inc(dft_used[l], 1)
                if l == 0:
                    pe.wait_ge(dft_in[l][0], 48)
                    for ct in range(2):
                        for s in range(2):
                            for cs in range(2):
                                mm = pe.matmul(G[(n + ct) % 2][:, LAT:T], AB[ct][:, 4 + s, cs * P:(cs + 1) * P],
                                               DFT[:, 0, cs * 512 + s * 256:cs * 512 + (s + 1) * 256],
                                               start=(s == 0 and cs == 0), stop=(s == 1 and cs == 1))
                        mm.then_inc(job_done, 1)
                pe.wait_ge(crstd_done[l], 1)
                pe.wait_ge(cat_hi[l], 4)
                attention(l, 0)
                attention(l, 1)
                k = 2 * l + 1
                for m in range(KT):
                    p, n = P_OUT[l] + m, G_OUT[l] + m
                    pe.wait_ge(lo_done, p + 1)
                    pe.wait_ge(g_free[n % 2], n // 2)
                    for f, kt in enumerate(CAT_ORDER):
                        if m == 0:
                            pe.wait_ge(cat_lo[l], f + 1)
                        mm = three(G[n % 2], kt, p % RAWS, CHI, CLO, kt, w, f == 0, f == KT - 1)
                    mm.then_inc(w_used, 1)
                    if m >= 2:
                        stat(k, m - 2, w)
                stat(k, KT - 2, w)
                stat(k, KT - 1, w)

                def chunk(l, j, last_chunk):
                    w = T if l == 0 else LAT
                    steps = FF_STEPS[l]
                    for idx, (kind, i) in enumerate(steps):
                        p = P_FF[l] + idx
                        pe.wait_ge(lo_done, j * len(steps) + (p + 1))
                        if kind == "m":
                            c = j * 3 + (12 + i // 4)
                            if i % 4 == 0:
                                pe.wait_ge(mod_row, c)
                            mm = mod_panel(p % RAWS, i % 4)
                            mm.then_inc(w_used, 1)
                            continue
                        n = G_FF[l] + i
                        pe.wait_ge(g_free[n % 2], j * 8 + n // 2)
                        for kt in range(KT):
                            if i < KT:
                                if i == 0:
                                    pe.wait_ge(hlo_ready, KT * (2 * l + 1) + kt + 1)
                                mm = three(G[n % 2], kt, p % RAWS, HHI, HLO, kt, w, kt == 0, kt == KT - 1)
                            else:
                                if i == KT:
                                    pe.wait_ge(hid_lo[l], j * KT + (kt + 1))
                                mm = three(G[n % 2], kt, p % RAWS, CHI, CLO, kt, w, kt == 0, kt == KT - 1)
                        mm.then_inc(w_used, 1)
                        if l == 0 and i in (5, 10, 15):
                            mod_turn(j * 3 + (12 + i // 5 - 1))
                        if last_chunk and i >= KT + 2:
                            stat(2 * l + 2, i - KT - 2, w)
                    if last_chunk:
                        stat(2 * l + 2, KT - 2, w)
                        stat(2 * l + 2, KT - 1, w)

                with pe.Fori(0, FFC - 1) as j:
                    chunk(l, j, False)
                chunk(l, FFC - 1, True)

        @block.vector
        def _(dve):
            def split_lo(i, p):
                dve.wait_ge(hi_done, p + 1)
                dve.tensor_tensor(WLO[:, i, :], RAW[:, i, :], WHI[:, i, :].bitcast(F32),
                                  ALU.subtract).then_inc(lo_done, 1)

            def mod_finish(l, c, cc):
                dve.wait_ge(mod_tp, c + 1)
                tp = MODTP.rearrange("p (i r) -> p i r", r=P)
                b = PAR[:, bass.ds(l * PL + PB + 4 * cc, 4)]
                for v in range(2):
                    last = dve.tensor_tensor(MT[:, :, v], tp[:, :, v], b, ALU.add)
                last.then_inc(mod_part, 1)
                dve.wait_ge(mod_part, c + 1)
                for v in range(2):
                    last = dve.tensor_tensor(MODT[:, l, bass.ds(4 * cc, 4), v], tp[:, :, 2 + v], MT[:, :, v], ALU.add)
                last.then_inc(mod_done, 1)

            def coef(l, n):
                for v in range(2):
                    last = dve.scalar_tensor_tensor(AC[:, l, n, :, v], MODT[:, l, (SC1, SC2)[n]:(SC1, SC2)[n] + KT, v], 1.0,
                                                    pcol(l, (PG1, PG2)[n], KT), ALU.add, ALU.mult)
                last.then_inc(ac_ready, 1)

            def normalize(k, w):
                dve.wait_ge(rstd_ready, k + 1)
                for kt in range(KT + 1):
                    if kt < KT:
                        if kt >= 2:
                            dve.wait_ge(hhi_ready, KT * k + kt - 1)
                        dve.tensor_tensor(XN[:, kt % 2, 0:w], X[:, kt, 0:w], RSTD[:, 0:w], ALU.mult).then_inc(
                            xn_ready, 1)
                    if kt:
                        q = kt - 1
                        dve.wait_ge(hhi_ready, KT * k + q + 1)
                        dve.tensor_tensor(HLO[:, q, 0:w], HT[:, q % 2, 0:w], HHI[:, q, 0:w].bitcast(F32),
                                          ALU.subtract).then_inc(hlo_ready, 1)

            def cat_low(l, f):
                w = T if l == 0 else LAT
                c = CAT_ORDER[f]
                dve.wait_ge(cat_hi[l], f + 1)
                dve.tensor_tensor(CLO[:, c, 0:w], CTMP[:, 0:w], CHI[:, c, 0:w].bitcast(F32), ALU.subtract).then_inc(
                    cat_lo[l], 1)

            def residual(l, m, n, gate, w):
                for v, (a, b) in enumerate(spans(w)):
                    last = dve.scalar_tensor_tensor(X[:, m, a:b], G[n % 2][:, a:b], MODT[:, l, gate + m, v:v + 1],
                                                    X[:, m, a:b], ALU.mult, ALU.add)
                last.then_inc(g_free[n % 2], 1)

            def attention(l, a):
                us = units(l, a)
                per = len(us) // 2

                def maxima(u):
                    h, q, c = us[u]
                    n = CTX if c else (LAT, T)[a]
                    dve.wait_ge(s_ready[l][a], u + 1)
                    S = s_at(a, u, n)
                    if a == 0 and not c:
                        dve.tensor_tensor(S[:, 0:256], S[:, 0:256], BM[:, VARIANT[q], h, :], ALU.add).then_inc(
                            s_bias[l][0], 1)
                        dve.wait_ge(s_bias[l][0], len([1 for x in us[:u + 1] if not x[2]]))
                    if a == 0:
                        dve.tensor_reduce(NMX[:, a, u:u + 1], S, AX_X, ALU.max, negate=True).then_inc(nm_ready[l][a], 1)
                    else:
                        dve.tensor_reduce(RIN[:, a, u:u + 1], S, AX_X, ALU.max, negate=True).then_inc(s_bias[l][1], 1)
                        dve.wait_ge(s_bias[l][1], u + 1)
                        dve.tensor_scalar(NMX[:, a, u:u + 1], RIN[:, a, u:u + 1], MLA_SCALE, None, ALU.mult).then_inc(
                            nm_ready[l][a], 1)

                def norm(u):
                    h, q, c = us[u]
                    n = CTX if c else (LAT, T)[a]
                    dve.wait_ge(exp_done[l][a], u + 1)
                    dve.reciprocal(RIN[:, a, u:u + 1], SUM[:, a, u:u + 1]).then_inc(ri_ready[l][a], 1)
                    dve.wait_ge(ri_ready[l][a], u + 1)
                    pr = PEXP[:, u % P_RING, 0:n]
                    dve.tensor_scalar(pr, pr, RIN[:, a, u:u + 1], None, ALU.mult).then_inc(pn_ready[l][a], 1)

                if a == 0:
                    dve.wait_ge(bias_in[l], 16)
                for s in range(len(us) + 5):
                    if s < len(us):
                        maxima(s)
                    if 1 <= s <= len(us):
                        norm(s - 1)
                    if s - 4 in (per - 1, 2 * per - 1):
                        cat_low(l, (4, 6)[a] + (s - 4) // per)

            def glu(l, ct):
                if ct == 0:
                    dve.wait_ge(pads_ready, l + 1)
                dve.wait_ge(*in_sq(l, f"a{ct}"))
                dve.wait_ge(*in_sq(l, f"g{ct}"))
                y = YPAD[:, ct, HALO:HALO + LAT].rearrange("p (r c) -> p c r", r=ROWS)
                last = dve.tensor_tensor(y, CACC[:, ct, 0:LAT].rearrange("p (c r) -> p c r", r=ROWS),
                                         SIG[:, 0:LAT].rearrange("p (c r) -> p c r", r=ROWS), ALU.mult)
                if l == 0:
                    last = dve.tensor_tensor(YPAD[:, ct, CTX0 + HALO:CTX0 + HALO + CTX], CACC[:, ct, LAT:T],
                                             SIG[:, LAT:T], ALU.mult)
                last.then_inc(glu_done[l], 1)

            def conv_tap(l, at):
                ct, tap = CONV_ORDER[at]
                wide = CONVW if l == 0 else LAT
                acc, y = CACC[:, ct, 0:wide], YPAD[:, ct, tap:tap + wide]
                if tap == 0:
                    dve.wait_ge(glu_done[l], ct + 1)
                    dve.tensor_scalar(acc, y, pcol(l, PCW + ct), pcol(l, PCB + ct), ALU.mult, ALU.add).then_inc(
                        conv_step[l], 1)
                else:
                    dve.wait_ge(conv_step[l], CONV_ORDER.index((ct, tap - 1)) + 1)
                    dve.scalar_tensor_tensor(acc, y, pcol(l, PCW + 2 * tap + ct), acc, ALU.mult, ALU.add).then_inc(
                        conv_step[l], 1)

            def conv_center(l):
                w = T if l == 0 else LAT
                dve.wait_ge(mean_done[l], 1)
                for ct in range(2):
                    for a, b in spans(w):
                        s = 0 if a == 0 else CTX0 - LAT
                        y = CACC[:, ct, a + s:b + s]
                        last = dve.scalar_tensor_tensor(y, STAT[:, a:b], -1.0 / 256, y, ALU.mult, ALU.add)
                    last.then_inc(cen_done[l], 1)

            def conv_low(l):
                w = T if l == 0 else LAT
                dve.wait_ge(crstd_done[l], 1)
                for ct in range(2):
                    for a, b in spans(w):
                        s = 0 if a == 0 else CTX0 - LAT
                        y = CACC[:, ct, a + s:b + s]
                        last = dve.tensor_tensor(y, y, RSTDC[:, a:b], ALU.mult)
                    last.then_inc(cn_done[l], 1)
                dve.wait_ge(cn_done[l], 2)
                for ct in range(2):
                    cat_low(l, ct)

            dve.memset(CW[:].bitcast(F32), 0.0).then_inc(cw_ready, 1)
            dve.memset(ONES[:], 1.0)
            dve.memset(MODROW[:], 0.0).then_inc(cw_ready, 1)
            dve.wait_ge(cw_ready, 2)
            dve.wait_ge(c_ready, 1)
            dve.tensor_copy(CW[:, :, 0:2], CSILU[:]).then_inc(c_ready, 1)
            dve.wait_ge(c_ready, 2)
            dve.tensor_tensor(CW[:, :, 2:4], CSILU[:], CW[:, :, 0:2].bitcast(F32), ALU.subtract).then_inc(cw_ready, 1)
            for p in range(AHEAD):
                split_lo(p, p)
            for c in range(4):
                for s in range(4):
                    p = 4 * c + s
                    split_lo((p + AHEAD) % RAWS, p + AHEAD)
                mod_finish(0, c, c)
            dve.wait_ge(mod_done, 4)
            coef(0, 0)

            for l in L2:
                w = T if l == 0 else LAT
                k = 2 * l
                if l == 1:
                    dve.wait_ge(mod_done, 24)
                    coef(1, 0)
                    coef(1, 1)
                normalize(k, T)
                for idx, (kind, i) in enumerate(IN_STEPS[l]):
                    p = P_IN[l] + idx
                    split_lo((p + AHEAD) % RAWS, p + AHEAD)
                    if kind == "m":
                        continue
                    tile, n = TILES[i], G_IN[l] + i
                    if tile in ("a1", "kv"):
                        glu(l, 0 if tile == "a1" else 1)
                    if i >= 2:
                        for c in range(CONV_STEP * (i - 2), min(CONV_STEP * (i - 1), 2 * TAPS)):
                            conv_tap(l, c)
                    if tile == "kr":
                        dve.wait_ge(rope_in[l], 16)
                        dve.wait_ge(w_used, p + 1)
                        dve.tensor_tensor(KRT[64:96, :], G[n % 2][64:96, 0:T], CS[64:96, :], ALU.mult)
                        dve.tensor_tensor(ROT[64:96, :], G[n % 2][96:128, 0:T], CS[96:128, :], ALU.mult).then_inc(
                            g_free[n % 2], 1)
                        dve.wait_ge(g_free[n % 2], n // 2 + 1)
                        dve.tensor_tensor(KRT[64:96, :], KRT[64:96, :], ROT[64:96, :], ALU.add).then_inc(kr_ready[l], 1)
                    if l == 0 and i and i % 2 == 0:
                        mod_finish(0, 4 + i // 2 - 1, 4 + i // 2 - 1)
                    if tile == "f0":
                        dve.wait_ge(kv_rstd[l], 1)
                        dve.scalar_tensor_tensor(KVA[:], KVA[:], pcol(l, PKVN), RKV[:], ALU.mult, ALU.mult).then_inc(
                            kvn_ready[l], 1)
                    if tile == "nq0":
                        dve.wait_ge(q_rstd[l], 1)
                        for ct in range(2):
                            last = dve.scalar_tensor_tensor(QA[:, ct, 0:w], QA[:, ct, 0:w], pcol(l, PQN + ct),
                                                            SQQ[:, 0, 0:w], ALU.mult, ALU.mult)
                        last.then_inc(qn_ready[l], 1)
                if l == 0:
                    mod_finish(0, 11, 11)
                    dve.wait_ge(mod_done, 12)
                    coef(0, 1)
                conv_center(l)
                for i, job in enumerate(JOBS[l]):
                    n = G_JOB[l] + i
                    j = int(job[-1])
                    if job[0] == "q":
                        dve.wait_ge(q_nope[l], j + 1)
                        if j:
                            dve.wait_ge(q_part[l], 2 * j)
                        dve.tensor_tensor(QT[64:96, j, 0:w], G[n % 2][64:96, 0:w], CS[64:96, 0:w], ALU.mult)
                        dve.tensor_tensor(ROT[64:96, 0:w], G[n % 2][96:128, 0:w], CS[96:128, 0:w], ALU.mult).then_inc(
                            g_free[n % 2], 1)
                        dve.wait_ge(g_free[n % 2], n // 2 + 1)
                        dve.tensor_tensor(QT[64:96, j, 0:w], QT[64:96, j, 0:w], ROT[64:96, 0:w], ALU.add).then_inc(
                            q_part[l], 2)
                        if j == HEADS - 1:
                            conv_low(l)
                    elif job[:2] == "ab":
                        dve.wait_ge(job_done, JD[l] + i + 1)
                        dve.tensor_copy(AB[0][:, j, :], G[n % 2][:, 0:256])
                        dve.tensor_copy(AB[1][:, j, :], G[n % 2][:, 256:512]).then_inc(g_free[n % 2], 1)
                for ct in range(2):
                    cat_low(l, 2 + ct)
                attention(l, 0)
                attention(l, 1)
                k = 2 * l + 1
                for m in range(KT):
                    p, n = P_OUT[l] + m, G_OUT[l] + m
                    split_lo((p + AHEAD) % RAWS, p + AHEAD)
                    dve.wait_ge(w_used, p + 1)
                    residual(l, m, n, GT1, w)
                normalize(k, w)

                def chunk(l, j, last_chunk):
                    w = T if l == 0 else LAT
                    steps = FF_STEPS[l]
                    for idx, (kind, i) in enumerate(steps):
                        q = P_FF[l] + idx + AHEAD
                        if not (l == 1 and last_chunk and idx >= len(steps) - AHEAD):
                            split_lo(q % RAWS, j * len(steps) + q)
                        if kind == "m":
                            continue
                        n = G_FF[l] + i
                        if i < KT:
                            dve.wait_ge(hid_hi[l], j * KT + (i + 1))
                            dve.tensor_tensor(CLO[:, i, 0:w], SQF[:, i % 2, 0:w], CHI[:, i, 0:w].bitcast(F32),
                                              ALU.subtract).then_inc(hid_lo[l], 1)
                        else:
                            dve.wait_ge(w_used, j * len(steps) + (P_FF[l] + idx + 1))
                            residual(l, i - KT, n, GT2, w)
                        if l == 0 and i in (5, 10, 15):
                            mod_finish(1, j * 3 + (12 + i // 5 - 1), j * 3 + (i // 5 - 1))

                with dve.Fori(0, FFC - 1) as j:
                    chunk(l, j, False)
                chunk(l, FFC - 1, True)

            dve.wait_ge(rstd_ready, 4 + 1)
            for kt in range(KT):
                if kt >= 2:
                    dve.wait_ge(out_sent[kt % 2], 16 * (kt // 2))
                dve.scalar_tensor_tensor(OUTT[:, kt % 2, :], X[:, kt, 0:LAT], PAR[:, PF + kt:PF + kt + 1], RSTD[:, 0:LAT],
                                         ALU.mult, ALU.mult).then_inc(out_ready, 1)

        @block.gpsimd
        def _(pool):
            pool.memset(IDENT[:], 0.0).then_inc(consts, 1)
            pool.wait_ge(consts, 1)
            pool.affine_select(out=IDENT[:], in_=IDENT[:], compare_op=ALU.not_equal, fill=1.0, base=0,
                               pattern=[[-1, P]], channel_multiplier=1).then_inc(consts, 1)
            for l in L2:
                pool.wait_ge(hlo_ready, KT * (2 * l) + KT)
                pool.memset(YPAD[:], 0.0).then_inc(pads_ready, 1)


def kernel(**inputs):
    import numpy as np
    import concourse.bacc as bacc
    from concourse.bass_utils import run_bass_kernel_spmd

    a = {k: np.asarray(v) for k, v in inputs.items()}

    def panel(w):
        kk, m = w.shape
        return w.reshape(kk // P, P, m // P, P).transpose(2, 1, 0, 3).reshape(m // P, P, kk)

    order = np.arange(LAT).reshape(ROWS, COLS).T.reshape(-1)
    x = np.concatenate([a["x"][0][order], a["ctx"][0]], 0)
    x = x.reshape(T, KT, P).transpose(2, 1, 0)

    swap = np.concatenate([np.arange(16, 32), np.arange(16)])
    kv0, kr0, nq0 = 256, 384, 416
    fn0, cv0 = 1184, 1440
    packed = {}
    for l in range(LAYERS):
        w = a["w_in"][l]
        kr = w[:, kr0:kr0 + 32]
        cols = [w[:, cv0:cv0 + 128], w[:, cv0 + 256:cv0 + 384], w[:, cv0 + 128:cv0 + 256], w[:, cv0 + 384:cv0 + 512],
                w[:, kv0:kv0 + 128], np.concatenate([kr, kr[:, swap]] * 2, 1), w[:, 0:256], w[:, fn0:fn0 + 256],
                w[:, nq0:nq0 + 768]]
        packed["in", l] = panel(np.concatenate(cols, 1))
        packed["out", l] = panel(a["w_out"][l])
        packed["ff1", l] = panel(a["w_ff1"][l])
        packed["ff2", l] = [panel(a["w_ff2"][l][D * j:D * (j + 1)]) for j in range(FFC)]
        packed["mod", l] = a["w_mod"][l].reshape(4, 2, P, 12, 512).transpose(3, 0, 2, 1, 4).reshape(12, 4, P, 1024)
    panels = np.empty((NPANEL, P, 1024), np.float32)
    for p, (name, l, *at) in enumerate(panel_order()):
        part = packed[name, l]
        for i in at:
            part = part[i]
        panels[p] = part

    def columns(v):
        return v.reshape(-1, P).T

    par = []
    for l in range(LAYERS):
        par += [columns(a["b_mod"][l]), columns(a["norm1_g"][l]), columns(a["norm2_g"][l]), columns(a["mla_q_norm"][l]),
                columns(a["mla_kv_norm"][l]), columns(a["cv_w_dw"][l]), columns(a["cv_b_dw"][l]),
                columns(a["cv_ln_g"][l]), columns(a["cv_ln_b"][l])]
    par += [np.stack([columns(a["c"][0]), columns(a["c_ctx"])], 2).reshape(P, 2 * KT), columns(a["final_g"]),
            np.full((P, 1), EPS, np.float32)]
    par = np.concatenate(par, 1)

    uq = a["mla_w_uq"].reshape(LAYERS, 2, P, HEADS, 96)
    uq = np.concatenate([uq, uq[..., 64 + swap]], -1).transpose(0, 2, 1, 3, 4).reshape(LAYERS, P, 2, 512)
    ukv = a["mla_w_ukv"].reshape(LAYERS, P, HEADS, 2, HD).transpose(0, 1, 3, 2, 4).reshape(LAYERS, P, 512)

    bias = np.empty((LAYERS, P, 3, HEADS, 256), np.float32)
    qc, qr = np.repeat(np.arange(16), ROWS), np.tile(np.arange(ROWS), 16)
    kc, kr = np.repeat(np.arange(32), ROWS), np.tile(np.arange(ROWS), 32)
    for v, block in enumerate((0, 1, 3)):
        col, key = 16 * block + qc[:, None], WINDOW0[block] // ROWS + kc[None, :]
        start = np.clip(col - 8, 0, COLS - 16)
        inside = (key >= start) & (key < start + 16)
        rel = np.clip(key - col + 15, 0, 30)
        rows = kr[None, :] - qr[:, None] + 7
        bias[:, :, v] = np.where(inside[None, :, None, :], a["na_rpb"][:, :, rows, rel].transpose(0, 2, 1, 3),
                                 np.float32(-1e30))

    inv = 10000.0 ** (-np.arange(0, 16, 2, dtype=np.float32) / np.float32(16))
    t = order
    ang = np.concatenate([(t // COLS)[:, None] * inv, (t % COLS)[:, None] * inv], 1).astype(np.float32)
    rope = np.zeros((64, T), np.float32)
    rope[0:32] = 1.0
    rope[0:32, :LAT] = np.tile(np.cos(ang), (1, 2)).T
    rope[32:48, :LAT] = -np.sin(ang).T
    rope[48:64, :LAT] = np.sin(ang).T

    n = np.arange(HD)
    w = 2 * np.pi * np.outer(n, n) / HD
    z = np.zeros((HD, HD))
    dft_ch = np.concatenate([np.block([[np.cos(w), z], [z, np.cos(w)]]), np.block([[-np.sin(w), z], [z, -np.sin(w)]])],
                            1).astype(np.float32)
    w = 2 * np.pi * (np.outer(order, order) % LAT) / LAT
    dft = np.concatenate([np.cos(w).reshape(4, P, LAT), np.sin(w).reshape(4, P, LAT)], 2)
    n = np.arange(CTX)
    w = (2 * np.pi * (np.outer(n, n) % CTX) / CTX).reshape(2, P, CTX).transpose(1, 0, 2).reshape(1, P, 512)
    dft = np.concatenate([dft, np.concatenate([np.cos(w), np.sin(w)], 2)], 0).astype(np.float32)

    nc = bacc.Bacc("TRN2", target_bir_lowering=False, num_devices=1)
    arrays, args = {}, []
    for name, v in dict(x=x, panels=panels, par=par, w_uq=uq, w_ukv=ukv, bias=bias, rope=rope, dft=dft,
                        dft_ch=dft_ch).items():
        arrays[f"in_{name}"] = np.ascontiguousarray(v)
        args.append(nc.dram_tensor(f"in_{name}", v.shape, F32, kind="ExternalInput").ap())
    args.append(nc.dram_tensor("out_y", (P, KT, LAT), F32, kind="ExternalOutput").ap())
    trunk(nc, *args)
    y = run_bass_kernel_spmd(nc, [arrays], core_ids=[0]).results[0]["out_y"]
    y = np.asarray(y).transpose(2, 1, 0).reshape(LAT, D)
    back = np.arange(LAT).reshape(COLS, ROWS).T.reshape(-1)
    return y[back].reshape(1, LAT, D)
```

```python
from contextlib import ExitStack

import concourse.bass as bass
from concourse import mybir

F32 = mybir.dt.float32
F32R = mybir.dt.float32r
ACT = mybir.ActivationFunctionType
ALU = mybir.AluOpType
AX_X = mybir.AxisListType.X

P = 128
D = 1024
KT = D // P
LAT, CTX = 512, 256
T = LAT + CTX
LAYERS = 2
ROWS, COLS = 8, 64
HEADS = 4
HD = 64
FFC = 4
TAPS, HALO = 31, 15
CTX0 = HALO + LAT + HALO
PADW = CTX0 + CTX + 2 * HALO
CONVW = PADW - 2 * HALO
EPS = 1e-6
MLA_SCALE = 96 ** -0.5
NA_SCALE = HD ** -0.5
WINDOW0 = [0, 64, 192, 256]
VARIANT = [0, 1, 1, 2]

PB, PG1, PG2, PQN, PKVN, PCW, PCB, PLG, PLB = 0, 48, 56, 64, 66, 67, 129, 131, 133
PL = 135
PC = LAYERS * PL
PF = PC + 2 * KT
PE_ = PF + KT
NPAR = PE_ + 1
SH1, SC1, GT1, SH2, SC2, GT2 = (KT * i for i in range(6))

TILES = ["a0", "g0", "a1", "g1", "kv", "kr", "q0", "q1", "f0", "f1", "nq0", "nq1", "nk0", "nk1", "nv0", "nv1"]
KEYS = {"kv", "kr", "nk0", "nk1", "nv0", "nv1"}


CONV_STEP = 5
CONV_ORDER = [(0, k) for k in range(2 * CONV_STEP)]
for _k in range(TAPS):
    CONV_ORDER += [(1, _k)] + ([(0, _k + 2 * CONV_STEP)] if _k + 2 * CONV_STEP < TAPS else [])


MOD0, MPARTS = 4, 4


def panel_order():
    order = [("in", 0, i) for i in range(16)]
    order += [("modp", 0, c, s) for c in range(MOD0, 12) for s in range(MPARTS)]
    order += [("out", 0, i) for i in range(8)]
    m1 = [("modd", 1, c, s) for c in range(12) for s in range(MPARTS)]
    for j in range(FFC):
        k = 12 * j
        for i in range(16):
            order.append(("ff1", 0, 8 * j + i) if i < 8 else ("ff2", 0, j, i - 8))
            if i % 4 < 3:
                order.append(m1[k])
                k += 1
    order += [("in", 1, i) for i in range(16)] + [("out", 1, i) for i in range(8)]
    for j in range(FFC):
        order += [("ff1", 1, 8 * j + i) for i in range(8)] + [("ff2", 1, j, i) for i in range(8)]
    return order


ORDER = [o[0] for o in panel_order()]
NPANEL = len(ORDER)
WEIGHTS = [sum(o[:3] != "mod" for o in ORDER[:p]) for p in range(NPANEL)]
ON_PE = [sum(o != "modd" for o in ORDER[:p]) for p in range(NPANEL)]
ON_DVE = [sum(o == "modd" for o in ORDER[:p]) for p in range(NPANEL)]
P_IN, P_OUT, P_FF = [0, 168], [48, 184], [56, 192]
P_MOD = 16
RAWS = 4
AHEAD = RAWS - 1

FF_STEPS = [[], []]
for _i in range(16):
    FF_STEPS[0] += [("g", _i)] + ([("m", 3 * (_i // 4) + _i % 4)] if _i % 4 < 3 else [])
    FF_STEPS[1] += [("g", _i)]
assert all(ORDER[p + i].startswith(k) for l in range(2) for k, p in (("in", P_IN[l]), ("out", P_OUT[l]), ("ff", P_FF[l]))
           for i in range(1))

V1_DVE, V1_POOL = (1, 2, 4, 6), (0, 3, 5, 7)


def trunk(nc, x, panels, mods, par, w_uq, w_ukv, bias, rope, dft, dft_ch, out):
    ctx = ExitStack()
    with ctx:
        base = (nc.sbuf_base + 31) // 32 * 32
        places = {}

        def at(name, shape, dt, offset):
            places[name] = offset
            return nc.alloc_sbuf_tensor_at(name, shape, dt, offset=base + offset)

        top = [0]

        def new(name, shape, dt=F32, size=None):
            n = 4
            for s in shape[1:]:
                n *= s
            o = top[0]
            top[0] += ((size or n) + 31) // 32 * 32
            return at(name, shape, dt, o)

        ROW = T * 4
        X = new("X", [P, KT, T])
        HHI = new("HHI", [P, KT, T], F32R)
        HLO = new("HLO", [P, KT, T], F32R)
        CHI = new("CHI", [P, KT, T], F32R)
        CLO = new("CLO", [P, KT, T], F32R)
        RAW = new("RAW", [P, RAWS, 1024])
        WLO = at("WLO", [P, RAWS, 1024], F32R, places["RAW"])
        WHI = new("WHI", [P, RAWS, 1024], F32R)
        YPAD = new("YPAD", [P, 2, PADW])
        NAQ = new("NAQ", [P, 2, T])
        NAK = new("NAK", [P, 2, T])
        CACC = new("CACC", [P, 2, CONVW])
        BM = new("BM", [P, 3, HEADS, 256])
        CS = new("CS", [P, T])
        CSD = new("CSD", [P, 256])
        IDENT = new("IDENT", [P, P])
        ONES = new("ONES", [P, P])
        PAR = new("PAR", [P, NPAR])
        MODT = new("MODT", [P, LAYERS, 48, 2])
        AC = new("AC", [P, LAYERS, 2, KT, 2])
        CSILU = new("CSILU", [P, KT, 2])
        MODROW = new("MODROW", [P, 512])
        ACC = new("ACC", [P, 2, 512])
        MT = new("MT", [P, 2, 4])
        NMX = new("NMX", [P, 2, 24])
        SUM = new("SUM", [P, 2, 24])
        RIN = new("RIN", [P, 2, 24])
        assert base + top[0] <= nc.sbuf_usable_end, (base + top[0], nc.sbuf_usable_end)

        MPRO = [at(f"MPRO{c}", [P, MPARTS, 1024], F32, o) for c, o in enumerate(
            [places["CHI"], places["CHI"] + 16384, places["CHI"] + 32768, places["HHI"]])]
        ACCP = at("ACCP", [P, MOD0, 3, 512], F32, places["HLO"])
        h0 = places["HHI"]
        QT = at("QT", [P, HEADS, T], F32, h0)
        KTT = at("KTT", [P, HEADS, T], F32, h0 + 4 * ROW)
        VM = at("VM", [P, 6, 256], F32, h0 + 8 * ROW)
        VN = at("VN", [P, 9, 256], F32, h0 + 10 * ROW)
        PEXP = at("PEXP", [P, 3, T], F32, h0 + 13 * ROW)
        DFT = at("DFT", [P, 2, 1024], F32, h0 + 13 * ROW)
        c0, l0 = places["CHI"], places["CLO"]
        QA = at("QA", [P, 2, T], F32, l0)
        WUQ = at("WUQ", [P, 2, 512], F32, l0 + 2 * ROW)
        WUKV = at("WUKV", [P, 512], F32, l0 + 2 * ROW + 4096)
        NAVT = at("NAVT", [P, 2, T], F32, l0 + 4 * ROW)
        SIG = at("SIG", [P, T], F32, l0 + 6 * ROW)
        PTN = at("PTN", [P, 3, 4, P], F32, places["YPAD"])
        RSTDC = at("RSTDC", [P, T], F32, l0 + 6 * ROW)
        KVA = at("KVA", [P, T], F32, c0)
        RKV = at("RKV", [P, T], F32, c0 + ROW)
        SQQ = at("SQQ", [P, 2, T], F32, c0 + 2 * ROW)
        AB = [at("AB0", [P, 6, 256], F32, c0 + 2 * ROW), at("AB1", [P, 6, 256], F32, l0 + 2 * ROW)]
        FU = at("FU", [P, 2, T], F32, c0 + 4 * ROW)
        KRT = at("KRT", [P, T], F32, c0 + 6 * ROW)
        ROT = at("ROT", [P, T], F32, c0 + 7 * ROW)
        SQC = at("SQC", [P, 2, T], F32, l0 + 6 * ROW)
        RSTD = at("RSTD", [P, T], F32, places["YPAD"])
        PTC = at("PTC", [P, 2, 2, CTX], F32, places["YPAD"])
        XN = at("XN", [P, 2, T], F32, places["NAQ"])
        HT = at("HT", [P, 2, T], F32, places["NAK"])
        SQ = at("SQ", [P, 2, T], F32, places["CACC"])
        RELU = at("RELU", [P, 2, T], F32, places["NAQ"])
        SQF = at("SQF", [P, 2, T], F32, places["NAK"])
        PTM = [at("PTM0", [P, 6, LAT], F32, places["NAQ"]), at("PTM1", [P, 6, LAT], F32, places["BM"])]
        CTMP = at("CTMP", [P, T], F32, places["CS"])
        OUTT = at("OUTT", [P, 2, LAT], F32, places["NAK"])

        PS = ctx.enter_context(nc.psum_tensor("PS", [P, 8 * 512], F32))
        G = [PS[:, 0:1024], PS[:, 1024:2048]]
        bank = [PS[:, 512 * b:512 * (b + 1)] for b in range(8)]
        STAT = PS[:, 2048:2048 + T]
        MODTPV = bank[7].rearrange("p (i r) -> p i r", r=P)
        MODCOL = bank[7][:, 0:8].rearrange("p (i v) -> p i v", v=2)
        MODACC, MODTP, MODSUM = bank[7], bank[7], [bank[7], bank[6]]

        def sem(name):
            return ctx.enter_context(nc.semaphore(name))

        raw_in = [sem(f"raw_in{i}") for i in range(RAWS)]
        hi_done, lo_done, w_used = sem("hi_done"), sem("lo_done"), sem("w_used")
        job_done, pads_ready = sem("job_done"), sem("pads_ready")
        g_free = [sem("g_free0"), sem("g_free1")]
        par_in, x_in, const_in, c_ready, row_zero, ones_set, consts = (
            sem(n) for n in ("par_in", "x_in", "const_in", "c_ready", "row_zero", "ones_set", "consts"))
        mpro_in = [sem(f"mpro_in{c}") for c in range(MOD0)]
        mpro_dve, mpro_pool, mod_step, mod_row, mod_col, mod_diag, mod_part, mod_done = (
            sem(n) for n in ("mpro_dve", "mpro_pool", "mod_step", "mod_row", "mod_col", "mod_diag", "mod_part",
                             "mod_done"))
        ac_ready = sem("ac_ready")
        sq_ready, sq_used, ln_done, rstd_ready, xn_ready, hhi_ready, hlo_ready = (
            sem(n) for n in
            ("sq_ready", "sq_used", "ln_done", "rstd_ready", "xn_ready", "hhi_ready",
             "hlo_ready"))
        L2 = range(LAYERS)

        def per_layer(*names):
            return ([sem(f"{n}_l{k}") for k in L2] for n in names)

        (bias_in, rope_in, wu_in, in_evac, glu_done, conv_step, kv_stat, kv_ln, kv_rstd, q_stat, q_ln,
         q_rstd, kvn_ready, qn_ready, kr_part, kr_ready, q_nope, q_part, kt_ready,
         dft_used, cat_hi, cat_lo) = per_layer(
            "bias_in", "rope_in", "wu_in", "in_evac", "glu_done", "conv_step", "kv_stat", "kv_ln",
            "kv_rstd", "q_stat", "q_ln", "q_rstd", "kvn_ready", "qn_ready", "kr_part", "kr_ready", "q_nope",
            "q_part", "kt_ready", "dft_used", "cat_hi", "cat_lo")
        dft_in = [[sem(f"dft_in{s}_l{k}") for s in range(2)] for k in L2]
        (mean_done, cen_done, csq_done, var_done, cln_done, crstd_done, cn_done) = per_layer(
            "mean_done", "cen_done", "csq_done", "var_done", "cln_done", "crstd_done", "cn_done")
        def per_att(n):
            return [[sem(f"{n}_{a}_l{k}") for a in ("na", "mla")] for k in L2]

        (s_ready, s_bias, nm_ready, exp_done, ri_ready, pn_ready, t_ready, pt_ready, pt_used) = (
            per_att(n) for n in ("s_ready", "s_bias", "nm_ready", "exp_done", "ri_ready", "pn_ready", "t_ready",
                                 "pt_ready", "pt_used"))
        hid_hi, hid_lo = per_layer("hid_hi", "hid_lo")
        out_ready, out_sent = sem("out_ready"), [sem("out_sent0"), sem("out_sent1")]

        def pcol(l, c, n=1):
            return PAR[:, l * PL + c:l * PL + c + n]

        EPSC = PAR[:, PE_:PE_ + 1]

        def width(l, tile):
            return T if l == 0 or tile in KEYS else LAT

        def spans(w):
            return [(0, LAT)] if w == LAT else [(0, LAT), (LAT, T)]

        G_IN = [0]
        JOBS = [["kn0", "kn1", "kn2", "kn3", "vm0", "vm1", "q0", "q1", "q2", "q3", "vn0", "vn1", "vn2"]
                + [f"ab{t}" for t in range(6 if l == 0 else 4)] for l in L2]
        G_JOB = [16]
        G_DFT = [G_JOB[0] + len(JOBS[0])]
        G_OUT = [G_DFT[0]]
        G_FF = [G_OUT[0] + 8]
        G_IN.append(G_FF[0] + 64)
        G_JOB.append(G_IN[1] + 16)
        G_DFT.append(G_JOB[1] + len(JOBS[1]))
        G_OUT.append(G_DFT[1])
        G_FF.append(G_OUT[1] + 8)
        JD = [0, len(JOBS[0]) + 2]

        def units(l, a):
            if a == 0:
                return [u for hh in range(2) for u in
                        [(2 * hh + p, q, False) for q in range(4) for p in range(2)]
                        + ([(2 * hh + p, q, True) for q in range(2) for p in range(2)] if l == 0 else [])]
            return [u for h in range(HEADS) for u in
                    [(h, q, False) for q in range(4)] + ([(h, q, True) for q in range(2)] if l == 0 else [])]

        def n_att(l):
            return len(units(l, 0)), len(units(l, 1))

        S_RING, T_RING, P_RING = [3, 2], [2, 1], 3

        def s_at(a, u, n):
            return PS[:, (512, 1024)[a] * (u % S_RING[a]):][:, 0:n]

        def t_at(a, u, n):
            return bank[3 + u % 2][:, 0:n] if a == 0 else PS[:, 2048:2048 + n]

        def av_at(a, c):
            return bank[(5, 6)[a] + c]

        CAT_ORDER = [6, 7, 4, 5, 2, 3, 0, 1]

        def in_sq(l, tile):
            n = G_IN[l] + TILES.index(tile)
            return g_free[n % 2], n // 2 + 1

        def split_ahead(l, idx, last_chunk):
            turns = FFC - 1 if last_chunk else 0
            q = P_FF[l] + turns * len(FF_STEPS[l]) + idx + AHEAD
            if q >= NPANEL:
                return None
            if ORDER[q] == "modd":
                return False, ON_DVE[q] - turns * (len(FF_STEPS[l]) - 2 * KT)
            return True, WEIGHTS[q] - turns * 2 * KT

        block = ctx.enter_context(nc.Block())

        @block.sync
        def _(sp):
            def load(i, p, n):
                sp.dma_start(RAW[:, i, :], panels[p, :, :]).then_inc(raw_in[i], 16)

            def place_free(p, j=0, pe=0, dv=0):
                if ORDER[p] == "modd":
                    sp.wait_ge(mod_step, j * (4 * dv) + 4 * (ON_DVE[p] + 1))
                else:
                    sp.wait_ge(w_used, j * pe + (ON_PE[p] + 1))

            def stream(first, count):
                with sp.Fori(0, count // RAWS) as j:
                    for i in range(RAWS):
                        place_free(first + i - RAWS, j, RAWS)
                        load(i, j * RAWS + (first + i), 1)

            sp.dma_start(PAR[:], par).then_inc(par_in, 16)
            for c in range(MOD0):
                sp.dma_start(MPRO[c][:], mods[MPARTS * c:MPARTS * (c + 1)].rearrange("s p m -> p s m")).then_inc(
                    mpro_in[c], 16)
                if c == 0:
                    sp.dma_start(X[:], x).then_inc(x_in, 16)
            for p in range(RAWS):
                load(p, p, 1)
            sp.dma_start(CSD[:], dft_ch).then_inc(const_in, 16)
            sp.dma_start(CS[64:P, :], rope).then_inc(rope_in[0], 16)
            sp.dma_start(BM[:], bias[0]).then_inc(bias_in[0], 16)
            for l in L2:
                sp.wait_ge(w_used, ON_PE[P_IN[l]] + 1)
                sp.dma_start(WUQ[:], w_uq[l]).then_inc(wu_in[l], 16)
                sp.dma_start(WUKV[:], w_ukv[l]).then_inc(wu_in[l], 16)
                if l == 0:
                    stream(RAWS, P_FF[0] - RAWS)
                    for i in range(RAWS):
                        place_free(P_FF[0] + i - RAWS)
                        load(i, P_FF[0] + i, 1)
                    sp.dma_start(BM[:], bias[1]).then_inc(bias_in[1], 16)
                    sp.dma_start(CS[64:P, :], rope).then_inc(rope_in[1], 16)
                    n = len(FF_STEPS[0])
                    with sp.Fori(0, FFC) as j:
                        for i in range(n):
                            place_free(P_FF[0] + i, j, 2 * KT, n - 2 * KT)
                            load(i % RAWS, j * n + (P_FF[0] + RAWS + i), 1)
            stream(P_IN[1] + RAWS, NPANEL - P_IN[1] - RAWS)
            for kt in range(KT):
                sp.wait_ge(out_ready, kt + 1)
                sp.dma_start(out[:, kt, :], OUTT[:, kt % 2, :]).then_inc(out_sent[kt % 2], 16)
            for half in range(2):
                sp.wait_ge(out_sent[half], 16 * KT // 2)

        @block.scalar
        def _(act):
            def split_hi(i, p):
                act.wait_ge(raw_in[i], slot_turn(p) * 16)
                act.activation(WHI[:, i, :], RAW[:, i, :], ACT.Copy).then_inc(hi_done, 1)

            def mod_copy(c):
                if c == MOD0:
                    act.wait_ge(row_zero, 1)
                act.wait_ge(w_used, P_MOD + MPARTS * (c - MOD0 + 1))
                act.activation(MODROW[0:2, :], MODACC[0:2, :], ACT.Copy).then_inc(mod_row, 1)

            def slot_turn(p):
                return p // RAWS + 1

            def square(k, kt, w, n):
                act.wait_ge(g_free[n % 2], n // 2 + 1)
                if kt >= 2:
                    act.wait_ge(sq_used, KT * k + kt - 1)
                act.activation(SQ[:, kt % 2, 0:w], X[:, kt, 0:w], ACT.Square).then_inc(sq_ready, 1)

            def rstd(k, w):
                act.wait_ge(sq_used, KT * (k + 1))
                act.activation(RSTD[:, 0:w], STAT[:, 0:w], ACT.Ln, bias=EPSC, scale=1.0 / D).then_inc(ln_done, 1)
                act.wait_ge(ln_done, k + 1)
                act.activation(RSTD[:, 0:w], RSTD[:, 0:w], ACT.Exp, scale=-0.5).then_inc(rstd_ready, 1)

            def modulate(k, l, n, w):
                act.wait_ge(ac_ready, 2 * l + n + 1)
                for kt in range(KT):
                    act.wait_ge(xn_ready, KT * k + kt + 1)
                    if kt >= 2:
                        act.wait_ge(hlo_ready, KT * k + kt - 1)
                    for v, (a, b) in enumerate(spans(w)):
                        sh = MODT[:, l, (SH1, SH2)[n] + kt, v:v + 1]
                        ac = AC[:, l, n, kt, v:v + 1]
                        act.activation(HT[:, kt % 2, a:b], XN[:, kt % 2, a:b], ACT.Identity, bias=sh, scale=ac)
                        last = act.activation(HHI[:, kt, a:b], XN[:, kt % 2, a:b], ACT.Identity, bias=sh, scale=ac)
                    last.then_inc(hhi_ready, 1)

            def cat_tile(l, f, pieces):
                if f:
                    act.wait_ge(cat_lo[l], f)
                c = CAT_ORDER[f]
                for a, b, src, func, kw, perm in pieces:
                    for dst in (CTMP[:, a:b], CHI[:, c, a:b]):
                        if perm:
                            dst = dst.rearrange("p (c r) -> p c r", r=ROWS)
                        last = act.activation(dst, src, func, **kw)
                last.then_inc(cat_hi[l], 1)

            def attention(l, a):
                us = units(l, a)
                f = (4, 6)[a]

                def probs(u):
                    h, q, c = us[u]
                    n = CTX if c else (LAT, T)[a]
                    act.wait_ge(nm_ready[l][a], u + 1)
                    if u >= P_RING:
                        act.wait_ge(t_ready[l][a], u - P_RING + 1)
                    act.activation(PEXP[:, u % P_RING, 0:n], s_at(a, u, n), ACT.Exp, bias=NMX[:, a, u:u + 1],
                                   scale=(1.0, MLA_SCALE)[a], accum_out=SUM[:, a, u:u + 1]).then_inc(
                        exp_done[l][a], 1)

                def turned(u):
                    h, q, c = us[u]
                    act.wait_ge(t_ready[l][a], u + 1)
                    if a == 0:
                        n = CTX if c else LAT
                        if u >= P_RING:
                            act.wait_ge(pt_used[l][a], u - P_RING + 1)
                        dst = PTN[:, u % P_RING, 0:n // P, :]
                        src = t_at(a, u, n).rearrange("p (t q) -> p t q", q=P)
                    else:
                        n = CTX if c else T
                        if h >= 2 and q == 0:
                            act.wait_ge(pt_used[l][a], (2 * (h - 2) + (1 if c else 2)) if l == 0 else h - 1)
                        big = PTC[:, h % 2, :, :] if c else PTM[h % 2][:, :, :]
                        dst = big[:, :, q * P:(q + 1) * P]
                        src = t_at(a, u, n).rearrange("p (t q) -> p t q", q=P)
                    act.activation(dst, src, ACT.Copy).then_inc(pt_ready[l][a], 1)

                def finish(hh):
                    act.wait_ge(pt_used[l][a], (hh + 1) * (len(us) // 2 if a == 0 else 4 if l == 0 else 2))
                    pieces = [(0, LAT, av_at(a, 0), ACT.Copy, {}, False)]
                    if l == 0:
                        pieces.append((LAT, T, av_at(a, 1)[:, 0:CTX], ACT.Copy, {}, False))
                    cat_tile(l, f + hh, pieces)

                lag = 2
                per = len(us) // 2
                if a == 0:
                    act.wait_ge(conv_step[l], 2 * TAPS)
                for s in range(len(us) + (5 if a == 0 else 8)):
                    if s in ((per + 3, 2 * per + 4), (per + 6, 2 * per + 7))[a]:
                        finish(0 if s < 2 * per else 1)
                    if s < len(us):
                        probs(s)
                    if 0 <= s - lag < len(us):
                        turned(s - lag)
                    if l == 0 and a == 0 and s % 6 == 4 and s < 24:
                        mod_copy(8 + s // 6)

            def conv_squares(l):
                w = T if l == 0 else LAT
                for ct in range(2):
                    act.wait_ge(cen_done[l], ct + 1)
                    for a, b in spans(w):
                        s = 0 if a == 0 else CTX0 - LAT
                        last = act.activation(SQC[:, ct, a:b], CACC[:, ct, a + s:b + s], ACT.Square)
                    last.then_inc(csq_done[l], 1)

            def conv_rstd(l):
                w = T if l == 0 else LAT
                act.wait_ge(var_done[l], 1)
                act.activation(RSTDC[:, 0:w], STAT[:, 0:w], ACT.Ln, bias=EPSC, scale=1.0 / 256).then_inc(cln_done[l], 1)
                act.wait_ge(cln_done[l], 1)
                act.activation(RSTDC[:, 0:w], RSTDC[:, 0:w], ACT.Exp, scale=-0.5).then_inc(crstd_done[l], 1)

            def conv_tiles(l):
                act.wait_ge(q_part[l], 2 * HEADS)
                for ct in range(2):
                    if l == 0 and ct:
                        mod_copy(6)
                    act.wait_ge(cn_done[l], 2)
                    kw = dict(bias=pcol(l, PLB + ct), scale=pcol(l, PLG + ct))
                    pieces = [(0, LAT, CACC[:, ct, 0:LAT].rearrange("p (r c) -> p c r", r=ROWS), ACT.Silu, kw, True)]
                    if l == 0:
                        pieces.append((LAT, T, CACC[:, ct, CTX0:CTX0 + CTX], ACT.Silu, kw, False))
                    cat_tile(l, ct, pieces)

            act.wait_ge(par_in, 16)
            act.activation(CSILU[:].rearrange("p a b -> p (a b)"), PAR[:, PC:PC + 2 * KT], ACT.Silu).then_inc(c_ready, 1)
            act.wait_ge(x_in, 16)
            for kt in range(KT):
                if kt >= 2:
                    act.wait_ge(sq_used, kt - 1)
                act.activation(SQ[:, kt % 2, :], X[:, kt, :], ACT.Square).then_inc(sq_ready, 1)
            for l in L2:
                w = T if l == 0 else LAT
                k = 2 * l
                rstd(k, T)
                if l == 0:
                    for p in range(AHEAD):
                        split_hi(p, p)
                modulate(k, l, 0, T)
                for i in range(16):
                    p = P_IN[l] + i
                    if i + AHEAD < 16:
                        split_hi((p + AHEAD) % RAWS, p + AHEAD)
                    tile, n = TILES[i], G_IN[l] + i
                    wt = width(l, tile)
                    src = G[n % 2][:, 0:wt]
                    if tile == "kr":
                        continue
                    act.wait_ge(w_used, ON_PE[p] + 1)
                    free = g_free[n % 2]
                    ct = int(tile[-1]) if tile[-1].isdigit() else 0
                    if tile[0] == "a":
                        act.activation(CACC[:, ct, 0:wt], src, ACT.Copy).then_inc(free, 1)
                    elif tile[0] == "g":
                        if ct:
                            act.wait_ge(glu_done[l], 1)
                        act.activation(SIG[:, 0:wt], src, ACT.Sigmoid).then_inc(free, 1)
                    elif tile == "kv":
                        act.activation(KVA[:, 0:wt], src, ACT.Copy)
                        act.activation(RKV[:, 0:wt], src, ACT.Square).then_inc(free, 1)
                    elif tile[0] == "q":
                        act.activation(QA[:, ct, 0:wt], src, ACT.Copy)
                        act.activation(SQQ[:, ct, 0:wt], src, ACT.Square).then_inc(free, 1)
                    else:
                        dst, sc = {"f": (FU, 1.0), "nq": (NAQ, NA_SCALE), "nk": (NAK, 1.0), "nv": (NAVT, 1.0)}[tile[:-1]]
                        act.activation(dst[:, ct, 0:wt], src, ACT.Copy, scale=sc).then_inc(free, 1)
                    if tile == "f0":
                        act.wait_ge(kv_stat[l], 1)
                        act.activation(RKV[:], STAT, ACT.Ln, bias=EPSC, scale=1.0 / 128).then_inc(kv_ln[l], 1)
                        act.wait_ge(kv_ln[l], 1)
                        act.activation(RKV[:], RKV[:], ACT.Exp, scale=-0.5).then_inc(kv_rstd[l], 1)
                    if tile == "nq0":
                        act.wait_ge(q_stat[l], 1)
                        rq = SQQ[:, 0, 0:w]
                        act.activation(rq, STAT[:, 0:w], ACT.Ln, bias=EPSC, scale=1.0 / 256).then_inc(q_ln[l], 1)
                        act.wait_ge(q_ln[l], 1)
                        act.activation(rq, rq, ACT.Exp, scale=-0.5).then_inc(q_rstd[l], 1)
                for s in range(2):
                    act.dma_start(DFT[:, s, :], dft[s]).then_inc(dft_in[l][s], 16)
                act.wait_ge(kr_ready[l], 1)
                for h in range(HEADS):
                    last = act.activation(KTT[64:96, h, :], KRT[64:96, :], ACT.Copy)
                last.then_inc(kt_ready[l], 1)
                for i, job in enumerate(JOBS[l]):
                    n = G_JOB[l] + i
                    if job[:2] == "ab":
                        continue
                    act.wait_ge(job_done, JD[l] + i + 1)
                    j = int(job[-1])
                    free = g_free[n % 2]
                    if job[:2] == "kn":
                        act.activation(KTT[0:64, j, :], G[n % 2][0:64, 0:T], ACT.Copy).then_inc(free, 1)
                    elif job[0] == "q":
                        act.activation(QT[0:64, j, 0:w], G[n % 2][0:64, 0:w], ACT.Copy).then_inc(q_nope[l], 1)
                    else:
                        V = VM if job[:2] == "vm" else VN
                        act.activation(V[:, 3 * j:3 * j + 3, :].rearrange("p t d -> p (t d)"), G[n % 2][:, 0:T],
                                       ACT.Copy).then_inc(free, 1)
                    if job == "kn3":
                        conv_squares(l)
                    if job == "q0":
                        conv_rstd(l)
                    if l == 0 and i % 6 == 3:
                        mod_copy(MOD0 + i // 6)
                conv_tiles(l)
                slices = 5 if l == 0 else 4
                for s in range(2, slices):
                    act.wait_ge(dft_used[l], s - 1)
                    act.dma_start(DFT[:, s % 2, :], dft[s]).then_inc(dft_in[l][s % 2], 16)
                if l == 0:
                    mod_copy(7)
                for ct in range(2):
                    n = G_DFT[l] + ct
                    act.wait_ge(job_done, JD[l] + len(JOBS[l]) + ct + 1)
                    pieces = [(0, LAT, G[n % 2][:, 0:LAT], ACT.Copy, dict(scale=(LAT * HD) ** -0.5), False)]
                    if l == 0:
                        pieces.append((LAT, T, G[n % 2][:, LAT:T], ACT.Copy, dict(scale=(CTX * HD) ** -0.5), False))
                    cat_tile(l, 2 + ct, pieces)
                attention(l, 0)
                for p in range(P_OUT[l], P_OUT[l] + AHEAD):
                    split_hi(p % RAWS, p)
                attention(l, 1)
                k = 2 * l + 1
                for m in range(KT):
                    if ORDER[P_OUT[l] + m + AHEAD][:3] != "mod":
                        split_hi((P_OUT[l] + m + AHEAD) % RAWS, P_OUT[l] + m + AHEAD)
                    if m:
                        square(k, m - 1, w, G_OUT[l] + m - 1)
                square(k, KT - 1, w, G_OUT[l] + KT - 1)
                rstd(k, w)
                modulate(k, l, 1, w)

                def chunk(l, j, last_chunk):
                    w = T if l == 0 else LAT
                    steps = FF_STEPS[l]
                    for idx, (kind, i) in enumerate(steps):
                        q = P_FF[l] + idx + AHEAD
                        nxt = split_ahead(l, idx, last_chunk)
                        if nxt and nxt[0]:
                            turn = (q // RAWS + 1) + j * (len(steps) // RAWS)
                            act.wait_ge(raw_in[q % RAWS], turn * 16)
                            act.activation(WHI[:, q % RAWS, :], RAW[:, q % RAWS, :], ACT.Copy).then_inc(hi_done, 1)
                        if kind == "m":
                            continue
                        n = G_FF[l] + i
                        if i < KT:
                            act.wait_ge(w_used, j * (2 * KT) + (ON_PE[P_FF[l]] + i + 1))
                            if i >= 2:
                                act.wait_ge(hid_lo[l], j * KT + (i - 1))
                            act.activation(RELU[:, i % 2, 0:w], G[n % 2][:, 0:w], ACT.Relu).then_inc(
                                g_free[n % 2], 1)
                            act.wait_ge(g_free[n % 2], j * KT + (n // 2 + 1))
                            act.activation(SQF[:, i % 2, 0:w], RELU[:, i % 2, 0:w], ACT.Square)
                            act.activation(CHI[:, i, 0:w], RELU[:, i % 2, 0:w], ACT.Square).then_inc(hid_hi[l], 1)
                        elif last_chunk and i > KT:
                            square(2 * l + 2, i - KT - 1, w, n - 1 + 16 * (FFC - 1))
                    if last_chunk:
                        square(2 * l + 2, KT - 1, w, G_FF[l] + 16 * FFC - 1)

                with act.Fori(0, FFC - 1) as j:
                    chunk(l, j, False)
                chunk(l, FFC - 1, True)
            rstd(4, LAT)

        @block.tensor
        def _(pe):
            def three(dst, wk, k_slot, hi, lo, kt, w, start, stop):
                wcol = slice(wk * P, (wk + 1) * P)
                for wt, xt, first, last in ((WHI, hi, True, False), (WHI, lo, False, False), (WLO, hi, False, True)):
                    for a, b in spans(w):
                        mm = pe.matmul(dst[:, a:b], wt[:, k_slot, wcol], xt[:, kt, a:b], start=start and first,
                                       stop=stop and last)
                return mm

            def mod_first(c):
                pe.wait_ge(mpro_dve, (c + 1) * (KT + len(V1_DVE)))
                pe.wait_ge(mpro_pool, (c + 1) * (2 * len(V1_POOL) - 1))
                if c:
                    pe.wait_ge(mod_done, c)
                for i in range(4):
                    for v, parts in enumerate(([0], [1, 2])):
                        for n, a in enumerate(parts):
                            mm = pe.matmul(MODCOL[:, i, v:v + 1], ACCP[:, c, a, i * P:(i + 1) * P], ONES[:, 0:1],
                                           start=(n == 0), stop=(n == len(parts) - 1))
                mm.then_inc(mod_col, 1)

            def mod_late(c):
                pe.wait_ge(mod_step, c * (4 * MPARTS) - 4 * MPARTS * (12 - 1))
                pe.wait_ge(mod_done, c)
                for v in range(2):
                    mm = pe.matmul(MODSUM[v], ONES[:], ACC[:, v, :], start=True, stop=True)
                mm.then_inc(mod_col, 1)

            def mod_panel(m):
                p, s = P_MOD + m, m % MPARTS
                pe.wait_ge(raw_in[p % RAWS], 16 * (p // RAWS + 1))
                if s == 0:
                    pe.wait_ge(mod_done, MOD0 + m // MPARTS)
                for kk in range(2):
                    mm = pe.matmul(MODACC[0:2, :], CSILU[:, 2 * s + kk, :], RAW[:, p % RAWS, 512 * kk:512 * (kk + 1)],
                                   start=(s == 0 and kk == 0), stop=(s == MPARTS - 1 and kk == 1))
                mm.then_inc(w_used, 1)

            def mod_turn(c):
                pe.wait_ge(mod_row, c - MOD0 + 1)
                for i in range(4):
                    mm = pe.transpose(MODTP[:, i * P:(i + 1) * P], MODROW[:, i * P:(i + 1) * P], IDENT[:])
                mm.then_inc(mod_col, 1)

            def stat(k, kt, w):
                pe.wait_ge(sq_ready, KT * k + kt + 1)
                for a, b in spans(w):
                    mm = pe.matmul(STAT[:, a:b], ONES[:], SQ[:, kt % 2, a:b], start=(kt == 0), stop=(kt == KT - 1))
                mm.then_inc(sq_used, 1)

            def attention(l, a):
                us = units(l, a)
                per, ph = len(us) // 2, len(us) // HEADS

                def scores(u):
                    h, q, c = us[u]
                    if u >= S_RING[a]:
                        pe.wait_ge(exp_done[l][a], u - S_RING[a] + 1)
                    q0 = (LAT if c else 0) + q * P
                    if a == 0:
                        hp = slice(HD * (h % 2), HD * (h % 2) + HD)
                        lhs = NAQ[hp, h // 2, q0:q0 + P]
                        keys = [(0, LAT, T)] if c else [(0, WINDOW0[q], WINDOW0[q] + 256), (256, LAT, T)]
                        src = [(o, NAK[hp, h // 2, x0:x1]) for o, x0, x1 in keys]
                    else:
                        lhs = QT[0:96, h, q0:q0 + P]
                        keys = [(0, LAT, T)] if c else [(0, 0, LAT), (LAT, LAT, T)]
                        src = [(o, KTT[0:96, h, x0:x1]) for o, x0, x1 in keys]
                    S = s_at(a, u, 768 if a else 512)
                    for o, k in src:
                        mm = pe.matmul(S[:, o:o + k.shape[-1]], lhs, k, start=True, stop=True)
                    mm.then_inc(s_ready[l][a], 1)

                def turn(u):
                    h, q, c = us[u]
                    n = (CTX if c else (LAT, T)[a]) // P
                    pe.wait_ge(pn_ready[l][a], u + 1)
                    if u >= T_RING[a]:
                        pe.wait_ge(pt_ready[l][a], u - T_RING[a] + 1)
                    tp = t_at(a, u, n * P)
                    for t in range(n):
                        mm = pe.transpose(tp[:, t * P:(t + 1) * P], PEXP[:, u % P_RING, t * P:(t + 1) * P], IDENT[:])
                    mm.then_inc(t_ready[l][a], 1)

                def values(u):
                    h, q, c = us[u]
                    pe.wait_ge(pt_ready[l][0], u + 1)
                    if u >= per:
                        pe.wait_ge(cat_hi[l], 5)
                    if c:
                        tiles = [4, 5]
                    else:
                        tiles = {0: [0, 1], 1: [6, 7], 2: [7, 8], 3: [2, 3]}[q] + [4, 5]
                    dst = av_at(0, int(c))[HD * (h % 2):HD * (h % 2) + HD, q * P:(q + 1) * P]
                    for t, vt in enumerate(tiles):
                        mm = pe.matmul(dst, VN[:, vt, HD * h:HD * h + HD], PTN[:, u % P_RING, t, :],
                                       start=(t == 0), stop=(t == len(tiles) - 1))
                    mm.then_inc(pt_used[l][0], 1)

                def values_head(s):
                    for h in range(HEADS):
                        r = s - (h * ph + 6 + (h >= 2))
                        if not 0 <= r < ph:
                            continue
                        if r == 0:
                            pe.wait_ge(pt_ready[l][1], h * ph + 4)
                            if h == 2:
                                pe.wait_ge(cat_hi[l], 7)
                        rows = slice(HD * (h % 2), HD * (h % 2) + HD)
                        if l == 0 and r == 3:
                            pe.wait_ge(pt_ready[l][1], h * ph + 6)
                            for t in (4, 5):
                                mm = pe.matmul(av_at(1, 1)[rows, 0:CTX], VM[:, t, HD * h:HD * h + HD],
                                               PTC[:, h % 2, t - 4, :], start=(t == 4), stop=(t == 5))
                            mm.then_inc(pt_used[l][1], 1)
                        for t in [[r], {0: [0, 1], 1: [2, 3], 2: [4], 3: [5]}.get(r)][ph == 4]:
                            mm = pe.matmul(av_at(1, 0)[rows, 0:LAT], VM[:, t, HD * h:HD * h + HD], PTM[h % 2][:, t, :],
                                           start=(t == 0), stop=(t == 5))
                        if r == ph - 1:
                            mm.then_inc(pt_used[l][1], 1)

                la, lb = 2, 3
                for s in range(len(us) + (4 if a == 0 else 7)):
                    if s < len(us):
                        scores(s)
                    if 0 <= s - la < len(us):
                        turn(s - la)
                    if a == 1:
                        values_head(s)
                    elif 0 <= s - lb < per:
                        values(s - lb)
                    elif per <= s - lb - 1:
                        values(s - lb - 1)
                    if l == 0 and a == 0 and s < 24:
                        if s % 6 < 4:
                            mod_panel(16 + 4 * (s // 6) + s % 6)
                        if s % 6 == 5:
                            mod_turn(8 + s // 6)

            def conv_mean(l):
                w = T if l == 0 else LAT
                pe.wait_ge(conv_step[l], 2 * TAPS)
                for ct in range(2):
                    for a, b in spans(w):
                        s = 0 if a == 0 else CTX0 - LAT
                        mm = pe.matmul(STAT[:, a:b], ONES[:], CACC[:, ct, a + s:b + s], start=(ct == 0), stop=(ct == 1))
                mm.then_inc(mean_done[l], 1)

            def conv_variance(l):
                w = T if l == 0 else LAT
                pe.wait_ge(cen_done[l], 2)
                for ct in range(2):
                    pe.wait_ge(csq_done[l], ct + 1)
                    for a, b in spans(w):
                        mm = pe.matmul(STAT[:, a:b], ONES[:], SQC[:, ct, a:b], start=(ct == 0), stop=(ct == 1))
                mm.then_inc(var_done[l], 1)

            pe.wait_ge(consts, 2)
            pe.wait_ge(ones_set, 1)
            for kt in range(KT):
                stat(0, kt, T)
            for c in range(MOD0):
                mod_first(c)

            for l in L2:
                w = T if l == 0 else LAT
                k = 2 * l
                for i in range(16):
                    p = P_IN[l] + i
                    pe.wait_ge(lo_done, WEIGHTS[p] + 1)
                    n = G_IN[l] + i
                    if n >= 2:
                        pe.wait_ge(g_free[n % 2], n // 2)
                    wt = width(l, TILES[i])
                    for kt in range(KT):
                        if i == 0:
                            pe.wait_ge(hlo_ready, KT * k + kt + 1)
                        mm = three(G[n % 2], kt, p % RAWS, HHI, HLO, kt, wt, kt == 0, kt == KT - 1)
                    mm.then_inc(w_used, 1)
                    if TILES[i] == "q1":
                        pe.wait_ge(*in_sq(l, "kv"))
                        for a, b in spans(T):
                            mm = pe.matmul(STAT[:, a:b], ONES[:], RKV[:, a:b], start=True, stop=True)
                        mm.then_inc(kv_stat[l], 1)
                    if TILES[i] == "f1":
                        pe.wait_ge(*in_sq(l, "q1"))
                        pe.wait_ge(kv_ln[l], 1)
                        for ct in range(2):
                            for a, b in spans(w):
                                mm = pe.matmul(STAT[:, a:b], ONES[:], SQQ[:, ct, a:b], start=(ct == 0), stop=(ct == 1))
                        mm.then_inc(q_stat[l], 1)
                conv_mean(l)
                pe.wait_ge(wu_in[l], 32)
                pe.wait_ge(kvn_ready[l], 1)
                for i, job in enumerate(JOBS[l]):
                    n = G_JOB[l] + i
                    j = int(job[-1])
                    pe.wait_ge(g_free[n % 2], n // 2)
                    dst = G[n % 2]
                    if job[:2] == "kn":
                        for a, b in spans(T):
                            mm = pe.matmul(dst[0:64, a:b], WUKV[:, 64 * j:64 * j + 64], KVA[:, a:b], start=True, stop=True)
                    elif job[:2] == "vm":
                        for t in range(3):
                            mm = pe.matmul(dst[:, 256 * t:256 * t + 256], KVA[:, (3 * j + t) * P:(3 * j + t + 1) * P],
                                           WUKV[:, 256:512], start=True, stop=True)
                    elif job[0] == "q":
                        if j == 0:
                            pe.wait_ge(qn_ready[l], 1)
                        for ct in range(2):
                            for a, b in spans(w):
                                mm = pe.matmul(dst[:, a:b], WUQ[:, ct, P * j:P * j + P], QA[:, ct, a:b], start=(ct == 0),
                                               stop=(ct == 1))
                    elif job[:2] == "vn":
                        for t in range(3):
                            vt = 3 * j + t
                            t0 = vt * P if vt < 6 else 64 + (vt - 6) * P
                            for ct in range(2):
                                mm = pe.transpose(dst[:, 256 * t + P * ct:256 * t + P * ct + P], NAVT[:, ct, t0:t0 + P],
                                                  IDENT[:])
                    else:
                        if j == 0:
                            pe.wait_ge(const_in, 16)
                        for ct in range(2):
                            mm = pe.matmul(dst[:, 256 * ct:256 * ct + 256], FU[:, ct, P * j:P * j + P], CSD[:], start=True,
                                           stop=True)
                    mm.then_inc(job_done, 1)
                    if job == "vm1":
                        conv_variance(l)
                    if l == 0 and i % 6 < 4 and i < 18:
                        mod_panel(4 * (i // 6) + i % 6)
                    if l == 0 and i % 6 == 5:
                        mod_turn(MOD0 + i // 6)
                n = G_DFT[l]
                pe.wait_ge(g_free[n % 2], n // 2)
                pe.wait_ge(g_free[(n + 1) % 2], (n + 1) // 2)
                for s in range(4):
                    pe.wait_ge(dft_in[l][s % 2], 16 * (s // 2 + 1))
                    for ct in range(2):
                        for cs in range(2):
                            mm = pe.matmul(G[(n + ct) % 2][:, 0:LAT], AB[ct][:, s, cs * P:(cs + 1) * P],
                                           DFT[:, s % 2, cs * 512:(cs + 1) * 512], start=(s == 0 and cs == 0),
                                           stop=(s == 3 and cs == 1))
                        if l == 1 and s == 3:
                            mm.then_inc(job_done, 1)
                    if l == 0 or s < 3:
                        mm.then_inc(dft_used[l], 1)
                    if l == 0:
                        mod_panel(12 + s)
                if l == 0:
                    pe.wait_ge(dft_in[l][0], 48)
                    for ct in range(2):
                        for s in range(2):
                            for cs in range(2):
                                mm = pe.matmul(G[(n + ct) % 2][:, LAT:T], AB[ct][:, 4 + s, cs * P:(cs + 1) * P],
                                               DFT[:, 0, cs * 512 + s * 256:cs * 512 + (s + 1) * 256],
                                               start=(s == 0 and cs == 0), stop=(s == 1 and cs == 1))
                        mm.then_inc(job_done, 1)
                if l == 0:
                    mod_turn(7)
                pe.wait_ge(crstd_done[l], 1)
                pe.wait_ge(cat_hi[l], 4)
                attention(l, 0)
                if l == 0:
                    pe.wait_ge(mod_done, 12)
                attention(l, 1)
                k = 2 * l + 1
                for m in range(KT):
                    p, n = P_OUT[l] + m, G_OUT[l] + m
                    pe.wait_ge(lo_done, WEIGHTS[p] + 1)
                    pe.wait_ge(g_free[n % 2], n // 2)
                    for f, kt in enumerate(CAT_ORDER):
                        if m == 0:
                            pe.wait_ge(cat_lo[l], f + 1)
                        mm = three(G[n % 2], kt, p % RAWS, CHI, CLO, kt, w, f == 0, f == KT - 1)
                    mm.then_inc(w_used, 1)
                    if m >= 2:
                        stat(k, m - 2, w)
                stat(k, KT - 2, w)
                stat(k, KT - 1, w)

                def chunk(l, j, last_chunk):
                    w = T if l == 0 else LAT
                    steps = FF_STEPS[l]
                    for idx, (kind, i) in enumerate(steps):
                        p = P_FF[l] + idx
                        if kind == "m":
                            continue
                        pe.wait_ge(lo_done, j * (2 * KT) + (WEIGHTS[p] + 1))
                        n = G_FF[l] + i
                        pe.wait_ge(g_free[n % 2], j * 8 + n // 2)
                        for kt in range(KT):
                            if i < KT:
                                if i == 0:
                                    pe.wait_ge(hlo_ready, KT * (2 * l + 1) + kt + 1)
                                mm = three(G[n % 2], kt, p % RAWS, HHI, HLO, kt, w, kt == 0, kt == KT - 1)
                            else:
                                if i == KT:
                                    pe.wait_ge(hid_lo[l], j * KT + (kt + 1))
                                mm = three(G[n % 2], kt, p % RAWS, CHI, CLO, kt, w, kt == 0, kt == KT - 1)
                        mm.then_inc(w_used, 1)
                        if l == 0 and i in (3, 8, 13):
                            mod_late(j * 3 + (12 + i // 5))
                        if last_chunk and i >= KT + 2:
                            stat(2 * l + 2, i - KT - 2, w)
                    if last_chunk:
                        stat(2 * l + 2, KT - 2, w)
                        stat(2 * l + 2, KT - 1, w)

                with pe.Fori(0, FFC - 1) as j:
                    chunk(l, j, False)
                chunk(l, FFC - 1, True)

        @block.vector
        def _(dve):
            def split_lo(i, p):
                dve.wait_ge(hi_done, p + 1)
                dve.tensor_tensor(WLO[:, i, :], RAW[:, i, :], WHI[:, i, :].bitcast(F32),
                                  ALU.subtract).then_inc(lo_done, 1)

            def mod_turned(c, src):
                dve.wait_ge(mod_col, c + 1)
                for v in range(2):
                    last = dve.tensor_tensor(MODT[:, 0, 4 * c:4 * c + 4, v], src[:, :, v],
                                             pcol(0, PB + 4 * c, 4), ALU.add)
                last.then_inc(mod_done, 1)

            def mod_finish(l, c, cc):
                dve.wait_ge(mod_col, c + 1)
                for v in range(2):
                    last = dve.tensor_tensor(ACC[:, v, :].rearrange("p (i r) -> p i r", r=P),
                                             MODSUM[v].rearrange("p (i r) -> p i r", r=P),
                                             IDENT[:].unsqueeze(1).broadcast_to([P, 4, P]), ALU.mult)
                last.then_inc(mod_diag, 1)
                dve.wait_ge(mod_diag, cc + 1)
                for v in range(2):
                    last = dve.tensor_reduce(MT[:, v, :], ACC[:, v, :].rearrange("p (i r) -> p i r", r=P), AX_X, ALU.add)
                last.then_inc(mod_part, 1)
                dve.wait_ge(mod_part, cc + 1)
                for v in range(2):
                    last = dve.tensor_tensor(MODT[:, l, bass.ds(4 * cc, 4), v], MT[:, v, :],
                                             PAR[:, bass.ds(l * PL + PB + 4 * cc, 4)], ALU.add)
                last.then_inc(mod_done, 1)

            def mod_partial(p, s, m, j):
                c = m // MPARTS
                if s == 0 and m:
                    mod_finish(1, j * 3 + (12 + c - 1), j * 3 + (c - 1))
                dve.wait_ge(raw_in[p % RAWS], j * (16 * len(FF_STEPS[0]) // RAWS) + 16 * (p // RAWS + 1))
                for kk in range(2):
                    for v in range(2):
                        n = 2 * kk + v
                        src = RAW[:, p % RAWS, 512 * kk:512 * (kk + 1)]
                        cs = CSILU[:, 2 * s + kk, v:v + 1]
                        if s == 0 and kk == 0:
                            if v == 0:
                                dve.wait_ge(mod_done, j * 3 + (12 + c))
                            dve.tensor_scalar(ACC[:, v, :], src, cs, None, ALU.mult).then_inc(mod_step, 1)
                        else:
                            dve.wait_ge(mod_step, j * 48 + (4 * m + n - 1))
                            dve.scalar_tensor_tensor(ACC[:, v, :], src, cs, ACC[:, v, :], ALU.mult,
                                                     ALU.add).then_inc(mod_step, 1)

            def coef(l, n):
                for v in range(2):
                    last = dve.scalar_tensor_tensor(AC[:, l, n, :, v], MODT[:, l, (SC1, SC2)[n]:(SC1, SC2)[n] + KT, v], 1.0,
                                                    pcol(l, (PG1, PG2)[n], KT), ALU.add, ALU.mult)
                last.then_inc(ac_ready, 1)

            def normalize(k, w):
                dve.wait_ge(rstd_ready, k + 1)
                for kt in range(KT + 1):
                    if kt < KT:
                        if kt >= 2:
                            dve.wait_ge(hhi_ready, KT * k + kt - 1)
                        dve.tensor_tensor(XN[:, kt % 2, 0:w], X[:, kt, 0:w], RSTD[:, 0:w], ALU.mult).then_inc(
                            xn_ready, 1)
                    if kt:
                        q = kt - 1
                        dve.wait_ge(hhi_ready, KT * k + q + 1)
                        dve.tensor_tensor(HLO[:, q, 0:w], HT[:, q % 2, 0:w], HHI[:, q, 0:w].bitcast(F32),
                                          ALU.subtract).then_inc(hlo_ready, 1)

            def cat_low(l, f):
                w = T if l == 0 else LAT
                c = CAT_ORDER[f]
                dve.wait_ge(cat_hi[l], f + 1)
                dve.tensor_tensor(CLO[:, c, 0:w], CTMP[:, 0:w], CHI[:, c, 0:w].bitcast(F32), ALU.subtract).then_inc(
                    cat_lo[l], 1)

            def residual(l, m, n, gate, w):
                for v, (a, b) in enumerate(spans(w)):
                    last = dve.scalar_tensor_tensor(X[:, m, a:b], G[n % 2][:, a:b], MODT[:, l, gate + m, v:v + 1],
                                                    X[:, m, a:b], ALU.mult, ALU.add)
                last.then_inc(g_free[n % 2], 1)

            def attention(l, a):
                us = units(l, a)
                per = len(us) // 2

                def maxima(u):
                    h, q, c = us[u]
                    n = CTX if c else (LAT, T)[a]
                    dve.wait_ge(s_ready[l][a], u + 1)
                    S = s_at(a, u, n)
                    if a == 0 and not c:
                        dve.tensor_tensor(S[:, 0:256], S[:, 0:256], BM[:, VARIANT[q], h, :], ALU.add).then_inc(
                            s_bias[l][0], 1)
                        dve.wait_ge(s_bias[l][0], len([1 for x in us[:u + 1] if not x[2]]))
                    if a == 0:
                        dve.tensor_reduce(NMX[:, a, u:u + 1], S, AX_X, ALU.max, negate=True).then_inc(nm_ready[l][a], 1)
                    else:
                        dve.tensor_reduce(RIN[:, a, u:u + 1], S, AX_X, ALU.max, negate=True).then_inc(s_bias[l][1], 1)
                        dve.wait_ge(s_bias[l][1], u + 1)
                        dve.tensor_scalar(NMX[:, a, u:u + 1], RIN[:, a, u:u + 1], MLA_SCALE, None, ALU.mult).then_inc(
                            nm_ready[l][a], 1)

                def norm(u):
                    h, q, c = us[u]
                    n = CTX if c else (LAT, T)[a]
                    dve.wait_ge(exp_done[l][a], u + 1)
                    dve.reciprocal(RIN[:, a, u:u + 1], SUM[:, a, u:u + 1]).then_inc(ri_ready[l][a], 1)
                    dve.wait_ge(ri_ready[l][a], u + 1)
                    pr = PEXP[:, u % P_RING, 0:n]
                    dve.tensor_scalar(pr, pr, RIN[:, a, u:u + 1], None, ALU.mult).then_inc(pn_ready[l][a], 1)

                if a == 0:
                    dve.wait_ge(bias_in[l], 16)
                for s in range(len(us) + (5 if a == 0 else 8)):
                    if s < len(us):
                        maxima(s)
                    if 1 <= s <= len(us):
                        norm(s - 1)
                    if s in ((per + 3, 2 * per + 4) if a == 0 else (per + 7, 2 * per + 7)):
                        cat_low(l, (4, 6)[a] + (0 if s < 2 * per else 1))
                    if l == 0 and a == 0 and s % 6 == 5 and s < 24:
                        mod_turned(8 + s // 6, MODTPV)

            def glu(l, ct):
                if ct == 0:
                    dve.wait_ge(pads_ready, l + 1)
                dve.wait_ge(*in_sq(l, f"a{ct}"))
                dve.wait_ge(*in_sq(l, f"g{ct}"))
                y = YPAD[:, ct, HALO:HALO + LAT].rearrange("p (r c) -> p c r", r=ROWS)
                last = dve.tensor_tensor(y, CACC[:, ct, 0:LAT].rearrange("p (c r) -> p c r", r=ROWS),
                                         SIG[:, 0:LAT].rearrange("p (c r) -> p c r", r=ROWS), ALU.mult)
                if l == 0:
                    last = dve.tensor_tensor(YPAD[:, ct, CTX0 + HALO:CTX0 + HALO + CTX], CACC[:, ct, LAT:T],
                                             SIG[:, LAT:T], ALU.mult)
                last.then_inc(glu_done[l], 1)

            def conv_tap(l, at):
                ct, tap = CONV_ORDER[at]
                wide = CONVW if l == 0 else LAT
                acc, y = CACC[:, ct, 0:wide], YPAD[:, ct, tap:tap + wide]
                if tap == 0:
                    dve.wait_ge(glu_done[l], ct + 1)
                    dve.tensor_scalar(acc, y, pcol(l, PCW + ct), pcol(l, PCB + ct), ALU.mult, ALU.add).then_inc(
                        conv_step[l], 1)
                else:
                    dve.wait_ge(conv_step[l], CONV_ORDER.index((ct, tap - 1)) + 1)
                    dve.scalar_tensor_tensor(acc, y, pcol(l, PCW + 2 * tap + ct), acc, ALU.mult, ALU.add).then_inc(
                        conv_step[l], 1)

            def conv_center(l):
                w = T if l == 0 else LAT
                dve.wait_ge(mean_done[l], 1)
                for ct in range(2):
                    for a, b in spans(w):
                        s = 0 if a == 0 else CTX0 - LAT
                        y = CACC[:, ct, a + s:b + s]
                        last = dve.scalar_tensor_tensor(y, STAT[:, a:b], -1.0 / 256, y, ALU.mult, ALU.add)
                    last.then_inc(cen_done[l], 1)

            def conv_low(l):
                w = T if l == 0 else LAT
                dve.wait_ge(crstd_done[l], 1)
                for ct in range(2):
                    for a, b in spans(w):
                        s = 0 if a == 0 else CTX0 - LAT
                        y = CACC[:, ct, a + s:b + s]
                        last = dve.tensor_tensor(y, y, RSTDC[:, a:b], ALU.mult)
                    last.then_inc(cn_done[l], 1)

            dve.memset(ONES[:], 1.0).then_inc(ones_set, 1)
            dve.memset(MODROW[:], 0.0).then_inc(row_zero, 1)
            dve.wait_ge(c_ready, 1)
            turns = []
            for n in range(KT):
                turns.append((0, n))
                if n < len(V1_DVE):
                    turns.append((1, V1_DVE[n]))
            for c in range(MOD0):
                dve.wait_ge(mpro_in[c], 16)
                for n, (v, kt) in enumerate(turns):
                    src = MPRO[c][:, kt // 2, 512 * (kt % 2):512 * (kt % 2 + 1)]
                    before = [i for i in range(n) if turns[i][0] == v]
                    if before:
                        dve.wait_ge(mpro_dve, c * len(turns) + before[-1] + 1)
                        dve.scalar_tensor_tensor(ACCP[:, c, v, :], src, CSILU[:, kt, v:v + 1], ACCP[:, c, v, :],
                                                 ALU.mult, ALU.add).then_inc(mpro_dve, 1)
                    else:
                        dve.tensor_scalar(ACCP[:, c, v, :], src, CSILU[:, kt, v:v + 1], None, ALU.mult).then_inc(
                            mpro_dve, 1)
                if c:
                    mod_turned(c - 1, MODCOL)
            for p in range(AHEAD):
                split_lo(p, p)
            mod_turned(MOD0 - 1, MODCOL)
            dve.wait_ge(mod_done, 4)
            coef(0, 0)

            for l in L2:
                w = T if l == 0 else LAT
                k = 2 * l
                if l == 1:
                    dve.wait_ge(mod_done, 24)
                    coef(1, 0)
                    coef(1, 1)
                normalize(k, T)
                for i in range(16):
                    p = P_IN[l] + i
                    if i + AHEAD < 16:
                        split_lo((p + AHEAD) % RAWS, WEIGHTS[p + AHEAD])
                    tile, n = TILES[i], G_IN[l] + i
                    if tile in ("a1", "kv"):
                        glu(l, 0 if tile == "a1" else 1)
                    if i >= 2:
                        for c in range(CONV_STEP * (i - 2), min(CONV_STEP * (i - 1), 2 * TAPS)):
                            conv_tap(l, c)
                    if tile == "kr":
                        dve.wait_ge(rope_in[l], 16)
                        dve.wait_ge(w_used, ON_PE[p] + 1)
                        dve.tensor_tensor(KRT[64:96, :], G[n % 2][64:96, 0:T], CS[64:96, :], ALU.mult)
                        dve.tensor_tensor(ROT[64:96, :], G[n % 2][96:128, 0:T], CS[96:128, :], ALU.mult).then_inc(
                            g_free[n % 2], 1)
                        dve.wait_ge(g_free[n % 2], n // 2 + 1)
                        dve.tensor_tensor(KRT[64:96, :], KRT[64:96, :], ROT[64:96, :], ALU.add).then_inc(kr_ready[l], 1)
                    if tile == "f0":
                        dve.wait_ge(kv_rstd[l], 1)
                        dve.scalar_tensor_tensor(KVA[:], KVA[:], pcol(l, PKVN), RKV[:], ALU.mult, ALU.mult).then_inc(
                            kvn_ready[l], 1)
                    if tile == "nq0":
                        dve.wait_ge(q_rstd[l], 1)
                        for ct in range(2):
                            last = dve.scalar_tensor_tensor(QA[:, ct, 0:w], QA[:, ct, 0:w], pcol(l, PQN + ct),
                                                            SQQ[:, 0, 0:w], ALU.mult, ALU.mult)
                        last.then_inc(qn_ready[l], 1)
                conv_center(l)
                for i, job in enumerate(JOBS[l]):
                    n = G_JOB[l] + i
                    j = int(job[-1])
                    if job[0] == "q":
                        dve.wait_ge(q_nope[l], j + 1)
                        if j:
                            dve.wait_ge(q_part[l], 2 * j)
                        dve.tensor_tensor(QT[64:96, j, 0:w], G[n % 2][64:96, 0:w], CS[64:96, 0:w], ALU.mult)
                        dve.tensor_tensor(ROT[64:96, 0:w], G[n % 2][96:128, 0:w], CS[96:128, 0:w], ALU.mult).then_inc(
                            g_free[n % 2], 1)
                        dve.wait_ge(g_free[n % 2], n // 2 + 1)
                        dve.tensor_tensor(QT[64:96, j, 0:w], QT[64:96, j, 0:w], ROT[64:96, 0:w], ALU.add).then_inc(
                            q_part[l], 2)
                        if j == HEADS - 1:
                            conv_low(l)
                    elif job[:2] == "ab":
                        dve.wait_ge(job_done, JD[l] + i + 1)
                        dve.tensor_copy(AB[0][:, j, :], G[n % 2][:, 0:256])
                        dve.tensor_copy(AB[1][:, j, :], G[n % 2][:, 256:512]).then_inc(g_free[n % 2], 1)
                    if l == 0 and i % 6 == 5:
                        mod_turned(MOD0 + i // 6, MODTPV)
                for f in range(4):
                    cat_low(l, f)
                if l == 0:
                    mod_turned(7, MODTPV)
                attention(l, 0)
                if l == 0:
                    dve.wait_ge(mod_done, 12)
                    coef(0, 1)
                for p in range(P_OUT[l], P_OUT[l] + AHEAD):
                    split_lo(p % RAWS, WEIGHTS[p])
                attention(l, 1)
                k = 2 * l + 1
                for m in range(KT):
                    p, n = P_OUT[l] + m, G_OUT[l] + m
                    if ORDER[p + AHEAD][:3] != "mod":
                        split_lo((p + AHEAD) % RAWS, WEIGHTS[p + AHEAD])
                    else:
                        mod_partial(p + AHEAD, ON_DVE[p + AHEAD], ON_DVE[p + AHEAD], 0)
                    dve.wait_ge(w_used, ON_PE[p] + 1)
                    residual(l, m, n, GT1, w)
                normalize(k, w)

                def chunk(l, j, last_chunk):
                    w = T if l == 0 else LAT
                    steps = FF_STEPS[l]
                    for idx, (kind, i) in enumerate(steps):
                        q = P_FF[l] + idx + AHEAD
                        nxt = split_ahead(l, idx, last_chunk)
                        if nxt and nxt[0]:
                            split_lo(q % RAWS, j * (2 * KT) + nxt[1])
                        elif nxt:
                            mod_partial(q, nxt[1] % MPARTS, nxt[1], j)
                        if kind == "m":
                            continue
                        n = G_FF[l] + i
                        if i < KT:
                            dve.wait_ge(hid_hi[l], j * KT + (i + 1))
                            dve.tensor_tensor(CLO[:, i, 0:w], SQF[:, i % 2, 0:w], CHI[:, i, 0:w].bitcast(F32),
                                              ALU.subtract).then_inc(hid_lo[l], 1)
                        else:
                            dve.wait_ge(w_used, j * (2 * KT) + (ON_PE[P_FF[l]] + i + 1))
                            residual(l, i - KT, n, GT2, w)
                        if l == 0 and last_chunk and i == 14:
                            mod_finish(1, 23, 11)

                with dve.Fori(0, FFC - 1) as j:
                    chunk(l, j, False)
                chunk(l, FFC - 1, True)

            dve.wait_ge(rstd_ready, 4 + 1)
            for kt in range(KT):
                if kt >= 2:
                    dve.wait_ge(out_sent[kt % 2], 16 * (kt // 2))
                dve.scalar_tensor_tensor(OUTT[:, kt % 2, :], X[:, kt, 0:LAT], PAR[:, PF + kt:PF + kt + 1], RSTD[:, 0:LAT],
                                         ALU.mult, ALU.mult).then_inc(out_ready, 1)

        @block.gpsimd
        def _(pool):
            pool.memset(IDENT[:], 0.0).then_inc(consts, 1)
            pool.wait_ge(consts, 1)
            pool.affine_select(out=IDENT[:], in_=IDENT[:], compare_op=ALU.not_equal, fill=1.0, base=0,
                               pattern=[[-1, P]], channel_multiplier=1).then_inc(consts, 1)
            pool.wait_ge(c_ready, 1)
            step = 0
            for c in range(MOD0):
                pool.wait_ge(mpro_in[c], 16)
                for n, kt in enumerate(V1_POOL):
                    src = MPRO[c][:, kt // 2, 512 * (kt % 2):512 * (kt % 2 + 1)]
                    dst = ACC[:, 0, :] if n else ACCP[:, c, 2, :]
                    if n:
                        pool.wait_ge(mpro_pool, step)
                    pool.tensor_scalar(dst, src, CSILU[:, kt, 1:2], None, ALU.mult).then_inc(mpro_pool, 1)
                    step += 1
                    if n:
                        pool.wait_ge(mpro_pool, step)
                        pool.tensor_tensor(ACCP[:, c, 2, :], ACCP[:, c, 2, :], dst, ALU.add).then_inc(mpro_pool, 1)
                        step += 1
            for l in L2:
                pool.wait_ge(hlo_ready, KT * (2 * l) + KT)
                pool.memset(YPAD[:], 0.0).then_inc(pads_ready, 1)


def kernel(**inputs):
    import numpy as np
    import concourse.bacc as bacc
    from concourse.bass_utils import run_bass_kernel_spmd

    a = {k: np.asarray(v) for k, v in inputs.items()}

    def panel(w):
        kk, m = w.shape
        return w.reshape(kk // P, P, m // P, P).transpose(2, 1, 0, 3).reshape(m // P, P, kk)

    order = np.arange(LAT).reshape(ROWS, COLS).T.reshape(-1)
    x = np.concatenate([a["x"][0][order], a["ctx"][0]], 0)
    x = x.reshape(T, KT, P).transpose(2, 1, 0)

    swap = np.concatenate([np.arange(16, 32), np.arange(16)])
    kv0, kr0, nq0 = 256, 384, 416
    fn0, cv0 = 1184, 1440
    packed = {}
    for l in range(LAYERS):
        w = a["w_in"][l]
        kr = w[:, kr0:kr0 + 32]
        cols = [w[:, cv0:cv0 + 128], w[:, cv0 + 256:cv0 + 384], w[:, cv0 + 128:cv0 + 256], w[:, cv0 + 384:cv0 + 512],
                w[:, kv0:kv0 + 128], np.concatenate([kr, kr[:, swap]] * 2, 1), w[:, 0:256], w[:, fn0:fn0 + 256],
                w[:, nq0:nq0 + 768]]
        packed["in", l] = panel(np.concatenate(cols, 1))
        packed["out", l] = panel(a["w_out"][l])
        packed["ff1", l] = panel(a["w_ff1"][l])
        packed["ff2", l] = [panel(a["w_ff2"][l][D * j:D * (j + 1)]) for j in range(FFC)]
        packed["mod", l] = a["w_mod"][l].reshape(4, 2, P, 12, 512).transpose(3, 0, 2, 1, 4).reshape(12, 4, P, 1024)
    panels = np.empty((NPANEL, P, 1024), np.float32)
    mods = packed["mod", 0][:MOD0].reshape(MOD0 * MPARTS, P, 1024)
    for p, (name, l, *at) in enumerate(panel_order()):
        part = packed[name[:3] if name[:3] == "mod" else name, l]
        for i in at:
            part = part[i]
        panels[p] = part

    def columns(v):
        return v.reshape(-1, P).T

    par = []
    for l in range(LAYERS):
        par += [columns(a["b_mod"][l]), columns(a["norm1_g"][l]), columns(a["norm2_g"][l]), columns(a["mla_q_norm"][l]),
                columns(a["mla_kv_norm"][l]), columns(a["cv_w_dw"][l]), columns(a["cv_b_dw"][l]),
                columns(a["cv_ln_g"][l]), columns(a["cv_ln_b"][l])]
    par += [np.stack([columns(a["c"][0]), columns(a["c_ctx"])], 2).reshape(P, 2 * KT), columns(a["final_g"]),
            np.full((P, 1), EPS, np.float32)]
    par = np.concatenate(par, 1)

    uq = a["mla_w_uq"].reshape(LAYERS, 2, P, HEADS, 96)
    uq = np.concatenate([uq, uq[..., 64 + swap]], -1).transpose(0, 2, 1, 3, 4).reshape(LAYERS, P, 2, 512)
    ukv = a["mla_w_ukv"].reshape(LAYERS, P, HEADS, 2, HD).transpose(0, 1, 3, 2, 4).reshape(LAYERS, P, 512)

    bias = np.empty((LAYERS, P, 3, HEADS, 256), np.float32)
    qc, qr = np.repeat(np.arange(16), ROWS), np.tile(np.arange(ROWS), 16)
    kc, kr = np.repeat(np.arange(32), ROWS), np.tile(np.arange(ROWS), 32)
    for v, block in enumerate((0, 1, 3)):
        col, key = 16 * block + qc[:, None], WINDOW0[block] // ROWS + kc[None, :]
        start = np.clip(col - 8, 0, COLS - 16)
        inside = (key >= start) & (key < start + 16)
        rel = np.clip(key - col + 15, 0, 30)
        rows = kr[None, :] - qr[:, None] + 7
        bias[:, :, v] = np.where(inside[None, :, None, :], a["na_rpb"][:, :, rows, rel].transpose(0, 2, 1, 3),
                                 np.float32(-1e30))

    inv = 10000.0 ** (-np.arange(0, 16, 2, dtype=np.float32) / np.float32(16))
    t = order
    ang = np.concatenate([(t // COLS)[:, None] * inv, (t % COLS)[:, None] * inv], 1).astype(np.float32)
    rope = np.zeros((64, T), np.float32)
    rope[0:32] = 1.0
    rope[0:32, :LAT] = np.tile(np.cos(ang), (1, 2)).T
    rope[32:48, :LAT] = -np.sin(ang).T
    rope[48:64, :LAT] = np.sin(ang).T

    n = np.arange(HD)
    w = 2 * np.pi * np.outer(n, n) / HD
    z = np.zeros((HD, HD))
    dft_ch = np.concatenate([np.block([[np.cos(w), z], [z, np.cos(w)]]), np.block([[-np.sin(w), z], [z, -np.sin(w)]])],
                            1).astype(np.float32)
    w = 2 * np.pi * (np.outer(order, order) % LAT) / LAT
    dft = np.concatenate([np.cos(w).reshape(4, P, LAT), np.sin(w).reshape(4, P, LAT)], 2)
    n = np.arange(CTX)
    w = (2 * np.pi * (np.outer(n, n) % CTX) / CTX).reshape(2, P, CTX).transpose(1, 0, 2).reshape(1, P, 512)
    dft = np.concatenate([dft, np.concatenate([np.cos(w), np.sin(w)], 2)], 0).astype(np.float32)

    nc = bacc.Bacc("TRN2", target_bir_lowering=False, num_devices=1)
    arrays, args = {}, []
    for name, v in dict(x=x, panels=panels, mods=mods, par=par, w_uq=uq, w_ukv=ukv, bias=bias, rope=rope, dft=dft,
                        dft_ch=dft_ch).items():
        arrays[f"in_{name}"] = np.ascontiguousarray(v)
        args.append(nc.dram_tensor(f"in_{name}", v.shape, F32, kind="ExternalInput").ap())
    args.append(nc.dram_tensor("out_y", (P, KT, LAT), F32, kind="ExternalOutput").ap())
    trunk(nc, *args)
    y = run_bass_kernel_spmd(nc, [arrays], core_ids=[0]).results[0]["out_y"]
    y = np.asarray(y).transpose(2, 1, 0).reshape(LAT, D)
    back = np.arange(LAT).reshape(COLS, ROWS).T.reshape(-1)
    return y[back].reshape(1, LAT, D)
```

```python
from contextlib import ExitStack

import concourse.bass as bass
from concourse import mybir

F32 = mybir.dt.float32
F32R = mybir.dt.float32r
ACT = mybir.ActivationFunctionType
ALU = mybir.AluOpType
AX_X = mybir.AxisListType.X

P = 128
D = 1024
KT = D // P
LAT, CTX = 512, 256
T = LAT + CTX
LAYERS = 2
ROWS, COLS = 8, 64
HEADS = 4
HD = 64
FFC = 4
TAPS, HALO = 31, 15
CTX0 = HALO + LAT + HALO
PADW = CTX0 + CTX + 2 * HALO
CONVW = PADW - 2 * HALO
EPS = 1e-6
MLA_SCALE = 96 ** -0.5
NA_SCALE = HD ** -0.5
WINDOW0 = [0, 64, 192, 256]
VARIANT = [0, 1, 1, 2]

PB, PG1, PG2, PQN, PKVN, PCW, PCB, PLG, PLB = 0, 48, 56, 64, 66, 67, 129, 131, 133
PL = 135
PC = LAYERS * PL
PF = PC + 2 * KT
PE_ = PF + KT
NPAR = PE_ + 1
SH1, SC1, GT1, SH2, SC2, GT2 = (KT * i for i in range(6))

TILES = ["a0", "g0", "a1", "g1", "kv", "kr", "q0", "q1", "f0", "f1", "nq0", "nq1", "nk0", "nk1", "nv0", "nv1"]
KEYS = {"kv", "kr", "nk0", "nk1", "nv0", "nv1"}


CONV_STEP = 5
CONV_ORDER = [(0, k) for k in range(2 * CONV_STEP)]
for _k in range(TAPS):
    CONV_ORDER += [(1, _k)] + ([(0, _k + 2 * CONV_STEP)] if _k + 2 * CONV_STEP < TAPS else [])


MOD0, MPARTS = 4, 4


FF_STEPS = []
for _i in range(16):
    FF_STEPS.append(("g", _i))
    if 2 <= _i < 15:
        FF_STEPS += [("m", None)] * (2 if _i in (2, 7, 11) else 1)
_m = iter(range(16))
FF_STEPS = [(k, next(_m) if k == "m" else i) for k, i in FF_STEPS]
PLAIN_STEPS = [("g", i) for i in range(16)]


def steps_of(l, last_chunk):
    return PLAIN_STEPS if l == 1 or last_chunk else FF_STEPS


def panel_order():
    order = [("in", 0, i) for i in range(16)]
    order += [("modp", 0, c, s) for c in range(MOD0, 12) for s in range(MPARTS)]
    order += [("out", 0, i) for i in range(8)]
    m1 = [("modd", 1, c, s) for c in range(12) for s in range(MPARTS)]
    for j in range(FFC):
        for kind, i in steps_of(0, j == FFC - 1):
            if kind == "m":
                order.append(m1[16 * j + i])
            else:
                order.append(("ff1", 0, 8 * j + i) if i < 8 else ("ff2", 0, j, i - 8))
    order += [("in", 1, i) for i in range(16)] + [("out", 1, i) for i in range(8)]
    for j in range(FFC):
        order += [("ff1", 1, 8 * j + i) for i in range(8)] + [("ff2", 1, j, i) for i in range(8)]
    return order


ORDER = [o[0] for o in panel_order()]
NPANEL = len(ORDER)
WEIGHTS = [sum(o[:3] != "mod" for o in ORDER[:p]) for p in range(NPANEL)]
ON_PE = [sum(o != "modd" for o in ORDER[:p]) for p in range(NPANEL)]
ON_DVE = [sum(o == "modd" for o in ORDER[:p]) for p in range(NPANEL)]
P_MOD = 16
P_IN, P_OUT, P_FF, P_LAST = [0, 168], [48, 184], [56, 192], [152, 240]
assert NPANEL == P_LAST[1] + 16
RAWS = 4
AHEAD = RAWS - 1
AT = {s: n for n, s in enumerate(FF_STEPS)}
SUM_BEHIND = [max(i for i in range(16) if AT["g", i] < (AT["m", m + 1] - AHEAD if m < 15 else 99)) for m in (3, 7, 11, 15)]
assert all(AT["g", i] >= AT["m", 4 * c + 3] - AHEAD for c, i in enumerate(SUM_BEHIND))

SWEEPS = [[(0, LAT), (LAT, T)], [(0, LAT // 2), (LAT // 2, LAT)]]
NORMS = 2 * LAYERS + 1
BOTH = KT // 2
TAIL = KT + BOTH


def sweeps(k):
    return SWEEPS[0 if k <= 2 else 1]


def tail_step(k, t):
    at_once = SWEEPS[0] if k <= 2 else [(0, LAT)]
    return (t if t < KT else t - BOTH), (at_once if t < BOTH else [sweeps(k)[t >= KT]])


def whole(over):
    return over[0][0], over[-1][1]



def trunk(nc, x, panels, mods, par, w_uq, w_ukv, bias, rope, dft, dft_ch, out):
    ctx = ExitStack()
    with ctx:
        base = (nc.sbuf_base + 31) // 32 * 32
        places = {}

        def at(name, shape, dt, offset):
            places[name] = offset
            return nc.alloc_sbuf_tensor_at(name, shape, dt, offset=base + offset)

        top = [0]

        def new(name, shape, dt=F32, size=None):
            n = 4
            for s in shape[1:]:
                n *= s
            o = top[0]
            top[0] += ((size or n) + 31) // 32 * 32
            return at(name, shape, dt, o)

        ROW = T * 4
        X = new("X", [P, KT, T])
        HHI = new("HHI", [P, KT, T], F32R)
        HLO = new("HLO", [P, KT, T], F32R)
        CHI = new("CHI", [P, KT, T], F32R)
        CLO = new("CLO", [P, KT, T], F32R)
        RAW = new("RAW", [P, RAWS, 1024])
        WLO = at("WLO", [P, RAWS, 1024], F32R, places["RAW"])
        WHI = new("WHI", [P, RAWS, 1024], F32R)
        YPAD = new("YPAD", [P, 2, PADW])
        NAQ = new("NAQ", [P, 2, T])
        NAK = new("NAK", [P, 2, T])
        CACC = new("CACC", [P, 2, CONVW])
        BM = new("BM", [P, 3, HEADS, 256])
        CS = new("CS", [P, T])
        CSD = new("CSD", [P, 256])
        IDENT = new("IDENT", [P, P])
        ONES = new("ONES", [P, P])
        PAR = new("PAR", [P, NPAR])
        MODT = new("MODT", [P, LAYERS, 48, 2])
        AC = new("AC", [P, LAYERS, 2, KT, 2])
        CSILU = new("CSILU", [P, KT, 2])
        MODROW = new("MODROW", [P, 512])
        ACC = new("ACC", [P, 2, 512])
        MT = new("MT", [P, 2, 4])
        NMX = new("NMX", [P, 2, 24])
        SUM = new("SUM", [P, 2, 24])
        RIN = new("RIN", [P, 2, 24])
        assert base + top[0] <= nc.sbuf_usable_end, (base + top[0], nc.sbuf_usable_end)

        MPRO = [at(f"MPRO{c}", [P, MPARTS, 1024], F32, o) for c, o in enumerate(
            [places["CHI"], places["CHI"] + 16384, places["CHI"] + 32768, places["HHI"]])]
        h0 = places["HHI"]
        QT = at("QT", [P, HEADS, T], F32, h0)
        KTT = at("KTT", [P, HEADS, T], F32, h0 + 4 * ROW)
        VM = at("VM", [P, 6, 256], F32, h0 + 8 * ROW)
        VN = at("VN", [P, 9, 256], F32, h0 + 10 * ROW)
        PEXP = at("PEXP", [P, 3, T], F32, h0 + 13 * ROW)
        DFT = at("DFT", [P, 2, 1024], F32, h0 + 13 * ROW)
        c0, l0 = places["CHI"], places["CLO"]
        QA = at("QA", [P, 2, T], F32, l0)
        WUQ = at("WUQ", [P, 2, 512], F32, l0 + 2 * ROW)
        WUKV = at("WUKV", [P, 512], F32, l0 + 2 * ROW + 4096)
        NAVT = at("NAVT", [P, 2, T], F32, l0 + 4 * ROW)
        SIG = at("SIG", [P, T], F32, l0 + 6 * ROW)
        PTN = at("PTN", [P, 3, 4, P], F32, places["YPAD"])
        RSTDC = at("RSTDC", [P, T], F32, l0 + 6 * ROW)
        KVA = at("KVA", [P, T], F32, c0)
        RKV = at("RKV", [P, T], F32, c0 + ROW)
        SQQ = at("SQQ", [P, 2, T], F32, c0 + 2 * ROW)
        AB = [at("AB0", [P, 6, 256], F32, c0 + 2 * ROW), at("AB1", [P, 6, 256], F32, l0 + 2 * ROW)]
        FU = at("FU", [P, 2, T], F32, c0 + 4 * ROW)
        KRT = at("KRT", [P, T], F32, c0 + 6 * ROW)
        ROT = at("ROT", [P, T], F32, c0 + 7 * ROW)
        SQC = at("SQC", [P, 2, T], F32, l0 + 6 * ROW)
        RSTD = at("RSTD", [P, T], F32, places["YPAD"])
        SQA = at("SQA", [P, T], F32, places["YPAD"] + ROW)
        PTC = at("PTC", [P, 2, 2, CTX], F32, places["YPAD"])
        XN = at("XN", [P, 2, T], F32, places["NAQ"])
        HT = at("HT", [P, 2, T], F32, places["NAK"])
        SQ = at("SQ", [P, 2, T], F32, places["CACC"])
        RELU = at("RELU", [P, 2, T], F32, places["NAQ"])
        SQF = at("SQF", [P, 2, T], F32, places["NAK"])
        PTM = [at("PTM0", [P, 6, LAT], F32, places["NAQ"]), at("PTM1", [P, 6, LAT], F32, places["BM"])]
        CTMP = at("CTMP", [P, T], F32, places["CS"])
        OUTT = at("OUTT", [P, KT, LAT], F32, h0)

        PS = ctx.enter_context(nc.psum_tensor("PS", [P, 8 * 512], F32))
        G = [PS[:, 0:1024], PS[:, 1024:2048]]
        bank = [PS[:, 512 * b:512 * (b + 1)] for b in range(8)]
        STAT = PS[:, 2048:2048 + T]
        MODACC, MODSUM = [bank[7], bank[6]], [bank[7], bank[6]]

        def sem(name):
            return ctx.enter_context(nc.semaphore(name))

        raw_in = [sem(f"raw_in{i}") for i in range(RAWS)]
        hi_done, lo_done, w_used = sem("hi_done"), sem("lo_done"), sem("w_used")
        held_done = sem("held_done")
        job_done, pads_ready = sem("job_done"), sem("pads_ready")
        g_free = [sem("g_free0"), sem("g_free1")]
        par_in, x_in, const_in, c_ready, row_zero, ones_set, consts = (
            sem(n) for n in ("par_in", "x_in", "const_in", "c_ready", "row_zero", "ones_set", "consts"))
        mpro_in = [sem(f"mpro_in{c}") for c in range(MOD0)]
        mpro_used, mod_step, mod_row, mod_col, mod_diag, mod_part, mod_done = (
            sem(n) for n in ("mpro_used", "mod_step", "mod_row", "mod_col", "mod_diag", "mod_part",
                             "mod_done"))
        ac_ready = sem("ac_ready")
        (sq_ready, sq_used, total_first, sq_added, total_done, ln_done, rstd_ready, ht_ready, xn_ready, hhi_ready,
         hlo_ready) = (
            sem(n) for n in ("sq_ready", "sq_used", "total_first", "sq_added", "total_done", "ln_done", "rstd_ready",
                             "ht_ready", "xn_ready", "hhi_ready", "hlo_ready"))
        L2 = range(LAYERS)

        def per_layer(*names):
            return ([sem(f"{n}_l{k}") for k in L2] for n in names)

        (bias_in, rope_in, wu_in, glu_done, conv_step, kv_stat, kv_ln, kv_rstd, q_stat, q_ln,
         q_rstd, kvn_ready, qn_ready, kr_ready, q_nope, q_part, kt_ready,
         dft_used, cat_hi, cat_lo) = per_layer(
            "bias_in", "rope_in", "wu_in", "glu_done", "conv_step", "kv_stat", "kv_ln",
            "kv_rstd", "q_stat", "q_ln", "q_rstd", "kvn_ready", "qn_ready", "kr_ready", "q_nope",
            "q_part", "kt_ready", "dft_used", "cat_hi", "cat_lo")
        dft_in = [[sem(f"dft_in{s}_l{k}") for s in range(2)] for k in L2]
        (mean_done, cen_done, csq_done, var_done, cln_done, crstd_done, cn_done) = per_layer(
            "mean_done", "cen_done", "csq_done", "var_done", "cln_done", "crstd_done", "cn_done")
        def per_att(n):
            return [[sem(f"{n}_{a}_l{k}") for a in ("na", "mla")] for k in L2]

        (s_ready, s_bias, nm_ready, exp_done, ri_ready, pn_ready, t_ready, pt_ready, pt_used) = (
            per_att(n) for n in ("s_ready", "s_bias", "nm_ready", "exp_done", "ri_ready", "pn_ready", "t_ready",
                                 "pt_ready", "pt_used"))
        hid_hi, hid_lo = per_layer("hid_hi", "hid_lo")
        out_ready, out_sent = sem("out_ready"), sem("out_sent")

        def pcol(l, c, n=1):
            return PAR[:, l * PL + c:l * PL + c + n]

        EPSC = PAR[:, PE_:PE_ + 1]

        def nth(k, g):
            return 2 * (k - 1) + g

        def width(l, tile):
            return T if l == 0 or tile in KEYS else LAT

        def spans(w):
            return [(0, LAT)] if w == LAT else [(0, LAT), (LAT, T)]

        G_IN = [0]
        JOBS = [["kn0", "kn1", "vm0", "vm1", "q0", "q1", "q2", "q3", "vn0", "vn1", "vn2"]
                + [f"ab{t}" for t in range(6 if l == 0 else 4)] for l in L2]
        G_JOB = [16]
        G_DFT = [G_JOB[0] + len(JOBS[0])]
        G_OUT = [G_DFT[0]]
        G_FF = [G_OUT[0] + TAIL]
        G_IN.append(G_FF[0] + 64 + BOTH)
        G_JOB.append(G_IN[1] + 16)
        G_DFT.append(G_JOB[1] + len(JOBS[1]))
        G_OUT.append(G_DFT[1])
        G_FF.append(G_OUT[1] + TAIL)
        JD = [0, len(JOBS[0]) + 2]

        def units(l, a):
            if a == 0:
                return [u for hh in range(2) for u in
                        [(2 * hh + p, q, False) for q in range(4) for p in range(2)]
                        + ([(2 * hh + p, q, True) for q in range(2) for p in range(2)] if l == 0 else [])]
            return [u for h in range(HEADS) for u in
                    [(h, q, False) for q in range(4)] + ([(h, q, True) for q in range(2)] if l == 0 else [])]

        def n_att(l):
            return len(units(l, 0)), len(units(l, 1))

        S_RING, T_RING, P_RING = [3, 2], [2, 1], 3

        def s_at(a, u, n):
            return PS[:, (512, 1024)[a] * (u % S_RING[a]):][:, 0:n]

        def t_at(a, u, n):
            return bank[3 + u % 2][:, 0:n] if a == 0 else PS[:, 2048:2048 + n]

        def av_at(a, c):
            return bank[(5, 6)[a] + c]

        CONV_AT = [dict(mean="kn1", squares="vm0", variance="q0", rstd="q1"),
                   dict(mean=None, squares="kn1", variance="vm1", rstd="q0")]

        CAT_ORDER = [6, 7, 4, 5, 2, 3, 0, 1]

        def in_sq(l, tile):
            n = G_IN[l] + TILES.index(tile)
            return g_free[n % 2], n // 2 + 1

        def split_ahead(l, idx, last_chunk):
            q = (P_LAST if last_chunk else P_FF)[l] + idx + AHEAD
            if ORDER[q] == "modd":
                return False, ON_DVE[q]
            return True, WEIGHTS[q] - (FFC - 1) * 2 * KT * last_chunk

        def ahead_in_tail(p0, t):
            q = p0 + (t + AHEAD if t <= BOTH else t - 1 if t > KT else NPANEL)
            return q if q < NPANEL else None

        block = ctx.enter_context(nc.Block())

        @block.sync
        def _(sp):
            def load(i, p):
                sp.dma_start(RAW[:, i, :], panels[p, :, :]).then_inc(raw_in[i], 16)

            def place_free(p, j=0, pe=0, dv=0):
                if ORDER[p] == "modd":
                    sp.wait_ge(mod_step, j * (4 * dv) + 4 * (ON_DVE[p] + 1))
                else:
                    sp.wait_ge(w_used, j * pe + (ON_PE[p] + 1))

            def stream(first, count):
                with sp.Fori(0, count // RAWS) as j:
                    for i in range(RAWS):
                        place_free(first + i - RAWS, j, RAWS)
                        load(i, j * RAWS + (first + i))

            sp.dma_start(PAR[:], par).then_inc(par_in, 16)
            for c in range(MOD0):
                sp.dma_start(MPRO[c][:], mods[MPARTS * c:MPARTS * (c + 1)].rearrange("s p m -> p s m")).then_inc(
                    mpro_in[c], 16)
                if c == 0:
                    sp.dma_start(X[:], x).then_inc(x_in, 16)
            for p in range(RAWS):
                load(p, p)
            sp.dma_start(CSD[:], dft_ch).then_inc(const_in, 16)
            sp.dma_start(CS[64:P, :], rope).then_inc(rope_in[0], 16)
            sp.dma_start(BM[:], bias[0]).then_inc(bias_in[0], 16)
            for l in L2:
                sp.wait_ge(w_used, ON_PE[P_IN[l]] + 1)
                sp.dma_start(WUQ[:], w_uq[l]).then_inc(wu_in[l], 16)
                sp.dma_start(WUKV[:], w_ukv[l]).then_inc(wu_in[l], 16)
                if l == 0:
                    stream(RAWS, P_FF[0] - RAWS)
                    for i in range(RAWS):
                        place_free(P_FF[0] + i - RAWS)
                        load(i, P_FF[0] + i)
                    sp.dma_start(BM[:], bias[1]).then_inc(bias_in[1], 16)
                    sp.dma_start(CS[64:P, :], rope).then_inc(rope_in[1], 16)
                    n = len(FF_STEPS)
                    with sp.Fori(0, FFC - 1) as j:
                        for i in range(n):
                            place_free(P_FF[0] + i, j, 2 * KT, n - 2 * KT)
                            load(i % RAWS, j * n + (P_FF[0] + RAWS + i))
                    stream(P_LAST[0] + RAWS, 2 * KT)
            stream(P_IN[1] + RAWS, NPANEL - P_IN[1] - RAWS)
            for g, (a, b) in enumerate(sweeps(NORMS - 1)):
                for kt in range(0, KT, 2):
                    sp.wait_ge(out_ready, KT * g + kt + 2)
                    sp.dma_start(out[:, kt:kt + 2, a:b], OUTT[:, kt:kt + 2, a:b]).then_inc(out_sent, 16)
            sp.wait_ge(out_sent, 16 * KT)

        @block.scalar
        def _(act):
            def split_hi(i, p):
                act.wait_ge(raw_in[i], slot_turn(p) * 16)
                act.activation(WHI[:, i, :], RAW[:, i, :], ACT.Copy).then_inc(hi_done, 1)

            def mod_copy(c):
                if c:
                    act.wait_ge(mod_col, c)
                else:
                    act.wait_ge(row_zero, 1)
                if c < MOD0:
                    act.wait_ge(mpro_used, c + 1)
                else:
                    act.wait_ge(w_used, P_MOD + MPARTS * (c - MOD0 + 1))
                act.activation(MODROW[0:2, :], MODACC[c % 2 if c < MOD0 else 0][0:2, :], ACT.Copy).then_inc(mod_row, 1)

            def slot_turn(p):
                return p // RAWS + 1

            def square(k, t, n0):
                kt, over = tail_step(k, t)
                a, b = whole(over)
                n = n0 + t
                act.wait_ge(g_free[n % 2], n // 2 + 1)
                if t >= 3:
                    act.wait_ge(sq_added, (TAIL - 1) * (k - 1) + t - 2)
                dst = SQ[:, t % 2, a:b] if t else SQA[:, a:b]
                act.activation(dst, X[:, kt, a:b], ACT.Square, scale=D ** -0.5).then_inc(sq_ready, 1)

            def rstd(dst, src, ln, n, done):
                act.activation(dst, src, ACT.Ln, bias=EPSC).then_inc(ln, 1)
                act.wait_ge(ln, n)
                act.activation(dst, dst, ACT.Exp, scale=-0.5).then_inc(done, 1)

            def rstd_sweep(k, g):
                a, b = sweeps(k)[g]
                act.wait_ge(total_done, nth(k, g) + 1)
                rstd(RSTD[:, a:b], STAT[:, a:b], ln_done, nth(k, g) + 2, rstd_ready)

            def modulate(k, g, kt):
                l, n = k // 2, k % 2
                act.wait_ge(ac_ready, k + 1)
                act.wait_ge(xn_ready, KT * (2 * k + g) + kt + 1)
                a, b = sweeps(k)[g]
                v = int(a == LAT)
                sh = MODT[:, l, (SH1, SH2)[n] + kt, v:v + 1]
                ac = AC[:, l, n, kt, v:v + 1]
                act.activation(HHI[:, kt, a:b], XN[:, kt % 2, a:b], ACT.Identity, bias=sh, scale=ac).then_inc(
                    hhi_ready, 1)

            def tail(k, p0, n0):
                for t in range(TAIL):
                    q = ahead_in_tail(p0, t)
                    if t <= BOTH:
                        split_hi(q % RAWS, q)
                    if t == KT + 1:
                        rstd_sweep(k, 0)
                    if t:
                        square(k, t - 1, n0)
                    if t > KT + 1 and k < NORMS - 1:
                        for kt in range(2):
                            modulate(k, 0, 2 * (t - KT - 2) + kt)
                    if t > KT and q:
                        split_hi(q % RAWS, q)
                square(k, TAIL - 1, n0)
                if k < NORMS - 1:
                    modulate(k, 0, BOTH)
                    modulate(k, 0, BOTH + 1)
                rstd_sweep(k, 1)
                if k < NORMS - 1:
                    for kt in range(BOTH + 2, KT):
                        modulate(k, 0, kt)
                    for kt in range(KT):
                        modulate(k, 1, kt)

            def cat_tile(l, f, pieces):
                if f:
                    act.wait_ge(cat_lo[l], f)
                c = CAT_ORDER[f]
                for a, b, src, func, kw, perm in pieces:
                    for dst in (CTMP[:, a:b], CHI[:, c, a:b]):
                        if perm:
                            dst = dst.rearrange("p (c r) -> p c r", r=ROWS)
                        last = act.activation(dst, src, func, **kw)
                last.then_inc(cat_hi[l], 1)

            def attention(l, a):
                us = units(l, a)
                f = (4, 6)[a]

                def probs(u):
                    h, q, c = us[u]
                    n = CTX if c else (LAT, T)[a]
                    act.wait_ge(nm_ready[l][a], u + 1)
                    if u >= P_RING:
                        act.wait_ge(t_ready[l][a], u - P_RING + 1)
                    act.activation(PEXP[:, u % P_RING, 0:n], s_at(a, u, n), ACT.Exp, bias=NMX[:, a, u:u + 1],
                                   scale=(1.0, MLA_SCALE)[a], accum_out=SUM[:, a, u:u + 1]).then_inc(
                        exp_done[l][a], 1)

                def turned(u):
                    h, q, c = us[u]
                    act.wait_ge(t_ready[l][a], u + 1)
                    if a == 0:
                        n = CTX if c else LAT
                        if u >= P_RING:
                            act.wait_ge(pt_used[l][a], u - P_RING + 1)
                        dst = PTN[:, u % P_RING, 0:n // P, :]
                        src = t_at(a, u, n).rearrange("p (t q) -> p t q", q=P)
                    else:
                        n = CTX if c else T
                        if h >= 2 and q == 0:
                            act.wait_ge(pt_used[l][a], (2 * (h - 2) + (1 if c else 2)) if l == 0 else h - 1)
                        big = PTC[:, h % 2, :, :] if c else PTM[h % 2][:, :, :]
                        dst = big[:, :, q * P:(q + 1) * P]
                        src = t_at(a, u, n).rearrange("p (t q) -> p t q", q=P)
                    act.activation(dst, src, ACT.Copy).then_inc(pt_ready[l][a], 1)

                def finish(hh):
                    act.wait_ge(pt_used[l][a], (hh + 1) * (len(us) // 2 if a == 0 else 4 if l == 0 else 2))
                    pieces = [(0, LAT, av_at(a, 0), ACT.Copy, {}, False)]
                    if l == 0:
                        pieces.append((LAT, T, av_at(a, 1)[:, 0:CTX], ACT.Copy, {}, False))
                    cat_tile(l, f + hh, pieces)

                lag = 2
                per = len(us) // 2
                if a == 0:
                    act.wait_ge(conv_step[l], 2 * TAPS)
                for s in range(len(us) + (5 if a == 0 else 8)):
                    if s in ((per + 3, 2 * per + 4), (per + 6, 2 * per + 7))[a]:
                        finish(0 if s < 2 * per else 1)
                    if s < len(us):
                        probs(s)
                    if 0 <= s - lag < len(us):
                        turned(s - lag)
                    if l == 0 and a == 0 and s % 6 == 4 and s < 24:
                        mod_copy(8 + s // 6)

            def conv_squares(l):
                w = T if l == 0 else LAT
                for ct in range(2):
                    act.wait_ge(cen_done[l], ct + 1)
                    for a, b in spans(w):
                        s = 0 if a == 0 else CTX0 - LAT
                        last = act.activation(SQC[:, ct, a:b], CACC[:, ct, a + s:b + s], ACT.Square,
                                              scale=256 ** -0.5)
                    last.then_inc(csq_done[l], 1)

            def conv_rstd(l):
                w = T if l == 0 else LAT
                act.wait_ge(var_done[l], 1)
                rstd(RSTDC[:, 0:w], STAT[:, 0:w], cln_done[l], 1, crstd_done[l])

            def conv_tiles(l):
                act.wait_ge(q_part[l], 2 * HEADS)
                for ct in range(2):
                    if l == 0 and ct:
                        mod_copy(6)
                    act.wait_ge(cn_done[l], 2)
                    kw = dict(bias=pcol(l, PLB + ct), scale=pcol(l, PLG + ct))
                    pieces = [(0, LAT, CACC[:, ct, 0:LAT].rearrange("p (r c) -> p c r", r=ROWS), ACT.Silu, kw, True)]
                    if l == 0:
                        pieces.append((LAT, T, CACC[:, ct, CTX0:CTX0 + CTX], ACT.Silu, kw, False))
                    cat_tile(l, ct, pieces)

            act.wait_ge(par_in, 16)
            act.activation(CSILU[:].rearrange("p a b -> p (a b)"), PAR[:, PC:PC + 2 * KT], ACT.Silu).then_inc(c_ready, 1)
            act.wait_ge(x_in, 16)
            for kt in range(KT):
                if kt >= 3:
                    act.wait_ge(sq_used, kt - 2)
                act.activation(SQ[:, kt % 2, :] if kt else SQA[:], X[:, kt, :], ACT.Square, scale=D ** -0.5).then_inc(
                    sq_ready, 1)
            mod_copy(0)
            mod_copy(1)
            act.wait_ge(total_first, 1)
            rstd(RSTD[:], STAT, ln_done, 1, rstd_ready)
            for p in range(2):
                split_hi(p, p)
            mod_copy(2)
            mod_copy(3)

            for l in L2:
                w = T if l == 0 else LAT
                if l == 0:
                    for g in range(2):
                        for kt in range(KT):
                            modulate(0, g, kt)
                        if g == 0:
                            split_hi(2, 2)
                for i in range(16):
                    p = P_IN[l] + i
                    if i + AHEAD < 16:
                        split_hi((p + AHEAD) % RAWS, p + AHEAD)
                    tile, n = TILES[i], G_IN[l] + i
                    wt = width(l, tile)
                    src = G[n % 2][:, 0:wt]
                    if tile == "kr":
                        continue
                    act.wait_ge(w_used, ON_PE[p] + 1)
                    free = g_free[n % 2]
                    ct = int(tile[-1]) if tile[-1].isdigit() else 0
                    if tile[0] == "a":
                        act.activation(CACC[:, ct, 0:wt], src, ACT.Copy).then_inc(free, 1)
                    elif tile[0] == "g":
                        if ct:
                            act.wait_ge(glu_done[l], 1)
                        act.activation(SIG[:, 0:wt], src, ACT.Sigmoid).then_inc(free, 1)
                    elif tile == "kv":
                        act.activation(KVA[:, 0:wt], src, ACT.Copy)
                        act.activation(RKV[:, 0:wt], src, ACT.Square, scale=128 ** -0.5).then_inc(free, 1)
                    elif tile[0] == "q":
                        act.activation(QA[:, ct, 0:wt], src, ACT.Copy)
                        act.activation(SQQ[:, ct, 0:wt], src, ACT.Square, scale=256 ** -0.5).then_inc(free, 1)
                    else:
                        dst, sc = {"f": (FU, 1.0), "nq": (NAQ, NA_SCALE), "nk": (NAK, 1.0), "nv": (NAVT, 1.0)}[tile[:-1]]
                        act.activation(dst[:, ct, 0:wt], src, ACT.Copy, scale=sc).then_inc(free, 1)
                    if tile == "f0":
                        act.wait_ge(kv_stat[l], 1)
                        rstd(RKV[:], STAT, kv_ln[l], 1, kv_rstd[l])
                    if tile == "nq0":
                        act.wait_ge(q_stat[l], 1)
                        rstd(SQQ[:, 0, 0:w], STAT[:, 0:w], q_ln[l], 1, q_rstd[l])
                for s in range(2):
                    act.dma_start(DFT[:, s, :], dft[s]).then_inc(dft_in[l][s], 16)
                act.wait_ge(kr_ready[l], 1)
                for h in range(HEADS):
                    last = act.activation(KTT[64:96, h, :], KRT[64:96, :], ACT.Copy)
                last.then_inc(kt_ready[l], 1)
                for i, job in enumerate(JOBS[l]):
                    n = G_JOB[l] + i
                    if job[:2] == "ab":
                        continue
                    act.wait_ge(job_done, JD[l] + i + 1)
                    j = int(job[-1])
                    free = g_free[n % 2]
                    if job[:2] == "kn":
                        act.activation(KTT[0:64, 2 * j, :], G[n % 2][0:64, 0:T], ACT.Copy)
                        act.activation(KTT[0:64, 2 * j + 1, :], G[n % 2][64:128, 0:T], ACT.Copy).then_inc(free, 1)
                    elif job[0] == "q":
                        act.activation(QT[0:64, j, 0:w], G[n % 2][0:64, 0:w], ACT.Copy).then_inc(q_nope[l], 1)
                    else:
                        V = VM if job[:2] == "vm" else VN
                        act.activation(V[:, 3 * j:3 * j + 3, :].rearrange("p t d -> p (t d)"), G[n % 2][:, 0:T],
                                       ACT.Copy).then_inc(free, 1)
                    if job == CONV_AT[l]["squares"]:
                        conv_squares(l)
                    if job == CONV_AT[l]["rstd"]:
                        conv_rstd(l)
                    if l == 0 and i % 6 == 3:
                        mod_copy(MOD0 + i // 6)
                conv_tiles(l)
                slices = 5 if l == 0 else 4
                for s in range(2, slices):
                    act.wait_ge(dft_used[l], s - 1)
                    act.dma_start(DFT[:, s % 2, :], dft[s]).then_inc(dft_in[l][s % 2], 16)
                if l == 0:
                    mod_copy(7)
                for ct in range(2):
                    n = G_DFT[l] + ct
                    act.wait_ge(job_done, JD[l] + len(JOBS[l]) + ct + 1)
                    pieces = [(0, LAT, G[n % 2][:, 0:LAT], ACT.Copy, dict(scale=(LAT * HD) ** -0.5), False)]
                    if l == 0:
                        pieces.append((LAT, T, G[n % 2][:, LAT:T], ACT.Copy, dict(scale=(CTX * HD) ** -0.5), False))
                    cat_tile(l, 2 + ct, pieces)
                attention(l, 0)
                for p in range(P_OUT[l], P_OUT[l] + AHEAD):
                    split_hi(p % RAWS, p)
                attention(l, 1)
                tail(2 * l + 1, P_OUT[l], G_OUT[l])

                def chunk(l, j, last_chunk):
                    w = T if l == 0 else LAT
                    for idx, (kind, i) in enumerate(steps_of(l, last_chunk)):
                        if last_chunk and i == KT:
                            break
                        q = (P_LAST if last_chunk else P_FF)[l] + idx + AHEAD
                        if split_ahead(l, idx, last_chunk)[0]:
                            turn = q // RAWS + 1 if last_chunk else (q // RAWS + 1) + j * (len(steps_of(l, False)) // RAWS)
                            act.wait_ge(raw_in[q % RAWS], turn * 16)
                            act.activation(WHI[:, q % RAWS, :], RAW[:, q % RAWS, :], ACT.Copy).then_inc(hi_done, 1)
                        if kind == "m":
                            continue
                        n = G_FF[l] + i
                        if i < KT:
                            act.wait_ge(w_used, j * (2 * KT) + (ON_PE[P_FF[l]] + i + 1))
                            if i >= 2:
                                act.wait_ge(hid_lo[l], j * KT + (i - 1))
                            act.activation(RELU[:, i % 2, 0:w], G[n % 2][:, 0:w], ACT.Relu).then_inc(
                                g_free[n % 2], 1)
                            act.wait_ge(g_free[n % 2], j * KT + (n // 2 + 1))
                            act.activation(SQF[:, i % 2, 0:w], RELU[:, i % 2, 0:w], ACT.Square)
                            act.activation(CHI[:, i, 0:w], RELU[:, i % 2, 0:w], ACT.Square).then_inc(hid_hi[l], 1)

                with act.Fori(0, FFC - 1) as j:
                    chunk(l, j, False)
                chunk(l, FFC - 1, True)
                tail(2 * l + 2, P_LAST[l] + KT, G_FF[l] + 16 * FFC - KT)

        @block.tensor
        def _(pe):
            def three(dst, wk, k_slot, hi, lo, kt, over, start, stop):
                wcol = slice(wk * P, (wk + 1) * P)
                for wt, xt, first, last in ((WHI, hi, True, False), (WHI, lo, False, False), (WLO, hi, False, True)):
                    for a, b in over:
                        mm = pe.matmul(dst[:, a:b], wt[:, k_slot, wcol], xt[:, kt, a:b], start=start and first,
                                       stop=stop and last)
                return mm

            def mod_late(c):
                pe.wait_ge(mod_step, c * (4 * MPARTS) - 4 * MPARTS * (12 - 1))
                pe.wait_ge(mod_done, c)
                for v in range(2):
                    mm = pe.matmul(MODSUM[v], ONES[:], ACC[:, v, :], start=True, stop=True)
                mm.then_inc(mod_col, 1)

            def mod_rows(acc, w, s):
                for kk in range(2):
                    mm = pe.matmul(acc[0:2, :], CSILU[:, 2 * s + kk, :], w[:, 512 * kk:512 * (kk + 1)],
                                   start=(s == 0 and kk == 0), stop=(s == MPARTS - 1 and kk == 1))
                return mm

            def mod_first(c):
                pe.wait_ge(mpro_in[c], 16)
                if c >= 2:
                    pe.wait_ge(mod_done, c - 1)
                for s in range(MPARTS):
                    mm = mod_rows(MODACC[c % 2], MPRO[c][:, s, :], s)
                mm.then_inc(mpro_used, 1)

            def mod_panel(m):
                p, s = P_MOD + m, m % MPARTS
                pe.wait_ge(raw_in[p % RAWS], 16 * (p // RAWS + 1))
                if s == 0:
                    pe.wait_ge(mod_done, MOD0 + m // MPARTS)
                mod_rows(MODACC[0], RAW[:, p % RAWS, :], s).then_inc(w_used, 1)

            def mod_turn(c):
                pe.wait_ge(mod_row, c + 1)
                for i in range(4):
                    mm = pe.transpose(MODACC[c % 2 if c < MOD0 else 0][:, i * P:(i + 1) * P],
                                      MODROW[:, i * P:(i + 1) * P], IDENT[:])
                mm.then_inc(mod_col, 1)

            def total(k, g):
                a, b = sweeps(k)[g]
                pe.wait_ge(sq_added, (TAIL - 1) * k - (BOTH if g == 0 else 0))
                pe.matmul(STAT[:, a:b], ONES[:], SQA[:, a:b], start=True, stop=True).then_inc(total_done, 1)

            def tail(k, p0, n0):
                for t in range(TAIL):
                    m, over = tail_step(k, t)
                    p, n = p0 + m, n0 + t
                    pe.wait_ge(lo_done, WEIGHTS[p] + 1)
                    pe.wait_ge(g_free[n % 2], n // 2)
                    for f, kt in enumerate(CAT_ORDER if k % 2 else range(KT)):
                        if t == 0 and k % 2:
                            pe.wait_ge(cat_lo[k // 2], f + 1)
                        elif t == 0:
                            pe.wait_ge(hid_lo[k // 2 - 1], KT * (FFC - 1) + f + 1)
                        mm = three(G[n % 2], kt, p % RAWS, CHI, CLO, kt, over, f == 0, f == KT - 1)
                    mm.then_inc(held_done if BOTH <= t < KT else w_used, 1)
                    if t == KT:
                        total(k, 0)

            def first_two(k, panels_at, n, lo_count, j):
                for g in range(2):
                    for i in range(2):
                        if g == 0:
                            pe.wait_ge(lo_done, j * (2 * KT) + (lo_count + i + 1))
                            m = n + i
                            if m >= 2:
                                pe.wait_ge(g_free[m % 2], j * KT + m // 2)
                        for kt in range(KT):
                            if i == 0:
                                pe.wait_ge(hlo_ready, KT * (2 * k + g) + kt + 1)
                            if k and g == 0 and i == 0 and kt == KT // 2:
                                total(k, 1)
                            mm = three(G[(n + i) % 2], kt, panels_at[i] % RAWS, HHI, HLO, kt, [sweeps(k)[g]],
                                       kt == 0, kt == KT - 1)
                        if g:
                            mm.then_inc(w_used, 1)

            def total_of_first():
                pe.wait_ge(sq_used, KT - 1)
                for a, b in spans(T):
                    mm = pe.matmul(STAT[:, a:b], ONES[:], SQA[:, a:b], start=True, stop=True)
                mm.then_inc(total_first, 1)

            def attention(l, a):
                us = units(l, a)
                per, ph = len(us) // 2, len(us) // HEADS

                def scores(u):
                    h, q, c = us[u]
                    if u >= S_RING[a]:
                        pe.wait_ge(exp_done[l][a], u - S_RING[a] + 1)
                    q0 = (LAT if c else 0) + q * P
                    if a == 0:
                        hp = slice(HD * (h % 2), HD * (h % 2) + HD)
                        lhs = NAQ[hp, h // 2, q0:q0 + P]
                        keys = [(0, LAT, T)] if c else [(0, WINDOW0[q], WINDOW0[q] + 256), (256, LAT, T)]
                        src = [(o, NAK[hp, h // 2, x0:x1]) for o, x0, x1 in keys]
                    else:
                        lhs = QT[0:96, h, q0:q0 + P]
                        keys = [(0, LAT, T)] if c else [(0, 0, LAT), (LAT, LAT, T)]
                        src = [(o, KTT[0:96, h, x0:x1]) for o, x0, x1 in keys]
                    S = s_at(a, u, 768 if a else 512)
                    for o, k in src:
                        mm = pe.matmul(S[:, o:o + k.shape[-1]], lhs, k, start=True, stop=True)
                    mm.then_inc(s_ready[l][a], 1)

                def turn(u):
                    h, q, c = us[u]
                    n = (CTX if c else (LAT, T)[a]) // P
                    pe.wait_ge(pn_ready[l][a], u + 1)
                    if u >= T_RING[a]:
                        pe.wait_ge(pt_ready[l][a], u - T_RING[a] + 1)
                    tp = t_at(a, u, n * P)
                    for t in range(n):
                        mm = pe.transpose(tp[:, t * P:(t + 1) * P], PEXP[:, u % P_RING, t * P:(t + 1) * P], IDENT[:])
                    mm.then_inc(t_ready[l][a], 1)

                def values(u):
                    h, q, c = us[u]
                    pe.wait_ge(pt_ready[l][0], u + 1)
                    if u >= per:
                        pe.wait_ge(cat_hi[l], 5)
                    if c:
                        tiles = [4, 5]
                    else:
                        tiles = {0: [0, 1], 1: [6, 7], 2: [7, 8], 3: [2, 3]}[q] + [4, 5]
                    dst = av_at(0, int(c))[HD * (h % 2):HD * (h % 2) + HD, q * P:(q + 1) * P]
                    for t, vt in enumerate(tiles):
                        mm = pe.matmul(dst, VN[:, vt, HD * h:HD * h + HD], PTN[:, u % P_RING, t, :],
                                       start=(t == 0), stop=(t == len(tiles) - 1))
                    mm.then_inc(pt_used[l][0], 1)

                def values_head(s):
                    for h in range(HEADS):
                        r = s - (h * ph + 6 + (h >= 2))
                        if not 0 <= r < ph:
                            continue
                        if r == 0:
                            pe.wait_ge(pt_ready[l][1], h * ph + 4)
                            if h == 2:
                                pe.wait_ge(cat_hi[l], 7)
                        rows = slice(HD * (h % 2), HD * (h % 2) + HD)
                        if l == 0 and r == 3:
                            pe.wait_ge(pt_ready[l][1], h * ph + 6)
                            for t in (4, 5):
                                mm = pe.matmul(av_at(1, 1)[rows, 0:CTX], VM[:, t, HD * h:HD * h + HD],
                                               PTC[:, h % 2, t - 4, :], start=(t == 4), stop=(t == 5))
                            mm.then_inc(pt_used[l][1], 1)
                        for t in [[r], {0: [0, 1], 1: [2, 3], 2: [4], 3: [5]}.get(r)][ph == 4]:
                            mm = pe.matmul(av_at(1, 0)[rows, 0:LAT], VM[:, t, HD * h:HD * h + HD], PTM[h % 2][:, t, :],
                                           start=(t == 0), stop=(t == 5))
                        if r == ph - 1:
                            mm.then_inc(pt_used[l][1], 1)

                la, lb = 2, 3
                for s in range(len(us) + (4 if a == 0 else 7)):
                    if s < len(us):
                        scores(s)
                    if 0 <= s - la < len(us):
                        turn(s - la)
                    if a == 1:
                        values_head(s)
                    elif 0 <= s - lb < per:
                        values(s - lb)
                    elif per <= s - lb - 1:
                        values(s - lb - 1)
                    if l == 0 and a == 0 and s < 24:
                        if s % 6 < 4:
                            mod_panel(16 + 4 * (s // 6) + s % 6)
                        if s % 6 == 5:
                            mod_turn(8 + s // 6)

            def conv_mean(l):
                w = T if l == 0 else LAT
                pe.wait_ge(conv_step[l], 2 * TAPS)
                for ct in range(2):
                    for a, b in spans(w):
                        s = 0 if a == 0 else CTX0 - LAT
                        mm = pe.matmul(STAT[:, a:b], ONES[:], CACC[:, ct, a + s:b + s], start=(ct == 0), stop=(ct == 1))
                mm.then_inc(mean_done[l], 1)

            def conv_variance(l):
                w = T if l == 0 else LAT
                pe.wait_ge(cen_done[l], 2)
                for ct in range(2):
                    pe.wait_ge(csq_done[l], ct + 1)
                    for a, b in spans(w):
                        mm = pe.matmul(STAT[:, a:b], ONES[:], SQC[:, ct, a:b], start=(ct == 0), stop=(ct == 1))
                mm.then_inc(var_done[l], 1)

            pe.wait_ge(consts, 2)
            pe.wait_ge(ones_set, 1)
            pe.wait_ge(c_ready, 1)
            mod_first(0)
            mod_first(1)
            mod_turn(0)
            mod_first(2)
            mod_turn(1)
            total_of_first()
            mod_first(3)
            mod_turn(2)
            mod_turn(3)

            for l in L2:
                w = T if l == 0 else LAT
                k = 2 * l
                for i in range(16):
                    p = P_IN[l] + i
                    n = G_IN[l] + i
                    if l == 0 and i < 2:
                        if i == 0:
                            first_two(0, [p, p + 1], n, WEIGHTS[p], 0)
                        continue
                    pe.wait_ge(lo_done, WEIGHTS[p] + 1)
                    if n >= 2:
                        pe.wait_ge(g_free[n % 2], n // 2)
                    wt = width(l, TILES[i])
                    for kt in range(KT):
                        if l == 1 and i == 0:
                            pe.wait_ge(hlo_ready, KT * 2 * k + kt + 1)
                            if kt == KT // 2:
                                total(2, 1)
                        if l == 1 and wt == T:
                            pe.wait_ge(hlo_ready, KT * (2 * k + 1) + kt + 1)
                        mm = three(G[n % 2], kt, p % RAWS, HHI, HLO, kt, spans(wt), kt == 0, kt == KT - 1)
                    mm.then_inc(w_used, 1)
                    if TILES[i] == "q1":
                        pe.wait_ge(*in_sq(l, "kv"))
                        for a, b in spans(T):
                            mm = pe.matmul(STAT[:, a:b], ONES[:], RKV[:, a:b], start=True, stop=True)
                        mm.then_inc(kv_stat[l], 1)
                    if TILES[i] == "f1":
                        pe.wait_ge(*in_sq(l, "q1"))
                        pe.wait_ge(kv_rstd[l], 1)
                        for ct in range(2):
                            for a, b in spans(w):
                                mm = pe.matmul(STAT[:, a:b], ONES[:], SQQ[:, ct, a:b], start=(ct == 0), stop=(ct == 1))
                        mm.then_inc(q_stat[l], 1)
                if not CONV_AT[l]["mean"]:
                    conv_mean(l)
                pe.wait_ge(wu_in[l], 32)
                pe.wait_ge(kvn_ready[l], 1)
                for i, job in enumerate(JOBS[l]):
                    n = G_JOB[l] + i
                    j = int(job[-1])
                    pe.wait_ge(g_free[n % 2], n // 2)
                    dst = G[n % 2]
                    if job[:2] == "kn":
                        for a, b in spans(T):
                            mm = pe.matmul(dst[:, a:b], WUKV[:, P * j:P * j + P], KVA[:, a:b], start=True, stop=True)
                    elif job[:2] == "vm":
                        for t in range(3):
                            mm = pe.matmul(dst[:, 256 * t:256 * t + 256], KVA[:, (3 * j + t) * P:(3 * j + t + 1) * P],
                                           WUKV[:, 256:512], start=True, stop=True)
                    elif job[0] == "q":
                        if j == 0:
                            pe.wait_ge(qn_ready[l], 1)
                        for ct in range(2):
                            for a, b in spans(w):
                                mm = pe.matmul(dst[:, a:b], WUQ[:, ct, P * j:P * j + P], QA[:, ct, a:b], start=(ct == 0),
                                               stop=(ct == 1))
                    elif job[:2] == "vn":
                        for t in range(3):
                            vt = 3 * j + t
                            t0 = vt * P if vt < 6 else 64 + (vt - 6) * P
                            for ct in range(2):
                                mm = pe.transpose(dst[:, 256 * t + P * ct:256 * t + P * ct + P], NAVT[:, ct, t0:t0 + P],
                                                  IDENT[:])
                    else:
                        if j == 0:
                            pe.wait_ge(const_in, 16)
                        for ct in range(2):
                            mm = pe.matmul(dst[:, 256 * ct:256 * ct + 256], FU[:, ct, P * j:P * j + P], CSD[:], start=True,
                                           stop=True)
                    mm.then_inc(job_done, 1)
                    if job == CONV_AT[l]["mean"]:
                        conv_mean(l)
                    if job == CONV_AT[l]["variance"]:
                        conv_variance(l)
                    if l == 0 and i % 6 < 4 and i < 18:
                        mod_panel(4 * (i // 6) + i % 6)
                    if l == 0 and i % 6 == 5:
                        mod_turn(MOD0 + i // 6)
                if l == 0:
                    mod_turn(6)
                n = G_DFT[l]
                pe.wait_ge(g_free[n % 2], n // 2)
                pe.wait_ge(g_free[(n + 1) % 2], (n + 1) // 2)
                for s in range(4):
                    pe.wait_ge(dft_in[l][s % 2], 16 * (s // 2 + 1))
                    for ct in range(2):
                        for cs in range(2):
                            mm = pe.matmul(G[(n + ct) % 2][:, 0:LAT], AB[ct][:, s, cs * P:(cs + 1) * P],
                                           DFT[:, s % 2, cs * 512:(cs + 1) * 512], start=(s == 0 and cs == 0),
                                           stop=(s == 3 and cs == 1))
                        if l == 1 and s == 3:
                            mm.then_inc(job_done, 1)
                    if l == 0 or s < 3:
                        mm.then_inc(dft_used[l], 1)
                    if l == 0:
                        mod_panel(12 + s)
                if l == 0:
                    pe.wait_ge(dft_in[l][0], 48)
                    for ct in range(2):
                        for s in range(2):
                            for cs in range(2):
                                mm = pe.matmul(G[(n + ct) % 2][:, LAT:T], AB[ct][:, 4 + s, cs * P:(cs + 1) * P],
                                               DFT[:, 0, cs * 512 + s * 256:cs * 512 + (s + 1) * 256],
                                               start=(s == 0 and cs == 0), stop=(s == 1 and cs == 1))
                        mm.then_inc(job_done, 1)
                if l == 0:
                    mod_turn(7)
                pe.wait_ge(crstd_done[l], 1)
                pe.wait_ge(cat_hi[l], 4)
                attention(l, 0)
                if l == 0:
                    pe.wait_ge(mod_done, 12)
                attention(l, 1)
                tail(2 * l + 1, P_OUT[l], G_OUT[l])

                def chunk(l, j, last_chunk):
                    w = T if l == 0 else LAT
                    for idx, (kind, i) in enumerate(steps_of(l, last_chunk)):
                        if last_chunk and i == KT:
                            break
                        if kind == "m":
                            continue
                        p = (P_LAST if last_chunk else P_FF)[l] + idx
                        n = G_FF[l] + i
                        if isinstance(j, int) and j == 0 and i < 2:
                            if i == 0:
                                first_two(2 * l + 1, [p, p + 1], n, WEIGHTS[p], j)
                            continue
                        pe.wait_ge(lo_done, j * (2 * KT) + (WEIGHTS[P_FF[l]] + i + 1))
                        pe.wait_ge(g_free[n % 2], j * 8 + n // 2)
                        for kt in range(KT):
                            if i == KT:
                                pe.wait_ge(hid_lo[l], j * KT + (kt + 1))
                            hi, lo = (HHI, HLO) if i < KT else (CHI, CLO)
                            if l == 0 and not last_chunk and i == SUM_BEHIND[0] + 1 and kt == KT // 2:
                                mod_late(j * 4 + 12)
                            mm = three(G[n % 2], kt, p % RAWS, hi, lo, kt, spans(w), kt == 0, kt == KT - 1)
                        mm.then_inc(w_used, 1)
                        if l == 0 and not last_chunk and i in SUM_BEHIND[1:]:
                            mod_late(j * 4 + (12 + SUM_BEHIND.index(i)))

                chunk(l, 0, False)
                with pe.Fori(1, FFC - 1) as j:
                    chunk(l, j, False)
                chunk(l, FFC - 1, True)
                tail(2 * l + 2, P_LAST[l] + KT, G_FF[l] + 16 * FFC - KT)
            total(NORMS - 1, 1)

        @block.vector
        def _(dve):
            def split_lo(i, p):
                dve.wait_ge(hi_done, p + 1)
                dve.tensor_tensor(WLO[:, i, :], RAW[:, i, :], WHI[:, i, :].bitcast(F32),
                                  ALU.subtract).then_inc(lo_done, 1)

            def mod_turned(c):
                dve.wait_ge(mod_col, c + 1)
                src = MODACC[c % 2 if c < MOD0 else 0].rearrange("p (i r) -> p i r", r=P)
                for v in range(2):
                    last = dve.tensor_tensor(MODT[:, 0, 4 * c:4 * c + 4, v], src[:, :, v],
                                             pcol(0, PB + 4 * c, 4), ALU.add)
                last.then_inc(mod_done, 1)

            def mod_finish(l, c, cc):
                dve.wait_ge(mod_col, c + 1)
                for v in range(2):
                    last = dve.tensor_tensor(ACC[:, v, :].rearrange("p (i r) -> p i r", r=P),
                                             MODSUM[v].rearrange("p (i r) -> p i r", r=P),
                                             IDENT[:].unsqueeze(1).broadcast_to([P, 4, P]), ALU.mult)
                last.then_inc(mod_diag, 1)
                dve.wait_ge(mod_diag, cc + 1)
                for v in range(2):
                    last = dve.tensor_reduce(MT[:, v, :], ACC[:, v, :].rearrange("p (i r) -> p i r", r=P), AX_X, ALU.add)
                last.then_inc(mod_part, 1)
                dve.wait_ge(mod_part, cc + 1)
                for v in range(2):
                    last = dve.tensor_tensor(MODT[:, l, bass.ds(4 * cc, 4), v], MT[:, v, :],
                                             PAR[:, bass.ds(l * PL + PB + 4 * cc, 4)], ALU.add)
                last.then_inc(mod_done, 1)

            def mod_partial(p, s, m, j):
                c = m // MPARTS
                if s == 0 and m:
                    mod_finish(1, j * 4 + (12 + c - 1), j * 4 + (c - 1))
                dve.wait_ge(raw_in[p % RAWS], j * (16 * len(FF_STEPS) // RAWS) + 16 * (p // RAWS + 1))
                for kk in range(2):
                    for v in range(2):
                        n = 2 * kk + v
                        src = RAW[:, p % RAWS, 512 * kk:512 * (kk + 1)]
                        cs = CSILU[:, 2 * s + kk, v:v + 1]
                        if s == 0 and kk == 0:
                            if v == 0:
                                dve.wait_ge(mod_done, j * 4 + (12 + c))
                            dve.tensor_scalar(ACC[:, v, :], src, cs, None, ALU.mult).then_inc(mod_step, 1)
                        else:
                            dve.wait_ge(mod_step, j * 64 + (4 * m + n - 1))
                            dve.scalar_tensor_tensor(ACC[:, v, :], src, cs, ACC[:, v, :], ALU.mult,
                                                     ALU.add).then_inc(mod_step, 1)

            def coef(l, n):
                for v in range(2):
                    last = dve.scalar_tensor_tensor(AC[:, l, n, :, v], MODT[:, l, (SC1, SC2)[n]:(SC1, SC2)[n] + KT, v], 1.0,
                                                    pcol(l, (PG1, PG2)[n], KT), ALU.add, ALU.mult)
                last.then_inc(ac_ready, 1)

            def h_whole(k, g, kt):
                a, b = sweeps(k)[g]
                l, n, v = k // 2, k % 2, int(a == LAT)
                dve.wait_ge(xn_ready, KT * (2 * k + g) + kt + 1)
                dve.wait_ge(ac_ready, k + 1)
                dve.tensor_scalar(HT[:, kt % 2, a:b], XN[:, kt % 2, a:b], AC[:, l, n, kt, v:v + 1],
                                  MODT[:, l, (SH1, SH2)[n] + kt, v:v + 1], ALU.mult, ALU.add).then_inc(ht_ready, 1)

            def low(k, g, kt):
                a, b = sweeps(k)[g]
                dve.wait_ge(ht_ready, KT * (2 * k + g) + kt + 1)
                dve.wait_ge(hhi_ready, KT * (2 * k + g) + kt + 1)
                dve.tensor_tensor(HLO[:, kt, a:b], HT[:, kt % 2, a:b], HHI[:, kt, a:b].bitcast(F32),
                                  ALU.subtract).then_inc(hlo_ready, 1)

            def finished(g, kt):
                a, b = sweeps(NORMS - 1)[g]
                if kt == 0:
                    dve.wait_ge(rstd_ready, nth(NORMS - 1, g) + 2)
                dve.scalar_tensor_tensor(OUTT[:, kt, a:b], X[:, kt, a:b], PAR[:, PF + kt:PF + kt + 1],
                                         RSTD[:, a:b], ALU.mult, ALU.mult).then_inc(out_ready, 1)

            def tail(k, p0, n0, gate):
                l = (k - 1) // 2

                def step(g, kt):
                    if k == NORMS - 1:
                        finished(g, kt)
                    else:
                        h_whole(k, g, kt)
                        low(k, g, kt)

                for t in range(TAIL):
                    q = ahead_in_tail(p0, t)
                    if t <= BOTH:
                        split_lo(q % RAWS, WEIGHTS[q])
                    m, over = tail_step(k, t)
                    if BOTH <= t < KT:
                        dve.wait_ge(held_done, BOTH * (k - 1) + t - BOTH + 1)
                    else:
                        dve.wait_ge(w_used, ON_PE[p0 + m] + 1)
                    residual(l, m, n0 + t, gate, over)
                    if t > KT + 1:
                        for kt in range(2):
                            step(0, 2 * (t - KT - 2) + kt)
                    if t > KT and q:
                        split_lo(q % RAWS, WEIGHTS[q])
                for kt in range(BOTH, KT):
                    step(0, kt)
                for kt in range(KT):
                    step(1, kt)

            def cat_low(l, f):
                w = T if l == 0 else LAT
                c = CAT_ORDER[f]
                dve.wait_ge(cat_hi[l], f + 1)
                dve.tensor_tensor(CLO[:, c, 0:w], CTMP[:, 0:w], CHI[:, c, 0:w].bitcast(F32), ALU.subtract).then_inc(
                    cat_lo[l], 1)

            def residual(l, m, n, gate, over):
                for a, b in over:
                    v = int(a == LAT)
                    last = dve.scalar_tensor_tensor(X[:, m, a:b], G[n % 2][:, a:b], MODT[:, l, gate + m, v:v + 1],
                                                    X[:, m, a:b], ALU.mult, ALU.add)
                last.then_inc(g_free[n % 2], 1)

            def attention(l, a):
                us = units(l, a)
                per = len(us) // 2

                def maxima(u):
                    h, q, c = us[u]
                    n = CTX if c else (LAT, T)[a]
                    dve.wait_ge(s_ready[l][a], u + 1)
                    S = s_at(a, u, n)
                    if a == 0 and not c:
                        dve.tensor_tensor(S[:, 0:256], S[:, 0:256], BM[:, VARIANT[q], h, :], ALU.add).then_inc(
                            s_bias[l][0], 1)
                        dve.wait_ge(s_bias[l][0], len([1 for x in us[:u + 1] if not x[2]]))
                    if a == 0:
                        dve.tensor_reduce(NMX[:, a, u:u + 1], S, AX_X, ALU.max, negate=True).then_inc(nm_ready[l][a], 1)
                    else:
                        dve.tensor_reduce(RIN[:, a, u:u + 1], S, AX_X, ALU.max, negate=True).then_inc(s_bias[l][1], 1)
                        dve.wait_ge(s_bias[l][1], u + 1)
                        dve.tensor_scalar(NMX[:, a, u:u + 1], RIN[:, a, u:u + 1], MLA_SCALE, None, ALU.mult).then_inc(
                            nm_ready[l][a], 1)

                def norm(u):
                    h, q, c = us[u]
                    n = CTX if c else (LAT, T)[a]
                    dve.wait_ge(exp_done[l][a], u + 1)
                    dve.reciprocal(RIN[:, a, u:u + 1], SUM[:, a, u:u + 1]).then_inc(ri_ready[l][a], 1)
                    dve.wait_ge(ri_ready[l][a], u + 1)
                    pr = PEXP[:, u % P_RING, 0:n]
                    dve.tensor_scalar(pr, pr, RIN[:, a, u:u + 1], None, ALU.mult).then_inc(pn_ready[l][a], 1)

                if a == 0:
                    dve.wait_ge(bias_in[l], 16)
                for s in range(len(us) + (5 if a == 0 else 8)):
                    if s < len(us):
                        maxima(s)
                    if 1 <= s <= len(us):
                        norm(s - 1)
                    if s in ((per + 3, 2 * per + 4) if a == 0 else (per + 7, 2 * per + 7)):
                        cat_low(l, (4, 6)[a] + (0 if s < 2 * per else 1))
                    if l == 0 and a == 0 and s % 6 == 5 and s < 24:
                        mod_turned(8 + s // 6)

            def glu(l, ct):
                if ct == 0:
                    dve.wait_ge(pads_ready, l + 1)
                dve.wait_ge(*in_sq(l, f"a{ct}"))
                dve.wait_ge(*in_sq(l, f"g{ct}"))
                y = YPAD[:, ct, HALO:HALO + LAT].rearrange("p (r c) -> p c r", r=ROWS)
                last = dve.tensor_tensor(y, CACC[:, ct, 0:LAT].rearrange("p (c r) -> p c r", r=ROWS),
                                         SIG[:, 0:LAT].rearrange("p (c r) -> p c r", r=ROWS), ALU.mult)
                if l == 0:
                    last = dve.tensor_tensor(YPAD[:, ct, CTX0 + HALO:CTX0 + HALO + CTX], CACC[:, ct, LAT:T],
                                             SIG[:, LAT:T], ALU.mult)
                last.then_inc(glu_done[l], 1)

            def conv_tap(l, at):
                ct, tap = CONV_ORDER[at]
                wide = CONVW if l == 0 else LAT
                acc, y = CACC[:, ct, 0:wide], YPAD[:, ct, tap:tap + wide]
                if tap == 0:
                    dve.wait_ge(glu_done[l], ct + 1)
                    dve.tensor_scalar(acc, y, pcol(l, PCW + ct), pcol(l, PCB + ct), ALU.mult, ALU.add).then_inc(
                        conv_step[l], 1)
                else:
                    dve.wait_ge(conv_step[l], CONV_ORDER.index((ct, tap - 1)) + 1)
                    dve.scalar_tensor_tensor(acc, y, pcol(l, PCW + 2 * tap + ct), acc, ALU.mult, ALU.add).then_inc(
                        conv_step[l], 1)

            def conv_center(l):
                w = T if l == 0 else LAT
                dve.wait_ge(mean_done[l], 1)
                for ct in range(2):
                    for a, b in spans(w):
                        s = 0 if a == 0 else CTX0 - LAT
                        y = CACC[:, ct, a + s:b + s]
                        last = dve.scalar_tensor_tensor(y, STAT[:, a:b], -1.0 / 256, y, ALU.mult, ALU.add)
                    last.then_inc(cen_done[l], 1)

            def conv_low(l):
                w = T if l == 0 else LAT
                dve.wait_ge(crstd_done[l], 1)
                for ct in range(2):
                    for a, b in spans(w):
                        s = 0 if a == 0 else CTX0 - LAT
                        y = CACC[:, ct, a + s:b + s]
                        last = dve.tensor_tensor(y, y, RSTDC[:, a:b], ALU.mult)
                    last.then_inc(cn_done[l], 1)

            dve.memset(ONES[:], 1.0).then_inc(ones_set, 1)
            dve.memset(MODROW[:], 0.0).then_inc(row_zero, 1)
            mod_turned(0)
            mod_turned(1)
            for p in range(2):
                split_lo(p, p)
            mod_turned(2)
            mod_turned(3)
            dve.wait_ge(mod_done, 4)
            coef(0, 0)

            for l in L2:
                w = T if l == 0 else LAT
                k = 2 * l
                if l == 0:
                    for g in range(2):
                        for kt in range(KT):
                            h_whole(0, g, kt)
                            low(0, g, kt)
                        if g == 0:
                            split_lo(2, 2)
                for i in range(16):
                    p = P_IN[l] + i
                    if i + AHEAD < 16:
                        split_lo((p + AHEAD) % RAWS, WEIGHTS[p + AHEAD])
                    tile, n = TILES[i], G_IN[l] + i
                    if tile in ("a1", "kv"):
                        glu(l, 0 if tile == "a1" else 1)
                    if i >= 2:
                        for c in range(CONV_STEP * (i - 2), min(CONV_STEP * (i - 1), 2 * TAPS)):
                            conv_tap(l, c)
                    if tile == "kr":
                        dve.wait_ge(rope_in[l], 16)
                        dve.wait_ge(w_used, ON_PE[p] + 1)
                        dve.tensor_tensor(KRT[64:96, :], G[n % 2][64:96, 0:T], CS[64:96, :], ALU.mult)
                        dve.tensor_tensor(ROT[64:96, :], G[n % 2][96:128, 0:T], CS[96:128, :], ALU.mult).then_inc(
                            g_free[n % 2], 1)
                        dve.wait_ge(g_free[n % 2], n // 2 + 1)
                        dve.tensor_tensor(KRT[64:96, :], KRT[64:96, :], ROT[64:96, :], ALU.add).then_inc(kr_ready[l], 1)
                    if tile == "f0":
                        dve.wait_ge(kv_rstd[l], 1)
                        dve.scalar_tensor_tensor(KVA[:], KVA[:], pcol(l, PKVN), RKV[:], ALU.mult, ALU.mult).then_inc(
                            kvn_ready[l], 1)
                    if tile == "nq0":
                        dve.wait_ge(q_rstd[l], 1)
                        for ct in range(2):
                            last = dve.scalar_tensor_tensor(QA[:, ct, 0:w], QA[:, ct, 0:w], pcol(l, PQN + ct),
                                                            SQQ[:, 0, 0:w], ALU.mult, ALU.mult)
                        last.then_inc(qn_ready[l], 1)
                conv_center(l)
                for i, job in enumerate(JOBS[l]):
                    n = G_JOB[l] + i
                    j = int(job[-1])
                    if job[0] == "q":
                        dve.wait_ge(q_nope[l], j + 1)
                        if j:
                            dve.wait_ge(q_part[l], 2 * j)
                        dve.tensor_tensor(QT[64:96, j, 0:w], G[n % 2][64:96, 0:w], CS[64:96, 0:w], ALU.mult)
                        dve.tensor_tensor(ROT[64:96, 0:w], G[n % 2][96:128, 0:w], CS[96:128, 0:w], ALU.mult).then_inc(
                            g_free[n % 2], 1)
                        dve.wait_ge(g_free[n % 2], n // 2 + 1)
                        dve.tensor_tensor(QT[64:96, j, 0:w], QT[64:96, j, 0:w], ROT[64:96, 0:w], ALU.add).then_inc(
                            q_part[l], 2)
                        if j == HEADS - 1:
                            conv_low(l)
                    elif job[:2] == "ab":
                        dve.wait_ge(job_done, JD[l] + i + 1)
                        dve.tensor_copy(AB[0][:, j, :], G[n % 2][:, 0:256])
                        dve.tensor_copy(AB[1][:, j, :], G[n % 2][:, 256:512]).then_inc(g_free[n % 2], 1)
                    if l == 0 and i % 6 == 5:
                        mod_turned(MOD0 + i // 6)
                if l == 0:
                    mod_turned(6)
                for f in range(4):
                    cat_low(l, f)
                if l == 0:
                    mod_turned(7)
                attention(l, 0)
                if l == 0:
                    dve.wait_ge(mod_done, 12)
                    coef(0, 1)
                for p in range(P_OUT[l], P_OUT[l] + AHEAD):
                    split_lo(p % RAWS, WEIGHTS[p])
                attention(l, 1)
                tail(2 * l + 1, P_OUT[l], G_OUT[l], GT1)

                def chunk(l, j, last_chunk):
                    w = T if l == 0 else LAT
                    for idx, (kind, i) in enumerate(steps_of(l, last_chunk)):
                        if last_chunk and i == KT:
                            break
                        q = (P_LAST if last_chunk else P_FF)[l] + idx + AHEAD
                        is_weight, count = split_ahead(l, idx, last_chunk)
                        if is_weight:
                            split_lo(q % RAWS, j * (2 * KT) + count)
                        else:
                            mod_partial(q, count % MPARTS, count, j)
                        if kind == "m":
                            continue
                        n = G_FF[l] + i
                        if i < KT:
                            dve.wait_ge(hid_hi[l], j * KT + (i + 1))
                            dve.tensor_tensor(CLO[:, i, 0:w], SQF[:, i % 2, 0:w], CHI[:, i, 0:w].bitcast(F32),
                                              ALU.subtract).then_inc(hid_lo[l], 1)
                        else:
                            dve.wait_ge(w_used, j * (2 * KT) + (ON_PE[P_FF[l]] + i + 1))
                            residual(l, i - KT, n, GT2, spans(w))
                        if l == 0 and not last_chunk and i == 15:
                            mod_finish(1, j * 4 + 15, j * 4 + 3)

                with dve.Fori(0, FFC - 1) as j:
                    chunk(l, j, False)
                chunk(l, FFC - 1, True)
                if l == 0:
                    dve.wait_ge(mod_done, 24)
                    coef(1, 0)
                    coef(1, 1)
                tail(2 * l + 2, P_LAST[l] + KT, G_FF[l] + 16 * FFC - KT, GT2)

        @block.gpsimd
        def _(pool):
            pool.memset(IDENT[:], 0.0).then_inc(consts, 1)
            pool.wait_ge(consts, 1)
            pool.affine_select(out=IDENT[:], in_=IDENT[:], compare_op=ALU.not_equal, fill=1.0, base=0,
                               pattern=[[-1, P]], channel_multiplier=1).then_inc(consts, 1)
            def xnorm(k, g, kt):
                a, b = sweeps(k)[g]
                if kt == 0:
                    pool.wait_ge(rstd_ready, nth(k, g) + 2 if k else 1)
                if kt >= 2:
                    pool.wait_ge(hhi_ready, KT * (2 * k + g) + kt - 1)
                    pool.wait_ge(ht_ready, KT * (2 * k + g) + kt - 1)
                pool.tensor_tensor(XN[:, kt % 2, a:b], X[:, kt, a:b], RSTD[:, a:b], ALU.mult).then_inc(xn_ready, 1)

            def add_square(k, t):
                a, b = whole(tail_step(k, t)[1])
                pool.wait_ge(sq_ready, KT + TAIL * (k - 1) + t + 1)
                if t >= 2:
                    pool.wait_ge(sq_added, (TAIL - 1) * (k - 1) + t - 1)
                pool.tensor_tensor(SQA[:, a:b], SQA[:, a:b], SQ[:, t % 2, a:b], ALU.add).then_inc(sq_added, 1)

            def halos(l):
                pool.wait_ge(hlo_ready, 2 * KT * (2 * l + 1))
                pool.memset(YPAD[:], 0.0).then_inc(pads_ready, 1)

            for kt in range(1, KT):
                pool.wait_ge(sq_ready, kt + 1)
                if kt >= 2:
                    pool.wait_ge(sq_used, kt - 1)
                pool.tensor_tensor(SQA[:], SQA[:], SQ[:, kt % 2, :], ALU.add).then_inc(sq_used, 1)
            for g in range(2):
                for kt in range(KT):
                    xnorm(0, g, kt)
            halos(0)
            for k in range(1, NORMS):
                inner = k < NORMS - 1
                for t in range(1, KT):
                    add_square(k, t)
                for t in range(KT, TAIL):
                    if inner and t != KT + 1:
                        xnorm(k, 0, 2 * max(t - KT - 1, 0))
                        xnorm(k, 0, 2 * max(t - KT - 1, 0) + 1)
                    add_square(k, t)
                if inner:
                    xnorm(k, 0, KT - 2)
                    xnorm(k, 0, KT - 1)
                    for kt in range(KT):
                        xnorm(k, 1, kt)
                if k == 2:
                    halos(1)


def kernel(**inputs):
    import numpy as np
    import concourse.bacc as bacc
    from concourse.bass_utils import run_bass_kernel_spmd

    a = {k: np.asarray(v) for k, v in inputs.items()}

    def panel(w):
        kk, m = w.shape
        return w.reshape(kk // P, P, m // P, P).transpose(2, 1, 0, 3).reshape(m // P, P, kk)

    order = np.arange(LAT).reshape(ROWS, COLS).T.reshape(-1)
    x = np.concatenate([a["x"][0][order], a["ctx"][0]], 0)
    x = x.reshape(T, KT, P).transpose(2, 1, 0)

    swap = np.concatenate([np.arange(16, 32), np.arange(16)])
    kv0, kr0, nq0 = 256, 384, 416
    fn0, cv0 = 1184, 1440
    packed = {}
    for l in range(LAYERS):
        w = a["w_in"][l]
        kr = w[:, kr0:kr0 + 32]
        cols = [w[:, cv0:cv0 + 128], w[:, cv0 + 256:cv0 + 384], w[:, cv0 + 128:cv0 + 256], w[:, cv0 + 384:cv0 + 512],
                w[:, kv0:kv0 + 128], np.concatenate([kr, kr[:, swap]] * 2, 1), w[:, 0:256], w[:, fn0:fn0 + 256],
                w[:, nq0:nq0 + 768]]
        packed["in", l] = panel(np.concatenate(cols, 1))
        packed["out", l] = panel(a["w_out"][l])
        packed["ff1", l] = panel(a["w_ff1"][l])
        packed["ff2", l] = [panel(a["w_ff2"][l][D * j:D * (j + 1)]) for j in range(FFC)]
        packed["mod", l] = a["w_mod"][l].reshape(4, 2, P, 12, 512).transpose(3, 0, 2, 1, 4).reshape(12, 4, P, 1024)
    panels = np.empty((NPANEL, P, 1024), np.float32)
    mods = packed["mod", 0][:MOD0].reshape(MOD0 * MPARTS, P, 1024)
    for p, (name, l, *at) in enumerate(panel_order()):
        part = packed[name[:3] if name[:3] == "mod" else name, l]
        for i in at:
            part = part[i]
        panels[p] = part

    def columns(v):
        return v.reshape(-1, P).T

    par = []
    for l in range(LAYERS):
        par += [columns(a["b_mod"][l]), columns(a["norm1_g"][l]), columns(a["norm2_g"][l]), columns(a["mla_q_norm"][l]),
                columns(a["mla_kv_norm"][l]), columns(a["cv_w_dw"][l]), columns(a["cv_b_dw"][l]),
                columns(a["cv_ln_g"][l]), columns(a["cv_ln_b"][l])]
    par += [np.stack([columns(a["c"][0]), columns(a["c_ctx"])], 2).reshape(P, 2 * KT), columns(a["final_g"]),
            np.full((P, 1), EPS, np.float32)]
    par = np.concatenate(par, 1)

    uq = a["mla_w_uq"].reshape(LAYERS, 2, P, HEADS, 96)
    uq = np.concatenate([uq, uq[..., 64 + swap]], -1).transpose(0, 2, 1, 3, 4).reshape(LAYERS, P, 2, 512)
    ukv = a["mla_w_ukv"].reshape(LAYERS, P, HEADS, 2, HD).transpose(0, 1, 3, 2, 4).reshape(LAYERS, P, 512)

    bias = np.empty((LAYERS, P, 3, HEADS, 256), np.float32)
    qc, qr = np.repeat(np.arange(16), ROWS), np.tile(np.arange(ROWS), 16)
    kc, kr = np.repeat(np.arange(32), ROWS), np.tile(np.arange(ROWS), 32)
    for v, block in enumerate((0, 1, 3)):
        col, key = 16 * block + qc[:, None], WINDOW0[block] // ROWS + kc[None, :]
        start = np.clip(col - 8, 0, COLS - 16)
        inside = (key >= start) & (key < start + 16)
        rel = np.clip(key - col + 15, 0, 30)
        rows = kr[None, :] - qr[:, None] + 7
        bias[:, :, v] = np.where(inside[None, :, None, :], a["na_rpb"][:, :, rows, rel].transpose(0, 2, 1, 3),
                                 np.float32(-1e30))

    inv = 10000.0 ** (-np.arange(0, 16, 2, dtype=np.float32) / np.float32(16))
    t = order
    ang = np.concatenate([(t // COLS)[:, None] * inv, (t % COLS)[:, None] * inv], 1).astype(np.float32)
    rope = np.zeros((64, T), np.float32)
    rope[0:32] = 1.0
    rope[0:32, :LAT] = np.tile(np.cos(ang), (1, 2)).T
    rope[32:48, :LAT] = -np.sin(ang).T
    rope[48:64, :LAT] = np.sin(ang).T

    n = np.arange(HD)
    w = 2 * np.pi * np.outer(n, n) / HD
    z = np.zeros((HD, HD))
    dft_ch = np.concatenate([np.block([[np.cos(w), z], [z, np.cos(w)]]), np.block([[-np.sin(w), z], [z, -np.sin(w)]])],
                            1).astype(np.float32)
    w = 2 * np.pi * (np.outer(order, order) % LAT) / LAT
    dft = np.concatenate([np.cos(w).reshape(4, P, LAT), np.sin(w).reshape(4, P, LAT)], 2)
    n = np.arange(CTX)
    w = (2 * np.pi * (np.outer(n, n) % CTX) / CTX).reshape(2, P, CTX).transpose(1, 0, 2).reshape(1, P, 512)
    dft = np.concatenate([dft, np.concatenate([np.cos(w), np.sin(w)], 2)], 0).astype(np.float32)

    nc = bacc.Bacc("TRN2", target_bir_lowering=False, num_devices=1)
    arrays, args = {}, []
    for name, v in dict(x=x, panels=panels, mods=mods, par=par, w_uq=uq, w_ukv=ukv, bias=bias, rope=rope, dft=dft,
                        dft_ch=dft_ch).items():
        arrays[f"in_{name}"] = np.ascontiguousarray(v)
        args.append(nc.dram_tensor(f"in_{name}", v.shape, F32, kind="ExternalInput").ap())
    args.append(nc.dram_tensor("out_y", (P, KT, LAT), F32, kind="ExternalOutput").ap())
    trunk(nc, *args)
    y = run_bass_kernel_spmd(nc, [arrays], core_ids=[0]).results[0]["out_y"]
    y = np.asarray(y).transpose(2, 1, 0).reshape(LAT, D)
    back = np.arange(LAT).reshape(COLS, ROWS).T.reshape(-1)
    return y[back].reshape(1, LAT, D)
```
